# Optimizing a Trainium2 kernel written in Bass

```python
import math
import jax, jax.numpy as jnp
from jax import lax
import numpy as np
import jax
import jax.numpy as jnp

D_MODEL = 1024
BATCH = 1
SEQ = 512
DEPTH = 1

RWKV_HEAD_DIM = 64
RWKV_HEADS = D_MODEL // (2 * RWKV_HEAD_DIM)
RWKV_WIDTH = RWKV_HEADS * RWKV_HEAD_DIM
DECAY_LORA = 64
ICLR_LORA = 64
GATE_LORA = 128
GN_EPS = 64e-5
N_DIR = 2

DA_HEAD_DIM = 64
DA_HEADS = D_MODEL // (4 * DA_HEAD_DIM)
DA_V_DIM = 2 * DA_HEAD_DIM
DA_QK_WIDTH = DA_HEADS * 2 * DA_HEAD_DIM
DA_V_WIDTH = DA_HEADS * DA_V_DIM
SUBLN_EPS = 1e-5
Q_BLOCK = 128

ROPE_THETA = 500000.0
ROPE_DIM = DA_HEAD_DIM // 4

D_FF = 4 * D_MODEL
PLE_DIM = 256
N_BRANCH = 2
RMS_EPS = 1e-6

RWKV_COLS = 3 * RWKV_WIDTH + N_DIR * DECAY_LORA + N_DIR * ICLR_LORA + GATE_LORA
DA_COLS = 2 * DA_QK_WIDTH + DA_V_WIDTH
GATE_COLS = N_BRANCH * D_MODEL
IN_COLS = RWKV_COLS + DA_COLS + GATE_COLS


def rmsnorm(x, g, eps=RMS_EPS):
    xf = x.astype(jnp.float32)
    y = xf * lax.rsqrt(jnp.mean(xf * xf, axis=-1, keepdims=True) + eps)
    return (y * g.astype(jnp.float32)).astype(x.dtype)

def centred_shift(u, mu_prev, mu_next):
    up = jnp.pad(u, ((0, 0), (1, 1), (0, 0)))
    return u + mu_prev * (up[:, :-2] - u) + mu_next * (up[:, 2:] - u)

def rwkv7_scan(r, w, k, v, kk, a, reverse):
    B, S, H, N = r.shape

    def step(state, inp):
        r_t, w_t, k_t, v_t, kk_t, a_t = inp
        sa = jnp.einsum('bhij,bhj->bhi', state, -kk_t)
        state = (state * w_t[:, :, None, :]
                 + sa[..., None] * (kk_t * a_t)[:, :, None, :]
                 + v_t[..., None] * k_t[:, :, None, :])
        y_t = jnp.einsum('bhij,bhj->bhi', state, r_t)
        return state, y_t

    xs = tuple(jnp.moveaxis(t, 1, 0) for t in (r, w, k, v, kk, a))
    s0 = jnp.zeros((B, H, N, N), jnp.float32)
    _, ys = lax.scan(step, s0, xs, reverse=reverse)
    return jnp.moveaxis(ys, 0, 1)

def rwkv7_branch(u, mu_prev, mu_next, w0, w2, a0, a2, g2, k_k, k_a, r_k, ln_w, ln_b, w_o):
    f32 = jnp.float32
    B, S, _ = u.shape
    H, N, W = RWKV_HEADS, RWKV_HEAD_DIM, RWKV_WIDTH
    u = centred_shift(u, mu_prev, mu_next).astype(f32)
    o1, o2, o3 = W, 2 * W, 3 * W
    o4 = o3 + N_DIR * DECAY_LORA
    o5 = o4 + N_DIR * ICLR_LORA
    r = u[..., :o1]
    k = u[..., o1:o2]
    v = u[..., o2:o3]
    wd = u[..., o3:o4].reshape(B, S, N_DIR, DECAY_LORA)
    ad = u[..., o4:o5].reshape(B, S, N_DIR, ICLR_LORA)
    gd = u[..., o5:]

    w_log = -jax.nn.softplus(-(w0.astype(f32) + jnp.einsum('bsdr,drc->bsdc', jnp.tanh(wd), w2.astype(f32)))) - 0.5
    decay = jnp.exp(-jnp.exp(w_log)).reshape(B, S, N_DIR, H, N)
    a = jax.nn.sigmoid(a0.astype(f32) + jnp.einsum('bsdr,drc->bsdc', ad, a2.astype(f32))).reshape(B, S, N_DIR, H, N)
    g = jax.nn.sigmoid(gd) @ g2.astype(f32)

    kk = (k * k_k.astype(f32)).reshape(B, S, H, N)
    kk = kk / jnp.maximum(jnp.sqrt(jnp.sum(kk * kk, axis=-1, keepdims=True)), 1e-12)
    r_h = r.reshape(B, S, H, N)
    v_h = v.reshape(B, S, H, N)
    k_dir = k.reshape(B, S, 1, H, N) * (1.0 + (a - 1.0) * k_a.astype(f32).reshape(H, N))

    y = (rwkv7_scan(r_h, decay[:, :, 0], k_dir[:, :, 0], v_h, kk, a[:, :, 0], False)
         + rwkv7_scan(r_h, decay[:, :, 1], k_dir[:, :, 1], v_h, kk, a[:, :, 1], True))

    mean = jnp.mean(y, axis=-1, keepdims=True)
    var = jnp.mean(jnp.square(y - mean), axis=-1, keepdims=True)
    y = ((y - mean) * lax.rsqrt(var + GN_EPS)).reshape(B, S, W)
    y = y * ln_w.astype(f32) + ln_b.astype(f32)
    bonus = jnp.sum(jnp.sum(r_h[:, :, None] * k_dir * r_k.astype(f32), axis=-1, keepdims=True), axis=2) * v_h
    y = (y + bonus.reshape(B, S, W)) * g
    return (y @ w_o.astype(f32)).astype(w_o.dtype)

def rope_tables(S):
    pos = jnp.arange(S, dtype=jnp.float32)
    inv_freq = ROPE_THETA ** (-jnp.arange(0, ROPE_DIM, 2, dtype=jnp.float32) / ROPE_DIM)
    ang = pos[:, None] * inv_freq[None, :]
    return jnp.cos(ang), jnp.sin(ang)

def partial_rope(x, cos, sin):
    half = ROPE_DIM // 2
    c = cos[:, None, None, :]
    s = sin[:, None, None, :]
    x1 = x[..., :half].astype(jnp.float32)
    x2 = x[..., half:ROPE_DIM].astype(jnp.float32)
    rot = jnp.concatenate([x1 * c - x2 * s, x2 * c + x1 * s], axis=-1)
    return jnp.concatenate([rot.astype(x.dtype), x[..., ROPE_DIM:]], axis=-1)

def diff_attn_branch(u, lq1, lk1, lq2, lk2, subln_w, w_o, lambda_init):
    f32 = jnp.float32
    B, S, _ = u.shape
    H, DH, DV = DA_HEADS, DA_HEAD_DIM, DA_V_DIM
    q = u[..., :DA_QK_WIDTH].reshape(B, S, H, 2, DH)
    k = u[..., DA_QK_WIDTH:2 * DA_QK_WIDTH].reshape(B, S, H, 2, DH)
    v = u[..., 2 * DA_QK_WIDTH:].reshape(B, S, H, DV)
    cos, sin = rope_tables(S)
    q = partial_rope(q, cos, sin) * (DH ** -0.5)
    k = partial_rope(k, cos, sin)
    lam = (jnp.exp(jnp.sum(lq1.astype(f32) * lk1.astype(f32)))
           - jnp.exp(jnp.sum(lq2.astype(f32) * lk2.astype(f32))) + lambda_init)

    kt = k.transpose(0, 2, 3, 1, 4)
    vt = v.transpose(0, 2, 1, 3)
    n_blk = S // Q_BLOCK
    qb = q.reshape(B, n_blk, Q_BLOCK, H, 2, DH).transpose(1, 0, 3, 4, 2, 5)

    def block(q_blk):
        s = jnp.einsum('bhcqd,bhckd->bhcqk', q_blk, kt).astype(f32)
        pr = jax.nn.softmax(s, axis=-1)
        pd = pr[:, :, 0] - lam * pr[:, :, 1]
        return jnp.einsum('bhqk,bhkv->bhqv', pd.astype(vt.dtype), vt)

    o = lax.map(block, qb)
    o = o.transpose(1, 0, 3, 2, 4).reshape(B, S, H, DV).astype(f32)
    o = o * lax.rsqrt(jnp.mean(o * o, axis=-1, keepdims=True) + SUBLN_EPS)
    o = o * subln_w.astype(f32) * (1.0 - lambda_init)
    return o.reshape(B, S, DA_V_WIDTH).astype(w_o.dtype) @ w_o

def first_inputs(seed: int = 0) -> dict:
    key = jax.random.key(seed)
    ks = iter(jax.random.split(key, 40))
    L, D, W = DEPTH, D_MODEL, RWKV_WIDTH
    f32 = jnp.float32

    def nrm(shape, scale):
        return jax.random.normal(next(ks), shape, f32) * scale

    def gain(shape):
        return 1.0 + 0.05 * jax.random.normal(next(ks), shape, f32)

    def unif(shape, lo, hi):
        return jax.random.uniform(next(ks), shape, f32, lo, hi)

    return {
        "x": nrm((BATCH, SEQ, D), 1.0),
        "p": nrm((DEPTH, BATCH, SEQ, PLE_DIM), 1.0),
        "norm_mix": gain((L, D)),
        "w_in": nrm((L, D, IN_COLS), D ** -0.5),
        "shift_mu_prev": unif((L, RWKV_COLS), 0.0, 0.5),
        "shift_mu_next": unif((L, RWKV_COLS), 0.0, 0.5),
        "rwkv_w0": unif((L, N_DIR, W), -6.0, 1.0),
        "rwkv_w2": nrm((L, N_DIR, DECAY_LORA, W), 0.1 * DECAY_LORA ** -0.5),
        "rwkv_a0": nrm((L, N_DIR, W), 0.5),
        "rwkv_a2": nrm((L, N_DIR, ICLR_LORA, W), 0.1 * ICLR_LORA ** -0.5),
        "rwkv_g2": nrm((L, GATE_LORA, W), GATE_LORA ** -0.5),
        "rwkv_k_k": 0.85 + 0.05 * jax.random.normal(next(ks), (L, W), f32),
        "rwkv_k_a": gain((L, W)),
        "rwkv_r_k": nrm((L, RWKV_HEADS, RWKV_HEAD_DIM), 0.1),
        "rwkv_ln_w": gain((L, W)),
        "rwkv_ln_b": nrm((L, W), 0.01),
        "rwkv_w_o": nrm((L, W, D), W ** -0.5),
        "da_lq1": nrm((L, DA_HEAD_DIM), 0.1),
        "da_lk1": nrm((L, DA_HEAD_DIM), 0.1),
        "da_lq2": nrm((L, DA_HEAD_DIM), 0.1),
        "da_lk2": nrm((L, DA_HEAD_DIM), 0.1),
        "da_subln_w": gain((L, DA_V_DIM)),
        "da_w_o": nrm((L, DA_V_WIDTH, D), DA_V_WIDTH ** -0.5),
        "w_out": nrm((L, D, D), D ** -0.5),
        "norm_ffn": gain((L, D)),
        "w_ff1": nrm((L, D, D_FF), D ** -0.5),
        "w_ff2": nrm((L, D_FF, D), D_FF ** -0.5),
        "norm_ple": gain((L, D)),
        "w_ple_gate": nrm((L, D, D), D ** -0.5),
        "w_ple_proj": nrm((L, PLE_DIM, D), PLE_DIM ** -0.5),
        "norm_final": gain((D,)),
    }

def first_block(x, p, norm_mix, w_in, shift_mu_prev, shift_mu_next, rwkv_w0, rwkv_w2, rwkv_a0,
              rwkv_a2, rwkv_g2, rwkv_k_k, rwkv_k_a, rwkv_r_k, rwkv_ln_w, rwkv_ln_b, rwkv_w_o,
              da_lq1, da_lk1, da_lq2, da_lk2, da_subln_w, da_w_o, w_out, norm_ffn, w_ff1, w_ff2,
              norm_ple, w_ple_gate, w_ple_proj, norm_final):
    B, S, D = x.shape
    for i in range(DEPTH):
        lambda_init = 0.8 - 0.6 * math.exp(-0.3 * i)
        h = rmsnorm(x, norm_mix[i])
        u = h @ w_in[i]
        u_rwkv = u[..., :RWKV_COLS]
        u_da = u[..., RWKV_COLS:RWKV_COLS + DA_COLS]
        gates = jax.nn.sigmoid(u[..., RWKV_COLS + DA_COLS:].astype(jnp.float32)).reshape(B, S, N_BRANCH, D)
        y_a = rwkv7_branch(u_rwkv, shift_mu_prev[i], shift_mu_next[i], rwkv_w0[i], rwkv_w2[i],
                           rwkv_a0[i], rwkv_a2[i], rwkv_g2[i], rwkv_k_k[i], rwkv_k_a[i], rwkv_r_k[i],
                           rwkv_ln_w[i], rwkv_ln_b[i], rwkv_w_o[i])
        y_b = diff_attn_branch(u_da, da_lq1[i], da_lk1[i], da_lq2[i], da_lk2[i], da_subln_w[i],
                               da_w_o[i], lambda_init)
        merged = (gates[:, :, 0] * y_a.astype(jnp.float32)
                  + gates[:, :, 1] * y_b.astype(jnp.float32)).astype(x.dtype)
        x = x + merged @ w_out[i]
        h = rmsnorm(x, norm_ffn[i])
        x = x + jnp.square(jax.nn.relu(h @ w_ff1[i])) @ w_ff2[i]
        h = rmsnorm(x, norm_ple[i])
        x = x + jax.nn.sigmoid(h @ w_ple_gate[i]) * (p[i] @ w_ple_proj[i])
    return rmsnorm(x, norm_final)


CTX_LEN = 256
GRID_W = 64

RET_HEADS = 4
RET_DK = 128
RET_DV = 128
RET_CHUNK = 128
RET_W = RET_HEADS * RET_DV
RET_SCALE = RET_DK ** -0.5

ATT_HEADS = 8
ATT_KV_HEADS = 2
ATT_GROUP = ATT_HEADS // ATT_KV_HEADS
ATT_HD = 64
ATT_W = ATT_HEADS * ATT_HD
ATT_SCALE = ATT_HD ** -0.5

MIX_W = RET_W + ATT_W
D_FF_2 = 4 * D_MODEL
ROPE_BASE = 10000.0
EPS = 1e-6

RQ_OFF = 0
RK_OFF = RQ_OFF + RET_HEADS * RET_DK
RV_OFF = RK_OFF + RET_HEADS * RET_DK
RG_OFF = RV_OFF + RET_W
AQ_OFF = RG_OFF + RET_W
AK_OFF = AQ_OFF + ATT_W
AV_OFF = AK_OFF + ATT_KV_HEADS * ATT_HD
D_IN = AV_OFF + ATT_KV_HEADS * ATT_HD
SPLIT_IDX = [RK_OFF, RV_OFF, RG_OFF, AQ_OFF, AK_OFF, AV_OFF]


def _rmsnorm(x, g):
    xf = x.astype(jnp.float32)
    y = xf * lax.rsqrt(jnp.mean(xf * xf, axis=-1, keepdims=True) + EPS)
    return (y * g.astype(jnp.float32)).astype(x.dtype)

def _modulate(h, shift, scale):
    return h * (1 + scale) + shift

def _freqs(n_pairs):
    return ROPE_BASE ** (-jnp.arange(n_pairs, dtype=jnp.float32) / n_pairs)

def _apply_rope(x, cos, sin):
    x1, x2 = jnp.split(x, 2, axis=-1)
    return jnp.concatenate([x1 * cos - x2 * sin, x1 * sin + x2 * cos], axis=-1).astype(x.dtype)

def _heads(t, n_heads):
    B, L, W = t.shape
    return t.reshape(B, L, n_heads, W // n_heads).transpose(0, 2, 1, 3)

def _retention_chunkwise(q, k, v, log_gamma, s0):
    B, H, L, dk = q.shape
    dv = v.shape[-1]
    n_chunks = L // RET_CHUNK

    def chunks(t):
        return jnp.moveaxis(t.reshape(B, H, n_chunks, RET_CHUNK, t.shape[-1]), 2, 0)

    idx = jnp.arange(RET_CHUNK, dtype=jnp.float32)
    lg = log_gamma.astype(jnp.float32)[:, None]
    rel = idx[:, None] - idx[None, :]
    intra = jnp.where(rel >= 0, jnp.exp(lg[:, :, None] * jnp.maximum(rel, 0.0)), 0.0)
    q_dec = jnp.exp(lg * (idx + 1.0))[:, :, None]
    k_dec = jnp.exp(lg * (RET_CHUNK - 1.0 - idx))[:, :, None]
    c_dec = jnp.exp(lg * RET_CHUNK)[:, :, None]

    def step(state, qkv):
        qf, kf, vf = (t.astype(jnp.float32) for t in qkv)
        scores = jnp.einsum('bhid,bhjd->bhij', qf, kf) * intra
        o = (jnp.einsum('bhij,bhjv->bhiv', scores, vf)
             + jnp.einsum('bhid,bhdv->bhiv', qf, state) * q_dec)
        state = state * c_dec + jnp.einsum('bhjd,bhjv->bhdv', kf * k_dec, vf)
        return state, o

    s_fin, o = lax.scan(step, s0, (chunks(q), chunks(k), chunks(v)))
    o = jnp.moveaxis(o, 0, 2).reshape(B, H, L, dv)
    return o, s_fin

def _retention_final_state(k, v, log_gamma):
    L = k.shape[2]
    pos = jnp.arange(L, dtype=jnp.float32)
    w = jnp.exp(log_gamma.astype(jnp.float32)[:, None] * (L - 1.0 - pos))
    return jnp.einsum('bhld,bhlv->bhdv', k.astype(jnp.float32) * w[:, :, None], v.astype(jnp.float32))

def _flip(t):
    return jnp.flip(t, axis=2)

def _bidir_retention(q, k, v, log_gamma, s0_fwd, s0_bwd):
    o_f, s_f = _retention_chunkwise(q, k, v, log_gamma[0], s0_fwd)
    o_b, s_b = _retention_chunkwise(_flip(q), _flip(k), _flip(v), log_gamma[1], s0_bwd)
    return o_f + _flip(o_b), s_f, s_b

def _ret_out(o, gate, gn_g):
    B, H, L, dv = o.shape
    mu = jnp.mean(o, axis=-1, keepdims=True)
    var = jnp.mean(jnp.square(o - mu), axis=-1, keepdims=True)
    o = ((o - mu) * lax.rsqrt(var + EPS)).transpose(0, 2, 1, 3).reshape(B, L, H * dv)
    o = o * gn_g.astype(jnp.float32)
    return (o * jax.nn.silu(gate.astype(jnp.float32))).astype(gate.dtype)

def _dense_attention(q, k, v):
    s = jnp.einsum('bqkgd,bskd->bkgqs', q, k).astype(jnp.float32) * ATT_SCALE
    p = jax.nn.softmax(s, axis=-1).astype(v.dtype)
    return jnp.einsum('bkgqs,bskd->bqkgd', p, v)

def _latent_attention(q, k_lat, v_lat, k_ctx, v_ctx):
    B, L = q.shape[:2]
    k_all = jnp.concatenate([k_ctx, k_lat], axis=1)
    v_all = jnp.concatenate([v_ctx, v_lat], axis=1)
    qb = jnp.moveaxis(q.reshape(B, L // Q_BLOCK, Q_BLOCK, ATT_KV_HEADS, ATT_GROUP, ATT_HD), 1, 0)
    o = lax.map(lambda qblk: _dense_attention(qblk, k_all, v_all), qb)
    return jnp.moveaxis(o, 0, 1).reshape(B, L, ATT_W)

def _sqrelu_mlp(h, w1, w2):
    return jnp.square(jax.nn.relu(h @ w1)) @ w2

def _layer(x, xc, c_act, cc_act, w_mod, b_mod, norm1_g, norm2_g, w_in, w_out,
           ret_log_rate, ret_gn_g, q_norm_g, k_norm_g, w_ff1, w_ff2,
           ret_cs, att_cs, ctx_out):
    B, L, _ = x.shape
    Lc = xc.shape[1]
    mod = (c_act @ w_mod + b_mod)[:, None, :]
    mod_c = (cc_act @ w_mod + b_mod)[None, None, :]
    sh1, sc1, g1, sh2, sc2, g2 = jnp.split(mod, 6, axis=-1)
    csh1, csc1, cg1, csh2, csc2, cg2 = jnp.split(mod_c, 6, axis=-1)
    log_gamma = jnp.log1p(-jnp.exp(ret_log_rate.astype(jnp.float32)))

    h = _modulate(_rmsnorm(x, norm1_g), sh1, sc1)
    hc = _modulate(_rmsnorm(xc, norm1_g), csh1, csc1)
    rq, rk, rv, rg, aq, ak, av = jnp.split(h @ w_in, SPLIT_IDX, axis=-1)
    if ctx_out:
        crq, crk, crv, crg, caq, cak, cav = jnp.split(hc @ w_in, SPLIT_IDX, axis=-1)
    else:
        crk, crv = jnp.split(hc @ w_in[:, RK_OFF:RG_OFF], 2, axis=-1)
        cak, cav = jnp.split(hc @ w_in[:, AK_OFF:D_IN], 2, axis=-1)

    crk_h = _heads(crk, RET_HEADS) * RET_SCALE
    crv_h = _heads(crv, RET_HEADS)
    if ctx_out:
        zeros = jnp.zeros((B, RET_HEADS, RET_DK, RET_DV), jnp.float32)
        ret_c, s_f, s_b = _bidir_retention(_heads(crq, RET_HEADS), crk_h, crv_h, log_gamma, zeros, zeros)
    else:
        s_f = _retention_final_state(crk_h, crv_h, log_gamma[0])
        s_b = _retention_final_state(_flip(crk_h), _flip(crv_h), log_gamma[1])
    rq_h = _apply_rope(_heads(rq, RET_HEADS), *ret_cs)
    rk_h = _apply_rope(_heads(rk, RET_HEADS), *ret_cs) * RET_SCALE
    ret, _, _ = _bidir_retention(rq_h, rk_h, _heads(rv, RET_HEADS), log_gamma, s_f, s_b)
    ret = _ret_out(ret, rg, ret_gn_g)

    q = _apply_rope(_rmsnorm(aq.reshape(B, L, ATT_HEADS, ATT_HD), q_norm_g), *att_cs)
    k = _apply_rope(_rmsnorm(ak.reshape(B, L, ATT_KV_HEADS, ATT_HD), k_norm_g), *att_cs)
    v = av.reshape(B, L, ATT_KV_HEADS, ATT_HD)
    kc = _rmsnorm(cak.reshape(B, Lc, ATT_KV_HEADS, ATT_HD), k_norm_g)
    vc = cav.reshape(B, Lc, ATT_KV_HEADS, ATT_HD)
    att = _latent_attention(q.reshape(B, L, ATT_KV_HEADS, ATT_GROUP, ATT_HD), k, v, kc, vc)

    x = x + g1 * (jnp.concatenate([ret, att], axis=-1) @ w_out)

    h2 = _modulate(_rmsnorm(x, norm2_g), sh2, sc2)
    x = x + g2 * _sqrelu_mlp(h2, w_ff1, w_ff2)

    if ctx_out:
        ret_c = _ret_out(ret_c, crg, ret_gn_g)
        qc = _rmsnorm(caq.reshape(B, Lc, ATT_KV_HEADS, ATT_GROUP, ATT_HD), q_norm_g)
        att_c = _dense_attention(qc, kc, vc).reshape(B, Lc, ATT_W)
        xc = xc + cg1 * (jnp.concatenate([ret_c, att_c], axis=-1) @ w_out)
        hc2 = _modulate(_rmsnorm(xc, norm2_g), csh2, csc2)
        xc = xc + cg2 * _sqrelu_mlp(hc2, w_ff1, w_ff2)
    return x, xc

def second_inputs(seed: int = 0) -> dict:
    key = jax.random.key(seed)
    ks = jax.random.split(key, 17)
    f32 = jnp.float32
    nrm = lambda k, shape, s: jax.random.normal(k, shape, f32) * s
    base_rate = -(5.0 + jnp.arange(RET_HEADS, dtype=f32)) * np.float32(np.log(2.0))
    return {
        "x": nrm(ks[0], (BATCH, SEQ, D_MODEL), 1.0),
        "c": nrm(ks[1], (BATCH, D_MODEL), 1.0),
        "ctx": nrm(ks[2], (BATCH, CTX_LEN, D_MODEL), 1.0),
        "c_ctx": nrm(ks[3], (D_MODEL,), 1.0),
        "w_mod": nrm(ks[4], (DEPTH, D_MODEL, 6 * D_MODEL), 0.01),
        "b_mod": nrm(ks[5], (DEPTH, 6 * D_MODEL), 0.02),
        "norm1_g": 1.0 + nrm(ks[6], (DEPTH, D_MODEL), 0.02),
        "norm2_g": 1.0 + nrm(ks[7], (DEPTH, D_MODEL), 0.02),
        "w_in": nrm(ks[8], (DEPTH, D_MODEL, D_IN), D_MODEL ** -0.5),
        "w_out": nrm(ks[9], (DEPTH, MIX_W, D_MODEL), MIX_W ** -0.5),
        "ret_log_rate": base_rate[None, None, :] + nrm(ks[10], (DEPTH, 2, RET_HEADS), 0.05),
        "ret_gn_g": 1.0 + nrm(ks[11], (DEPTH, RET_W), 0.02),
        "q_norm_g": 1.0 + nrm(ks[12], (DEPTH, ATT_HD), 0.02),
        "k_norm_g": 1.0 + nrm(ks[13], (DEPTH, ATT_HD), 0.02),
        "w_ff1": nrm(ks[14], (DEPTH, D_MODEL, D_FF_2), D_MODEL ** -0.5),
        "w_ff2": nrm(ks[15], (DEPTH, D_FF_2, D_MODEL), D_FF_2 ** -0.5),
        "final_norm_g": 1.0 + nrm(ks[16], (D_MODEL,), 0.02),
    }

def second_block(x, c, ctx, c_ctx, w_mod, b_mod, norm1_g, norm2_g, w_in, w_out,
              ret_log_rate, ret_gn_g, q_norm_g, k_norm_g, w_ff1, w_ff2, final_norm_g):
    L = x.shape[1]
    ROWS = L // GRID_W
    t = jnp.arange(L, dtype=jnp.float32)
    ret_ang = t[:, None] * _freqs(RET_DK // 2)
    ret_cs = (jnp.cos(ret_ang), jnp.sin(ret_ang))
    row = jnp.repeat(jnp.arange(ROWS, dtype=jnp.float32), GRID_W)
    col = jnp.tile(jnp.arange(GRID_W, dtype=jnp.float32), ROWS)
    af = _freqs(ATT_HD // 4)
    att_ang = jnp.concatenate([row[:, None] * af, col[:, None] * af], axis=-1)[:, None, :]
    att_cs = (jnp.cos(att_ang), jnp.sin(att_ang))

    c_act = jax.nn.silu(c)
    cc_act = jax.nn.silu(c_ctx)
    xc = ctx
    for l in range(DEPTH):
        x, xc = _layer(x, xc, c_act, cc_act, w_mod[l], b_mod[l], norm1_g[l], norm2_g[l],
                       w_in[l], w_out[l], ret_log_rate[l], ret_gn_g[l], q_norm_g[l], k_norm_g[l],
                       w_ff1[l], w_ff2[l], ret_cs, att_cs, l < DEPTH - 1)
    return _rmsnorm(x, final_norm_g)


def setup_inputs(seed=0):
    out = dict(first_inputs(seed))
    for name, value in second_inputs(seed + 1).items():
        if name != "x":
            out[name + "_2"] = value
    return out


def reference(
    x, p, norm_mix, w_in, shift_mu_prev, shift_mu_next, rwkv_w0, rwkv_w2, rwkv_a0, rwkv_a2,
    rwkv_g2, rwkv_k_k, rwkv_k_a, rwkv_r_k, rwkv_ln_w, rwkv_ln_b, rwkv_w_o, da_lq1, da_lk1,
    da_lq2, da_lk2, da_subln_w, da_w_o, w_out, norm_ffn, w_ff1, w_ff2, norm_ple, w_ple_gate,
    w_ple_proj, norm_final, c_2, ctx_2, c_ctx_2, w_mod_2, b_mod_2, norm1_g_2, norm2_g_2, w_in_2,
    w_out_2, ret_log_rate_2, ret_gn_g_2, q_norm_g_2, k_norm_g_2, w_ff1_2, w_ff2_2,
    final_norm_g_2,
):
    x = first_block(
        x, p, norm_mix, w_in, shift_mu_prev, shift_mu_next, rwkv_w0, rwkv_w2, rwkv_a0, rwkv_a2,
        rwkv_g2, rwkv_k_k, rwkv_k_a, rwkv_r_k, rwkv_ln_w, rwkv_ln_b, rwkv_w_o, da_lq1, da_lk1,
        da_lq2, da_lk2, da_subln_w, da_w_o, w_out, norm_ffn, w_ff1, w_ff2, norm_ple, w_ple_gate,
        w_ple_proj, norm_final,
    )
    return second_block(
        x, c_2, ctx_2, c_ctx_2, w_mod_2, b_mod_2, norm1_g_2, norm2_g_2, w_in_2, w_out_2,
        ret_log_rate_2, ret_gn_g_2, q_norm_g_2, k_norm_g_2, w_ff1_2, w_ff2_2, final_norm_g_2,
    )


_drawn_inputs = setup_inputs


def setup_inputs(seed=0):
    import zlib

    import numpy as np

    out = dict(_drawn_inputs(seed))
    spreads = {}
    factors = {'rwkv_w2': 8.0,
     'rwkv_a2': 7.043,
     'rwkv_k_k': 4.258,
     'rwkv_k_a': 3.56,
     'rwkv_ln_w': 4.355,
     'rwkv_ln_b': 8.0,
     'da_lk1': 5.232,
     'da_lq2': 5.833,
     'da_lk2': 8.0,
     'da_subln_w': 2.758,
     'norm_ple': 8.0,
     'c_ctx_2': 3.975,
     'norm1_g_2': 8.0,
     'norm2_g_2': 22.745,
     'ret_gn_g_2': 8.0,
     'q_norm_g_2': 8.0,
     'k_norm_g_2': 8.0,
     'final_norm_g_2': 7.596}
    for name, (base, spread) in spreads.items():
        noise = np.random.default_rng([zlib.crc32(name.encode()), seed]).standard_normal(out[name].shape)
        drawn = base * np.exp(spread * noise) if base else spread * noise
        out[name] = jnp.asarray(drawn.astype(out[name].dtype))
    for name, factor in factors.items():
        out[name] = (out[name] * factor).astype(out[name].dtype)
    return out
```

```python
from contextlib import ExitStack

import numpy as np

import concourse.bass as bass
from concourse import mybir

F32 = mybir.dt.float32
F32R = mybir.dt.float32r
ALU = mybir.AluOpType
ACT = mybir.ActivationFunctionType
AX_X = mybir.AxisListType.X

P = 128
D = 1024
T = 512
TC = 256
KT = D // P
TB = T // P

RW = 512
RT = RW // P
CH = 64
NCH = T // CH
R_TILES = 15
DA_HEADS = 4
FF_GROUPS = 4
RMS_EPS = 1e-6
GN_EPS = 64e-5
SUBLN_EPS = 1e-5
LAMBDA_INIT = 0.8 - 0.6
DECAY_RATE = float(np.exp(-0.5))

RET_HEADS = 4
RET_SCALE = 128 ** -0.5
ATT_TILES = 4
ATT_SCALE = 64 ** -0.5
KEYS = TC + T
CTX_T = TC // P
KEY_T = KEYS // P

PARAM_COLS = {}
_at = 0
for _name, _n in (("norm_mix", 8), ("mu_prev", 15), ("mu_next", 15), ("w0", 8), ("a0", 8), ("k_k", 4),
                  ("k_a", 4), ("r_k", 4), ("ln_w", 4), ("ln_b", 4), ("subln", 1), ("norm_ffn", 8),
                  ("norm_ple", 8), ("norm_final", 8), ("b_mod", 48), ("norm1", 8), ("norm2", 8),
                  ("gn_g", 4), ("q_norm", 1), ("k_norm", 1), ("final2", 8), ("c", 8), ("c_ctx", 8),
                  ("lam", 4), ("rate", 8)):
    PARAM_COLS[_name] = (_at, _n)
    _at += _n
N_PARAMS = _at


def rope_rotation(half):
    width = 2 * half[1]
    out = np.zeros((P, P), np.float32)
    for base in range(0, P, half[0]):
        for m in range(half[1]):
            out[base + m + half[1], base + m] = -1.0
            out[base + m, base + m + half[1]] = 1.0
    assert width <= half[0]
    return out


def shape_constants():
    f = np.float32
    i = np.arange(P)
    same_chunk = (i[:, None] // CH) == (i[None, :] // CH)
    out = {
        "ident": np.eye(P, dtype=f),
        "ones": np.ones((P, P), f),
        "head_ones": ((i[:, None] // 64) == (i[None, :] // 64)).astype(f),
        "head_mean": ((i[:, None] // 64) == (i[None, :] // 64)).astype(f) / f(64),
        "ident64": (i[:, None] % 64 == np.arange(64)[None, :]).astype(f),
        "rot_da": rope_rotation((64, 8)),
        "rot_att": rope_rotation((64, 32)),
        "rot_ret": rope_rotation((128, 64)),
    }
    t = np.arange(T)
    out["keep"] = np.concatenate([np.broadcast_to((t % CH != first).astype(f), (P, T))
                                  for first in (0, CH - 1)], 1)
    before = [i[:, None] < i[None, :], i[:, None] > i[None, :]]
    out["strict"] = np.concatenate([(b & same_chunk).astype(f) for b in before], 1)
    out["incl"] = np.concatenate([((b | (i[:, None] == i[None, :])) & same_chunk).astype(f) for b in before], 1)
    pair = (i[:, None] // 2) == (i[None, :] // 2)
    out["pair"] = np.concatenate([(b & pair).astype(f) for b in before], 1)
    levels = []
    for d in range(2):
        for s in (2, 4, 8, 16, 32):
            cols = i[(i // s) % 2 == d]
            rows = (i // s) % 2 == 1 - d
            levels.append((rows[:, None] & ((i[:, None] // (2 * s)) == (cols[None, :] // (2 * s)))).astype(f))
    out["level"] = np.concatenate(levels, 1)
    out["eps"] = np.broadcast_to(np.array([RMS_EPS, GN_EPS, SUBLN_EPS, 10 * np.log(2.0), 0.0, 1.0], f), (P, 6))

    def per_channel(cos, sin):
        return np.concatenate([np.asarray(cos, f).T, np.asarray(sin, f).T], 1)

    pos = np.arange(T, dtype=f)
    inv = f(500000.0) ** (-np.arange(0, 16, 2, dtype=f) / f(16))
    ang = pos[:, None] * inv[None, :]
    cos, sin = np.ones((T, 64), f), np.zeros((T, 64), f)
    cos[:, 0:8] = cos[:, 8:16] = np.cos(ang)
    sin[:, 0:8] = sin[:, 8:16] = np.sin(ang)
    out["rope_da"] = per_channel(np.tile(cos, (1, 2)), np.tile(sin, (1, 2)))
    fr = f(10000.0) ** (-np.arange(64, dtype=f) / f(64))
    ang = pos[:, None] * fr
    out["rope_ret"] = per_channel(np.tile(np.cos(ang), (1, 2)), np.tile(np.sin(ang), (1, 2)))
    af = f(10000.0) ** (-np.arange(16, dtype=f) / f(16))
    row, col = (t // 64).astype(f), (t % 64).astype(f)
    ang = np.concatenate([row[:, None] * af, col[:, None] * af], -1)
    out["rope_att"] = per_channel(np.tile(np.cos(ang), (1, 4)), np.tile(np.sin(ang), (1, 4)))
    rel = (np.arange(896)[None, :] - 384 - i[:, None]).astype(f)
    out["rel"] = np.concatenate([np.maximum(rel, 0), np.maximum(-rel, 0), (rel >= 0).astype(f), (rel <= 0).astype(f)], 1)
    out["steps"] = np.concatenate([np.broadcast_to(pos + 1, (P, T)), np.broadcast_to(T - pos, (P, T))], 1)
    l = i[:, None] + P * np.arange(CTX_T)[None, :]
    out["ctx_steps"] = np.concatenate([TC - 1 - l, l], 1)
    return {k: np.ascontiguousarray(v, dtype=f) for k, v in out.items()}


CONST_SHAPES = {k: v.shape for k, v in shape_constants().items()}


STREAM = ([("w_da", 0, 12, 8, True), ("w_rwkv", 0, 15, 8, True)]
          + [e for n in range(8) for e in (("w_gate", n, 1, 8, True), ("w_rwkv_o", n, 1, 4, True),
                                           ("w_gate", 8 + n, 1, 8, True), ("w_da_o", n, 1, 4, True))]
          + [("w_out", 0, 8, 8, True)])


def ff_order():
    out = [("up", 0)]
    for g in range(1, FF_GROUPS):
        out += [("up", g), ("down", g - 1)]
    return out + [("down", FF_GROUPS - 1)]


def ff_stream(up, down):
    return [(up if kind == "up" else down, 8 * g, 8, 8, True) for kind, g in ff_order()]


STREAM += ff_stream("w_ff1", "w_ff2")
STREAM += [e for n in range(8) for e in (("w_ple_gate", n, 1, 8, True), ("w_ple_proj", n, 1, 2, True))]
STREAM += [("w_in2", 0, 22, 8, True), ("w_out2", 0, 8, 8, True)]
STREAM += ff_stream("w_ff1_2", "w_ff2_2")
TILES = [(name, first + j, kt, split) for name, first, n, kt, split in STREAM for j in range(n)]
WEIGHTS = {name: (max(t for m, t, _, _ in TILES if m == name) + 1, kt) for name, _, kt, _ in TILES}

RAW_SLOTS = 4
SPLIT_SLOTS = 3
AHEAD = 2
MOD_PARTS = 6
MOD_SLOTS = 2
BANKS = 4


class Job:

    def __init__(self, weight, moving, width=T):
        self.weight, self.moving, self.width = weight, moving, width


class Program:

    def __init__(self, nc, ctx, dram):
        self.nc, self.ctx, self.dram = nc, ctx, dram
        self.pair = [ctx.enter_context(nc.psum_tensor(f"pair{i}", [P, 1024], F32)) for i in range(4)]
        self.bank = [self.pair[i // 2][:, 512 * (i % 2):512 * (i % 2) + 512] for i in range(8)]
        self.raw = self.tile("w_raw", [P, RAW_SLOTS, 1024])
        self.raw_landed = [self.sem(f"raw_landed{i}") for i in range(RAW_SLOTS)]
        self.hi_made, self.lo_made = self.sem("w_hi_made"), self.sem("w_lo_made")
        self.job_done = self.sem("job_done")
        self.norm_sems = [self.sem("norm_" + k) for k in ("sq", "sum", "log", "rstd", "y", "hi", "lo", "x")]
        self.norms = self.norms_split = self.norm_sums = self.norm_befores = 0
        self.streamed = 0
        self.taken = 0
        self.jobs = 0
        self.splits = 0
        self.split_no = {}
        self.last_job = {}
        self.split_slot = {}

    def sem(self, name):
        return self.ctx.enter_context(self.nc.semaphore(name))

    def stage_sems(self, prefix, names):
        return {k: self.nc.alloc_semaphore(name=prefix + k) for k in names}

    def release(self, sems):
        self.nc.clear_and_free_semaphores(list(sems.values()))
        self.nc.all_engine_barrier()

    def tile(self, name, shape, dtype=F32, ctx=None):
        return (ctx or self.ctx).enter_context(self.nc.sbuf_tensor(name, shape, dtype))

    def plan(self, jobs):
        self.first_job = self.jobs
        self.first_tile = self.taken
        for job in jobs:
            if job.weight not in self.last_job:
                assert job.weight == self.taken
                self.taken += 1
                if TILES[job.weight][3]:
                    self.split_slot[self.splits] = job.weight
                    self.splits += 1
                    self.split_no[job.weight] = self.splits
            self.jobs += 1
            self.last_job[job.weight] = self.jobs

    def stream(self, sp, until):
        for w in range(self.streamed, min(until, len(TILES))):
            name, tile, kt, split = TILES[w]
            old = w - RAW_SLOTS
            if old >= 0 and TILES[old][3]:
                sp.wait_ge(self.lo_made, self.split_no[old])
            elif old >= 0:
                sp.wait_ge(self.job_done, self.last_job[old])
            sp.dma_start(self.raw[:, w % RAW_SLOTS, 0:kt * P], self.dram[name][tile])\
                .then_inc(self.raw_landed[w % RAW_SLOTS], 16)
        self.streamed = max(self.streamed, min(until, len(TILES)))

    def landed(self, w):
        return self.raw_landed[w % RAW_SLOTS], 16 * (w // RAW_SLOTS + 1)


def gemm_block(pr, hi, lo, jobs, act_step, dve_step, evac_sem, evac_at, pe_wait=None,
               bank0=0, pool_step=None, pe_after=None, act_after=None):
    nc = pr.nc
    pr.plan(jobs)
    first, tiles = pr.first_job, range(pr.first_tile, pr.taken)
    of_tile = {w: [n for n, job in enumerate(jobs) if job.weight == w] for w in tiles}

    def bank(n):
        return pr.bank[bank0 + n % BANKS]

    with nc.Block() as block:
        @block.sync
        def _(sp):
            pr.stream(sp, pr.taken + RAW_SLOTS)

        @block.tensor
        def _(pe):
            for n, job in enumerate(jobs):
                w = job.weight
                kt = TILES[w][2]
                slot = (pr.split_no[w] - 1) % SPLIT_SLOTS
                if n == of_tile[w][0]:
                    pe.wait_ge(pr.lo_made, pr.split_no[w])
                if n >= BANKS and evac_at is not None:
                    pe.wait_ge(evac_sem, evac_at(n - BANKS))
                if pe_wait is not None:
                    pe_wait(pe, n)
                out = bank(n)[:, 0:job.width]
                for k in range(kt):
                    w_hi, w_lo = hi[:, slot, k * P:(k + 1) * P], lo[:, slot, k * P:(k + 1) * P]
                    x_hi, x_lo = job.moving[k]
                    nc.tensor.matmul(out, w_hi, x_hi, start=(k == 0), stop=False)
                    nc.tensor.matmul(out, w_hi, x_lo, start=False, stop=False)
                    last = nc.tensor.matmul(out, w_lo, x_hi, start=False, stop=(k == kt - 1))
                last.then_inc(pr.job_done, 1)
            if pe_after is not None:
                pe_after(pe)

        @block.gpsimd
        def _(pool):
            if pool_step is not None:
                pool_step(pool)

        @block.scalar
        def _(act):
            for i in range(len(tiles) + AHEAD):
                if i < len(tiles):
                    w = tiles[i]
                    s = pr.split_no[w] - 1
                    act.wait_ge(*pr.landed(w))
                    if s >= SPLIT_SLOTS:
                        act.wait_ge(pr.job_done, pr.last_job[pr.split_slot[s - SPLIT_SLOTS]])
                    cols = TILES[w][2] * P
                    nc.scalar.copy(hi[:, s % SPLIT_SLOTS, 0:cols], pr.raw[:, w % RAW_SLOTS, 0:cols])\
                        .then_inc(pr.hi_made, 1)
                if i >= AHEAD:
                    for n in of_tile[tiles[i - AHEAD]]:
                        act_step(act, n, bank(n), first + n + 1)
            if act_after is not None:
                act_after(act)

        @block.vector
        def _(dve):
            for i in range(len(tiles) + AHEAD):
                if i < len(tiles):
                    w = tiles[i]
                    s = pr.split_no[w] - 1
                    cols = TILES[w][2] * P
                    dve.wait_ge(*pr.landed(w))
                    dve.wait_ge(pr.hi_made, s + 1)
                    if s >= SPLIT_SLOTS:
                        dve.wait_ge(pr.job_done, pr.last_job[pr.split_slot[s - SPLIT_SLOTS]])
                    nc.vector.tensor_tensor(lo[:, s % SPLIT_SLOTS, 0:cols], pr.raw[:, w % RAW_SLOTS, 0:cols],
                                            hi[:, s % SPLIT_SLOTS, 0:cols].bitcast(F32), ALU.subtract)\
                        .then_inc(pr.lo_made, 1)
                if i >= AHEAD:
                    for n in of_tile[tiles[i - AHEAD]]:
                        dve_step(dve, n, bank(n), first + n + 1)


def copy_out(pr, evac, dest, func=ACT.Copy, scale=1.0):
    def act_step(act, n, bank, done):
        act.wait_ge(pr.job_done, done)
        out = dest(n)
        pr.nc.scalar.activation(out, bank[:, 0:out.shape[-1]], func, scale=scale(n) if callable(scale) else scale)\
            .then_inc(evac, 1)
    return act_step


def nothing(*_):
    pass


class NormAhead:

    def __init__(self, pr, sq, rstd):
        self.pr, self.sq, self.rstd, self.uses, self.splits = pr, sq, rstd, -1, 0
        self.sq_made, self.summed, self.log_made, self.rstd_made, self.hi_made, self.lo_made = (
            pr.sem("ahead_" + k) for k in ("sq", "sum", "log", "rstd", "hi", "lo"))

    def begin(self, x, gain=None, x_hi=None, x_lo=None):
        self.x, self.gain, self.x_hi, self.x_lo = x, gain, x_hi, x_lo
        self.uses += 1
        self.base = KT * self.uses
        self.split_base = KT * self.splits
        self.splits += gain is not None
        return self

    def act(self, act, tile, finished, count):
        nc, at = self.pr.nc, self.base + tile
        act.wait_ge(finished, count)
        if at >= 2:
            act.wait_ge(self.summed, at - 1)
        nc.scalar.activation(self.sq[:, tile % 2, :], self.x[:, tile, :], ACT.Square).then_inc(self.sq_made, 1)
        if self.gain is not None:
            nc.scalar.activation(self.x_hi[:, tile, :], self.x[:, tile, :], ACT.Copy, scale=self.gain(tile)).then_inc(self.hi_made, 1)

    def dve(self, dve, tile):
        if self.gain is not None:
            dve.wait_ge(self.hi_made, self.split_base + tile + 1)
            self.pr.nc.vector.scalar_tensor_tensor(self.x_lo[:, tile, :], self.x[:, tile, :], self.gain(tile),
                                                   self.x_hi[:, tile, :].bitcast(F32), ALU.mult, ALU.subtract)\
                .then_inc(self.lo_made, 1)

    def pe(self, pe, tile):
        pe.wait_ge(self.sq_made, self.base + tile + 1)
        if tile == 0 and self.uses:
            pe.wait_ge(self.log_made, self.uses)
        self.pr.nc.tensor.matmul(self.pr.bank[7], self.pr.c["ones"], self.sq[:, tile % 2, :], start=(tile == 0),
                                 stop=(tile == KT - 1)).then_inc(self.summed, 1)

    def finish(self, act):
        nc = self.pr.nc
        act.wait_ge(self.summed, self.base + KT)
        nc.scalar.activation(self.rstd[:, 0, :], self.pr.bank[7], ACT.Ln, scale=1.0 / D, bias=self.pr.eps(0)).then_inc(self.log_made, 1)
        act.wait_ge(self.log_made, self.uses + 1)
        nc.scalar.activation(self.rstd[:, 1, :], self.rstd[:, 0, :], ACT.Exp, scale=-0.5).then_inc(self.rstd_made, 1)


def norm_block(pr, scratch, x, x_hi, x_lo, gain, width=T, bias=None, out=None, known=False, before=None):
    nc = pr.nc
    sq, rstd, y = scratch["sq"], scratch["rstd"], scratch["y"]
    sq_made, sum_done, log_made, rstd_made, y_made, hi_made, lo_made, x_made = pr.norm_sems
    q, q_sum, q_x = pr.norms, pr.norm_sums, pr.norm_befores
    split = pr.norms_split
    pr.norms += 1
    pr.norm_sums += not known
    pr.norm_befores += before is not None
    pr.norms_split += out is None
    total = pr.bank[7][:, 0:width]
    with nc.Block() as block:
        @block.sync
        def _(sp):
            pr.stream(sp, pr.taken + RAW_SLOTS)

        @block.tensor
        def _(pe):
            if not known:
                for k in range(KT):
                    pe.wait_ge(sq_made, KT * q_sum + k + 1)
                    last = nc.tensor.matmul(total, pr.c["ones"], sq[:, k, 0:width], start=(k == 0), stop=(k == KT - 1))
                last.then_inc(sum_done, 1)

        @block.scalar
        def _(act):
            if not known:
                for k in range(KT):
                    if before:
                        act.wait_ge(x_made, KT * q_x + k + 1)
                    nc.scalar.activation(sq[:, k, 0:width], x(k), ACT.Square).then_inc(sq_made, 1)
                act.wait_ge(sum_done, q_sum + 1)
                nc.scalar.activation(rstd[:, 0, 0:width], total, ACT.Ln, scale=1.0 / D, bias=pr.eps(0)).then_inc(log_made, 1)
                act.wait_ge(log_made, q_sum + 1)
                nc.scalar.activation(rstd[:, 1, 0:width], rstd[:, 0, 0:width], ACT.Exp, scale=-0.5).then_inc(rstd_made, 1)
            if out is None:
                for k in range(KT):
                    act.wait_ge(y_made, KT * q + k + 1)
                    nc.scalar.activation(x_hi[:, k, 0:width], y[:, k, 0:width], ACT.Identity,
                                         bias=bias(k) if bias else pr.eps(4)).then_inc(hi_made, 1)

        @block.vector
        def _(dve):
            if before:
                for k in range(KT):
                    nc.vector.scalar_tensor_tensor(x(k), x(k), before[0](k), before[1], ALU.mult, ALU.mult).then_inc(x_made, 1)
            if not known:
                dve.wait_ge(rstd_made, q_sum + 1)
            for k in range(KT + 1):
                if k < KT:
                    nc.vector.scalar_tensor_tensor(y[:, k, 0:width] if out is None else out(k), x(k), gain(k),
                                                   rstd[:, 1, 0:width], ALU.mult, ALU.mult).then_inc(y_made, 1)
                if k >= 1 and out is None:
                    dve.wait_ge(y_made, KT * q + k)
                    dve.wait_ge(hi_made, KT * split + k)
                    nc.vector.scalar_tensor_tensor(x_lo[:, k - 1, 0:width], y[:, k - 1, 0:width],
                                                   bias(k - 1) if bias else 0.0,
                                                   x_hi[:, k - 1, 0:width].bitcast(F32), ALU.add, ALU.subtract)\
                        .then_inc(lo_made, 1)


def split_parts(x_hi, x_lo, n):
    return [(x_hi[:, k, :], x_lo[:, k, :]) for k in range(n)]


def da_attention_block(pr, U, room, out_hi, out_lo):
    nc, c = pr.nc, pr.c
    with ExitStack() as ctx:
        t = lambda name, shape, dtype=F32: pr.tile("da_" + name, shape, dtype, ctx)
        table, turned, rot_sb = room[:, 4:6, :], room[:, 6:8, :], t("rot", [P, P])
        vN = room[:, 0:4, :]
        prob = room[:, 8:12, :].rearrange("p (a b) t -> p a b t", a=2)
        probT = t("probT", [P, 2, TB, T])
        oT = t("oT", [P, 4, T])
        small = t("small", [P, 2, 8])
        lam = t("lam", [P, 8])
        s = pr.stage_sems("da_", ("table_in", "rot_done", "sin_made", "cos_made", "roped", "v_done", "v_out", "score", "negmax",
              "exp", "inv", "scaled", "diff", "tr_done", "tr_out", "pv_done", "o_out", "lam_in", "lam_sum",
              "lam_exp", "lam_made", "sq", "sum", "log", "rstd", "y", "hi", "lo"))
        units = [(h, q) for h in range(DA_HEADS) for q in range(TB)]
        with nc.Block() as block:
            @block.sync
            def _(sp):
                sp.dma_start(table[:, :, :], pr.dram["rope_da"].rearrange("p (a t) -> p a t", a=2))\
                    .then_inc(s["table_in"], 16)
                sp.dma_start(rot_sb[:, :], pr.dram["rot_da"]).then_inc(s["table_in"], 16)
                pr.stream(sp, pr.taken + RAW_SLOTS)

            @block.tensor
            def _(pe):
                pe.wait_ge(s["table_in"], 32)
                for i in range(8):
                    if i >= 2:
                        pe.wait_ge(s["sin_made"], i - 1)
                    nc.tensor.matmul(pr.bank[i % 2], rot_sb[:, :], U[:, i, :], start=True, stop=True)\
                        .then_inc(s["rot_done"], 1)
                for b in range(TB):
                    if b >= 2:
                        pe.wait_ge(s["v_out"], b - 1)
                    for j in range(4):
                        last = nc.tensor.transpose(pr.bank[2 + b % 2][:, j * P:(j + 1) * P],
                                                   U[:, 8 + j, b * P:(b + 1) * P], c["ident"])
                    last.then_inc(s["v_done"], 1)
                pe.wait_ge(s["lam_in"], 2)
                nc.tensor.matmul(pr.bank[4][:, 0:2], c["ones"], lam[:, 0:2], start=True, stop=True)\
                    .then_inc(s["lam_sum"], 1)
                pe.wait_ge(s["roped"], 8)
                pe.wait_ge(s["v_out"], TB)
                pe.wait_ge(s["lam_exp"], 1)
                for i in range(len(units) + 2):
                    if i < len(units):
                        h, q = units[i]
                        if i >= 2:
                            pe.wait_ge(s["exp"], 2 * (i - 1))
                        for m in range(2):
                            last = nc.tensor.matmul(pr.bank[2 * (i % 2) + m],
                                                    U[64 * m:64 * m + 64, h, q * P:(q + 1) * P],
                                                    U[64 * m:64 * m + 64, 4 + h, :], start=True, stop=True)
                        last.then_inc(s["score"], 1)
                    if i >= 2:
                        j = i - 2
                        h, q = units[j]
                        pe.wait_ge(s["diff"], j + 1)
                        if j >= 2:
                            pe.wait_ge(s["tr_out"], j - 1)
                        for k in range(TB):
                            last = nc.tensor.transpose(pr.bank[4 + j % 2][:, k * P:(k + 1) * P],
                                                       prob[:, j % 2, 0, k * P:(k + 1) * P], c["ident"])
                        last.then_inc(s["tr_done"], 1)
                        if q == TB - 1:
                            pe.wait_ge(s["tr_out"], j + 1)
                            if h >= 2:
                                pe.wait_ge(s["o_out"], h - 1)
                            for k in range(TB):
                                last = nc.tensor.matmul(pr.bank[6 + h % 2], vN[:, k, h * P:(h + 1) * P],
                                                        probT[:, h % 2, k, :], start=(k == 0), stop=(k == TB - 1))
                            last.then_inc(s["pv_done"], 1)
                for h in range(DA_HEADS):
                    pe.wait_ge(s["sq"], h + 1)
                    nc.tensor.matmul(pr.bank[h], c["ones"], turned[:, h % 2, :], start=True, stop=True)\
                        .then_inc(s["sum"], 1)

            @block.scalar
            def _(act):
                for b in range(TB):
                    act.wait_ge(s["v_done"], b + 1)
                    nc.scalar.copy(vN[:, b, :], pr.bank[2 + b % 2]).then_inc(s["v_out"], 1)
                act.wait_ge(s["lam_sum"], 1)
                nc.scalar.activation(lam[:, 2:4], pr.bank[4][:, 0:2], ACT.Exp).then_inc(s["lam_exp"], 1)
                for i in range(len(units) + 2):
                    if i < len(units):
                        for m in range(2):
                            act.wait_ge(s["negmax"], 2 * i + m + 1)
                            if i >= 2:
                                act.wait_ge(s["tr_done"], i - 1)
                            nc.scalar.activation(prob[:, i % 2, m, :], pr.bank[2 * (i % 2) + m], ACT.Exp,
                                                 bias=small[:, i % 2, m:m + 1],
                                                 accum_out=small[:, i % 2, 2 + m:3 + m]).then_inc(s["exp"], 1)
                    if i >= 2:
                        j = i - 2
                        h, q = units[j]
                        act.wait_ge(s["tr_done"], j + 1)
                        if h >= 2:
                            act.wait_ge(s["pv_done"], h - 1)
                        nc.scalar.copy(probT[:, h % 2, :, q * P:(q + 1) * P],
                                       pr.bank[4 + j % 2].rearrange("p (k t) -> p k t", k=TB)).then_inc(s["tr_out"], 1)
                        if q == TB - 1:
                            act.wait_ge(s["pv_done"], h + 1)
                            nc.scalar.copy(oT[:, h, :], pr.bank[6 + h % 2]).then_inc(s["o_out"], 1)
                for h in range(DA_HEADS):
                    act.wait_ge(s["o_out"], h + 1)
                    if h >= 2:
                        act.wait_ge(s["y"], h - 1)
                    nc.scalar.activation(turned[:, h % 2, :], oT[:, h, :], ACT.Square).then_inc(s["sq"], 1)
                    act.wait_ge(s["sum"], h + 1)
                    nc.scalar.activation(prob[:, h % 2, 0, :], pr.bank[h], ACT.Ln, scale=1.0 / P, bias=pr.eps(2))\
                        .then_inc(s["log"], 1)
                    act.wait_ge(s["log"], h + 1)
                    nc.scalar.activation(prob[:, h % 2, 1, :], prob[:, h % 2, 0, :], ACT.Exp, scale=-0.5)\
                        .then_inc(s["rstd"], 1)
                    act.wait_ge(s["y"], h + 1)
                    nc.scalar.copy(out_hi[:, h, :], oT[:, h, :]).then_inc(s["hi"], 1)

            @block.vector
            def _(dve):
                dve.wait_ge(s["table_in"], 32)
                for i in range(8):
                    dve.wait_ge(s["rot_done"], i + 1)
                    if i >= 2:
                        dve.wait_ge(s["roped"], i - 1)
                    nc.vector.tensor_tensor(turned[:, i % 2, :], pr.bank[i % 2], table[:, 1, :], ALU.mult)\
                        .then_inc(s["sin_made"], 1)
                    nc.vector.tensor_tensor(U[:, i, :], U[:, i, :], table[:, 0, :], ALU.mult)\
                        .then_inc(s["cos_made"], 1)
                    dve.wait_ge(s["sin_made"], i + 1)
                    dve.wait_ge(s["cos_made"], i + 1)
                    nc.vector.tensor_tensor(U[:, i, :], U[:, i, :], turned[:, i % 2, :], ALU.add)\
                        .then_inc(s["roped"], 1)
                lp = pr.param("lam")
                for m in range(2):
                    nc.vector.tensor_tensor(lam[:, m:m + 1], lp(2 * m), lp(2 * m + 1), ALU.mult).then_inc(s["lam_in"], 1)
                dve.wait_ge(s["lam_exp"], 1)
                nc.vector.tensor_tensor(lam[:, 4:5], lam[:, 3:4], lam[:, 2:3], ALU.subtract).then_inc(s["lam_made"], 1)
                dve.wait_ge(s["lam_made"], 1)
                nc.vector.tensor_scalar_add(lam[:, 5:6], lam[:, 4:5], -LAMBDA_INIT).then_inc(s["lam_made"], 1)
                dve.wait_ge(s["lam_made"], 2)

                for i in range(len(units) + 1):
                    if i < len(units):
                        dve.wait_ge(s["score"], i + 1)
                        if i >= 2:
                            dve.wait_ge(s["diff"], i - 1)
                        for m in range(2):
                            nc.vector.tensor_reduce(small[:, i % 2, m:m + 1], pr.bank[2 * (i % 2) + m], AX_X,
                                                    ALU.max, negate=True).then_inc(s["negmax"], 1)
                    if i >= 1:
                        j = i - 1
                        w = small[:, j % 2, :]
                        dve.wait_ge(s["exp"], 2 * j + 2)
                        nc.vector.reciprocal(w[:, 4:6], w[:, 2:4]).then_inc(s["inv"], 1)
                        dve.wait_ge(s["inv"], 2 * j + 1)
                        nc.vector.tensor_tensor(w[:, 6:7], w[:, 5:6], lam[:, 5:6], ALU.mult).then_inc(s["inv"], 1)
                        nc.vector.tensor_scalar(prob[:, j % 2, 0, :], prob[:, j % 2, 0, :], w[:, 4:5], None, ALU.mult)\
                            .then_inc(s["scaled"], 1)
                        dve.wait_ge(s["inv"], 2 * j + 2)
                        dve.wait_ge(s["scaled"], j + 1)
                        nc.vector.scalar_tensor_tensor(prob[:, j % 2, 0, :], prob[:, j % 2, 1, :], w[:, 6:7],
                                                       prob[:, j % 2, 0, :], ALU.mult, ALU.add).then_inc(s["diff"], 1)
                for h in range(DA_HEADS):
                    dve.wait_ge(s["rstd"], h + 1)
                    nc.vector.scalar_tensor_tensor(oT[:, h, :], oT[:, h, :], pr.c["subln_scaled"],
                                                   prob[:, h % 2, 1, :], ALU.mult, ALU.mult).then_inc(s["y"], 1)
                    dve.wait_ge(s["hi"], h + 1)
                    nc.vector.tensor_tensor(out_lo[:, h, :], oT[:, h, :], out_hi[:, h, :].bitcast(F32), ALU.subtract)\
                        .then_inc(s["lo"], 1)
        pr.release(s)


def rwkv_block(pr, U, w_lora, room):
    nc, c = pr.nc, pr.c
    L_KINDS = ("L", "A1", "M", "A2")
    with ExitStack() as ctx:
        t = lambda name, shape: pr.tile("rw_" + name, shape, F32, ctx)
        keep, strict, incl, pair = (t(k, [P, 2, w]) for k, w in (("keep", T), ("strict", P), ("incl", P), ("pair", P)))
        level = t("level", [P, 10, 64])
        kkr, kk, ks, rinv = t("kkr", [P, T]), t("kk", [P, T]), t("ks", [P, T]), t("rinv", [P, T])
        v_tokens = t("vN", [P, 2, TB, P])
        dirs = []
        for d in range(2):
            td = lambda name, shape: t(f"{name}{d}", shape)
            scr, kb, kh, rt = td("scr", [P, 5 * T]), td("kb", [P, 2, 2, T]), td("kh", [P, 2, T]), td("rt", [P, 2, T])
            pin = td("pin", [P, 2, NCH, CH + 1])
            mats = {k: td("m" + k, [P, 8, P]) for k in L_KINDS}
            fixed = dict(
                cum=room[:, 4 * d, :], sg=room[:, 4 * d + 1, :], aa=room[:, 4 * d + 2, :], pinv=room[:, 4 * d + 3, :],
                X=scr[:, 0:1024].rearrange("p (q t) -> p q t", q=8), Y=scr[:, 1024:2048].rearrange("p (q t) -> p q t", q=8),
                M1=scr[:, 2048:2560].rearrange("p (q t) -> p q t", q=8),
                KtN=td("ktn", [P, TB, P]), BhN=td("bhn", [P, TB, P]), KhN=td("khn", [P, TB, P]),
                mats=mats, Phi=mats["L"], Z=mats["M"])
            dirs.append([dict(fixed, pin=pin[:, j], Kt=kb[:, j, 0, :], Bh=kb[:, j, 1, :], Kh=kh[:, j, :], Rb=kh[:, j, :],
                              Rt=rt[:, j, :], N=kb[:, j, :, :].rearrange("p a (q t) -> p (a q) t", t=P)) for j in range(2)])
        both = lambda p: [(d, dirs[d][p % 2]) for d in range(2)]
        STEPS = 18
        Y_BANKS = (6, 7, 0, 1)
        TR_BANKS = (0, 1, 6, 7, 0, 1)
        GRAMS = [("L", "Bh", "Kt"), ("M", "Kh", "Kt"), ("A1", "Bh", "Rt"), ("A2", "Kh", "Rt")]
        names = ("const", "kkr", "kksq", "kksum", "kkmax", "kklog", "rinv", "kk", "lora", "sig", "ones", "prep", "cum", "bk", "exps",
                 "vtr", "vout", "tr", "trout", "gram", "mask", "ybegin", "y0", "xtr", "xout", "m1", "m1out", "px", "xsub",
                 "ytr", "yout", "mv", "mvout", "n", "nout", "phizero", "zzero", "phi", "phiout", "psi", "psiout",
                 "rb", "rbout", "step", "zout", "y", "yo", "ksum", "bonus", "bsum", "bout", "scaled")
        s = pr.stage_sems("rw_", names)

        def ex(a, d):
            return a["pin"][:, :, d:d + CH]

        def inc(a, d):
            return a["pin"][:, :, 1 - d:1 - d + CH]

        def chunks(x):
            return x.rearrange("p (n t) -> p n t", n=NCH)

        def half_cols(x, lev, d):
            return x.rearrange("p q (n two w) -> p q n two w", two=2, w=2 ** lev)[:, :, :, d, :]

        ORDER = [list(range(NCH)), list(range(NCH))[::-1]]
        heads = [(hh, b) for hh in range(2) for b in range(TB)]

        with nc.Block() as block:
            @block.sync
            def _(sp):
                for dst, key in ((keep, "keep"), (strict, "strict"), (incl, "incl"), (pair, "pair")):
                    sp.dma_start(dst[:, :, :], pr.dram[key].rearrange("p (a t) -> p a t", a=2)).then_inc(s["const"], 16)
                sp.dma_start(level[:, :, :], pr.dram["level"].rearrange("p (a t) -> p a t", a=10)).then_inc(s["const"], 16)
                pr.stream(sp, pr.taken + RAW_SLOTS)

            @block.gpsimd
            def _(pool):
                for p in range(RT):
                    for d, a in both(p):
                        pool.wait_ge(s["mv"], 2 * p + d + 1)
                        for hh in range(2):
                            nc.gpsimd.memset(a["Phi"][64 * hh:64 * hh + 64, :, 64 - 64 * hh:128 - 64 * hh], 0.0)\
                                .then_inc(s["phizero"], 1)
                            nc.gpsimd.memset(a["Z"][64 * hh:64 * hh + 64, :, 64 - 64 * hh:128 - 64 * hh], 0.0)\
                                .then_inc(s["zzero"], 1)
                            nc.gpsimd.memset(a["Z"][64 * hh:64 * hh + 64, ORDER[d][0], 64 * hh:64 * hh + 64], 0.0)\
                                .then_inc(s["zzero"], 1)

            @block.tensor
            def _(pe):
                def gram(p, n):
                    d, (key, left, right) = n % 2, GRAMS[n // 2]
                    a = dirs[d][p % 2]
                    out = pr.pair[2 - d] if key == "L" else pr.pair[1]
                    for hh, b in heads:
                        rows, cols, q = slice(64 * hh, 64 * hh + 64), slice(b * P, (b + 1) * P), hh * TB + b
                        last = nc.tensor.matmul(out[:, q * P:(q + 1) * P], a[left][rows, cols], a[right][rows, cols],
                                                start=True, stop=True)
                    last.then_inc(s["gram"], 1)

                def prepare(p, n):
                    if n == 0:
                        nc.tensor.matmul(pr.bank[3], w_lora[0:64, 0, p * P:(p + 1) * P], U[0:64, 12, :],
                                         start=True, stop=True).then_inc(s["lora"], 1)
                    elif n == 1:
                        pe.wait_ge(s["kksq"], p + 1)
                        nc.tensor.matmul(pr.bank[2], c["head_ones"], kk[:, :], start=True, stop=True).then_inc(s["kksum"], 1)
                    elif n == 2:
                        pe.wait_ge(s["sig"], 4 * p + 1)
                        nc.tensor.matmul(pr.bank[3], w_lora[0:64, 1, p * P:(p + 1) * P], U[0:64, 13, :],
                                         start=True, stop=True).then_inc(s["lora"], 1)
                    elif n == 3:
                        pe.wait_ge(s["kkmax"], p + 1)
                        nc.tensor.matmul(pr.bank[2], w_lora[64:128, 0, p * P:(p + 1) * P], U[64:128, 12, :],
                                         start=True, stop=True).then_inc(s["lora"], 1)
                    elif n == 4:
                        pe.wait_ge(s["sig"], 4 * p + 2)
                        nc.tensor.matmul(pr.bank[3], w_lora[64:128, 1, p * P:(p + 1) * P], U[64:128, 13, :],
                                         start=True, stop=True).then_inc(s["lora"], 1)
                    elif n == 5:
                        pe.wait_ge(s["sig"], 4 * p + 3)
                        for b in range(TB):
                            last = nc.tensor.transpose(pr.bank[2][:, b * P:(b + 1) * P], U[:, 8 + p, b * P:(b + 1) * P], c["ident"])
                        last.then_inc(s["vtr"], 1)
                    elif n == 16:
                        pe.wait_ge(s["vout"], p + 1)
                        pe.wait_ge(s["bonus"], p + 1)
                        nc.tensor.matmul(pr.bank[2], c["head_ones"], ks[:, :], start=True, stop=True).then_inc(s["bsum"], 1)

                def beside(p, n):
                    if 6 <= n < 12:
                        if n == 6 and p + 1 < RT:
                            pe.wait_ge(s["vout"], p + 2)
                            pe.wait_ge(s["sig"], 4 * p + 8)
                        elif n > 6:
                            pe.wait_ge(s["mask"], 8 * p + n - 4)
                        gram(p, n - 4)
                    elif p + 1 < RT:
                        prepare(p + 1, n)

                for n in range(STEPS):
                    prepare(0, n)
                for p in range(RT):
                    if p:
                        pe.wait_ge(s["zout"], 14 * p)
                    pe.wait_ge(s["scaled"], 8 * (p + 1))
                    gram(p, 0)
                    pe.wait_ge(s["bout"], p + 1)
                    gram(p, 1)
                    if p:
                        pe.wait_ge(s["yo"], 2 * p)
                    for d, a in both(p):
                        for j, key in enumerate(("Kt", "Bh", "Kh")):
                            i = 3 * d + j
                            if i >= 4:
                                pe.wait_ge(s["trout"], 6 * p + i - 3)
                            for b in range(TB):
                                last = nc.tensor.transpose(pr.bank[TR_BANKS[i]][:, b * P:(b + 1) * P],
                                                           a[key][:, b * P:(b + 1) * P], c["ident"])
                            last.then_inc(s["tr"], 1)
                    pe.wait_ge(s["trout"], 6 * (p + 1))
                    for d, a in both(p):
                        pe.wait_ge(s["y0"], 2 * p + d + 1)
                        for q in range(8):
                            last = nc.tensor.transpose(pr.pair[2 + d][:, q * P:(q + 1) * P], a["Y"][:, q, :], c["ident"])
                        last.then_inc(s["xtr"], 1)
                    pe.wait_ge(s["xout"], 2 * p + 2)
                    pe.wait_ge(s["mask"], 8 * p + 2)
                    for lev in range(1, 6):
                        u = 5 * p + lev - 1
                        for d, a in both(p):
                            for q in range(8):
                                last = nc.tensor.matmul(pr.bank[d][:, q * 64:(q + 1) * 64], a["mats"]["L"][:, q, :],
                                                        half_cols(a["X"], lev, d)[:, q], start=True, stop=True)
                            last.then_inc(s["m1"], 1)
                        beside(p, 3 * lev - 3)
                        for d, a in both(p):
                            pe.wait_ge(s["m1out"], 2 * u + d + 1)
                            if lev > 1:
                                pe.wait_ge(s["yout"], 2 * (u - 1) + d + 1)
                            for q in range(8):
                                last = nc.tensor.matmul(pr.bank[d][:, q * 64:(q + 1) * 64], a["Y"][:, q, :],
                                                        a["M1"][:, q, :], start=True, stop=True)
                            last.then_inc(s["px"], 1)
                        beside(p, 3 * lev - 2)
                        for d, a in both(p):
                            pe.wait_ge(s["xsub"], 2 * u + d + 1)
                            for q in range(8):
                                last = nc.tensor.transpose(pr.pair[2 + d][:, q * P:(q + 1) * P], a["X"][:, q, :], c["ident"])
                            last.then_inc(s["ytr"], 1)
                        beside(p, 3 * lev - 1)
                    vN = v_tokens[:, p % 2]
                    pe.wait_ge(s["mask"], 8 * (p + 1))
                    for d, a in both(p):
                        for hh, b in heads:
                            q = hh * TB + b
                            last = nc.tensor.matmul(pr.bank[d][:, q * 64:(q + 1) * 64], a["mats"]["M"][:, q, :],
                                                    vN[:, b, 64 * hh:64 * hh + 64], start=True, stop=True)
                        last.then_inc(s["mv"], 1)
                    for d, a in both(p):
                        pe.wait_ge(s["mvout"], 2 * p + d + 1)
                        pe.wait_ge(s["yout"], 2 * (5 * p + 4) + d + 1)
                        for hh, b in heads:
                            q = hh * TB + b
                            out = pr.pair[1 + d][:, q * P:(q + 1) * P]
                            nc.tensor.matmul(out[:, 0:64], a["Y"][:, q, :], a["M1"][:, q, :], start=True, stop=True)
                            last = nc.tensor.matmul(out[:, 64:128], a["Y"][:, q, :], a["KtN"][:, b, 64 * hh:64 * hh + 64],
                                                    start=True, stop=True)
                        last.then_inc(s["n"], 1)
                    for d, a in both(p):
                        pe.wait_ge(s["nout"], 2 * p + d + 1)
                        if d == 1:
                            pe.wait_ge(s["phiout"], 2 * (2 * p) + 2)
                        for cc in range(2):
                            r = slice(64 * cc, 64 * cc + 64)
                            for hh, b in heads:
                                last = nc.tensor.matmul(pr.pair[0][64 * hh:64 * hh + 64, 512 * cc + 64 * b:512 * cc + 64 * b + 64],
                                                        a["N"][r, hh * TB + b, 64:128], a["BhN"][r, b, 64 * hh:64 * hh + 64],
                                                        start=True, stop=True)
                        last.then_inc(s["phi"], 1)
                        if d == 1:
                            pe.wait_ge(s["psiout"], 4 * (2 * p) + 4)
                        for cc in range(2):
                            r = slice(64 * cc, 64 * cc + 64)
                            for hh, b in heads:
                                h = slice(64 * hh, 64 * hh + 64)
                                out = pr.pair[3][h, 512 * cc + 64 * b:512 * cc + 64 * b + 64]
                                nc.tensor.matmul(out, a["KhN"][r, b, h], vN[r, b, h], start=True, stop=False)
                                last = nc.tensor.matmul(out, a["BhN"][r, b, h], a["N"][r, hh * TB + b, 0:64],
                                                        start=False, stop=True)
                        last.then_inc(s["psi"], 1)
                        for hh, b in heads:
                            last = nc.tensor.matmul(pr.bank[2 + d][64 * hh:64 * hh + 64, b * P:(b + 1) * P],
                                                    a["N"][:, hh * TB + b, 64:128], a["mats"]["A1"][:, hh * TB + b, :],
                                                    start=True, stop=True)
                        last.then_inc(s["rb"], 1)
                    pe.wait_ge(s["phiout"], 4 * (p + 1))
                    pe.wait_ge(s["psiout"], 8 * (p + 1))
                    fixed_parts = [(b, hh, d, a, k) for b in range(TB) for hh in range(2) for d, a in both(p) for k in range(2)]
                    for i in range(NCH - 1):
                        for d, a in both(p):
                            at = ORDER[d][i]
                            if i == 0:
                                pe.wait_ge(s["phizero"], 2 * (2 * p + d + 1))
                                pe.wait_ge(s["zzero"], 4 * (2 * p + d + 1))
                            else:
                                pe.wait_ge(s["zout"], 14 * p + 2 * (i - 1) + d + 1)
                            out = pr.bank[4 + d][:, (i % 4) * P:(i % 4 + 1) * P]
                            nc.tensor.matmul(out, a["Phi"][:, 4 * (at % 2) + at // 2, :], a["Z"][:, at, :],
                                             start=True, stop=True).then_inc(s["step"], 1)
                        for b, hh, d, a, k in fixed_parts[5 * i:5 * (i + 1)]:
                            q, h = hh * TB + b, slice(64 * hh, 64 * hh + 64)
                            left, right = ((vN[:, b, h], a["mats"]["A2"]), (a["N"][:, q, 0:64], a["mats"]["A1"]))[k]
                            nc.tensor.matmul(pr.bank[Y_BANKS[b]][h, 0:P], left, right[:, q, :],
                                             start=(d == 0 and k == 0), stop=False, skip_group_check=True)
                    pe.wait_ge(s["rbout"], 2 * p + 2)
                    if p + 1 < RT:
                        prepare(p + 1, 16)
                    pe.wait_ge(s["zout"], 14 * p + 14)
                    for b in range(TB):
                        for d, a in both(p):
                            for cc in range(2):
                                last = nc.tensor.matmul(pr.bank[Y_BANKS[b]][:, 64 * cc:64 * cc + 64], a["Z"][:, 2 * b + cc, :],
                                                        a["Rb"][:, (2 * b + cc) * CH:(2 * b + cc + 1) * CH],
                                                        start=False, stop=(d == 1), skip_group_check=True)
                    last.then_inc(s["y"], 1)

            @block.scalar
            def _(act):
                def sigmoid(p, n):
                    d, m = divmod(n, 2)
                    key, prm = (("sg", "w0"), ("aa", "a0"))[m]
                    act.wait_ge(s["lora"], 4 * p + n + 1)
                    if p:
                        act.wait_ge(s["scaled"], 8 * p)
                        act.wait_ge(s["ksum"], p)
                    nc.scalar.activation(dirs[d][0][key], pr.bank[2 if n == 2 else 3], ACT.Sigmoid, bias=pr.param(prm)(4 * d + p))\
                        .then_inc(s["sig"], 1)

                def prepare(p, n):
                    if n == 0:
                        act.wait_ge(s["kkr"], p + 1)
                        if p:
                            act.wait_ge(s["scaled"], 8 * p)
                        nc.scalar.activation(kk[:, :], kkr[:, :], ACT.Square).then_inc(s["kksq"], 1)
                        sigmoid(p, 0)
                    elif n in (2, 3, 4):
                        sigmoid(p, n - 1)
                    elif n == 5:
                        act.wait_ge(s["vtr"], p + 1)
                        if p >= 2:
                            act.wait_ge(s["y"], p - 1)
                        nc.scalar.copy(v_tokens[:, p % 2], pr.bank[2].rearrange("p (b t) -> p b t", b=TB)).then_inc(s["vout"], 1)
                    elif n == 6:
                        act.wait_ge(s["kkmax"], p + 1)
                        nc.scalar.activation(rinv[:, :], rinv[:, :], ACT.Ln, scale=2.0 ** 20).then_inc(s["kklog"], 1)
                    elif n == 9:
                        act.wait_ge(s["kklog"], p + 1)
                        nc.scalar.activation(rinv[:, :], rinv[:, :], ACT.Exp, scale=-0.5, bias=pr.eps(3)).then_inc(s["rinv"], 1)
                    elif n in (10, 12):
                        d, a = both(p)[n // 12]
                        act.wait_ge(s["cum"], 2 * p + d + 1)
                        if p >= 2:
                            act.wait_ge(s["zout"], 14 * (p - 1))
                            act.wait_ge(s["psiout"], 8 * (p - 1))
                        if p:
                            act.wait_ge(s["scaled"], 8 * p)
                        nc.scalar.activation(inc(a, d), chunks(a["cum"]), ACT.Exp, scale=-DECAY_RATE).then_inc(s["exps"], 1)
                        nc.scalar.activation(a["pinv"], a["cum"], ACT.Exp, scale=DECAY_RATE).then_inc(s["exps"], 1)

                for n in range(STEPS):
                    prepare(0, n)
                for p in range(RT):
                    if p:
                        act.wait_ge(s["y"], p)
                    for d, a in both(p):
                        for j, key in enumerate(("KtN", "BhN", "KhN")):
                            act.wait_ge(s["tr"], 6 * p + 3 * d + j + 1)
                            nc.scalar.copy(a[key][:, :, :], pr.bank[TR_BANKS[3 * d + j]].rearrange("p (b t) -> p b t", b=TB))\
                                .then_inc(s["trout"], 1)
                    for d, a in both(p):
                        act.wait_ge(s["xtr"], 2 * p + d + 1)
                        nc.scalar.copy(a["X"], pr.pair[2 + d][:, :].rearrange("p (q t) -> p q t", q=8)).then_inc(s["xout"], 1)
                    for lev in range(1, 6):
                        u = 5 * p + lev - 1
                        for n in range(3 * lev - 3, 3 * lev):
                            if n % 3 == 2:
                                for d, a in both(p):
                                    act.wait_ge(s["ytr"], 2 * u + d + 1)
                                    nc.scalar.copy(a["Y"], pr.pair[2 + d][:, :].rearrange("p (q t) -> p q t", q=8))\
                                        .then_inc(s["yout"], 1)
                            if p + 1 < RT:
                                prepare(p + 1, n)
                    for d, a in both(p):
                        act.wait_ge(s["mv"], 2 * p + d + 1)
                        nc.scalar.copy(a["M1"], pr.bank[d].rearrange("p (q t) -> p q t", q=8)).then_inc(s["mvout"], 1)
                    for d, a in both(p):
                        act.wait_ge(s["n"], 2 * p + d + 1)
                        act.wait_ge(s["gram"], 8 * (p + 1))
                        nc.scalar.mul(a["N"], pr.pair[1 + d][:, :].rearrange("p (q t) -> p q t", q=8), -1.0).then_inc(s["nout"], 1)
                    act.wait_ge(s["y"], p + 1)
                    for j in range(2):
                        nc.scalar.copy(U[:, p, 256 * j:256 * j + 256].rearrange("p (b t) -> p b t", b=2),
                                       pr.pair[3 - 3 * j][:, :].rearrange("p (b t) -> p b t", b=2)[:, :, 0:P]).then_inc(s["yo"], 1)

            @block.vector
            def _(dve):
                def back(d):
                    return slice(None, None, -1) if d else slice(None)

                def prepare(p, n):
                    r, k, v = (U[:, 4 * j + p, :] for j in range(3))
                    (_, a0), (_, a1) = both(p)
                    if n == 0:
                        if p:
                            dve.wait_ge(s["kk"], p)
                            dve.wait_ge(s["kksq"], p)
                        nc.vector.tensor_scalar(kkr[:, :], k, pr.param("k_k")(p), None, ALU.mult).then_inc(s["kkr"], 1)
                    elif n == 2:
                        dve.wait_ge(s["kksum"], p + 1)
                        nc.vector.tensor_scalar(rinv[:, :], pr.bank[2], 1e-24, None, ALU.max).then_inc(s["kkmax"], 1)
                    elif n in (3, 5):
                        d = (n - 3) // 2
                        a = (a0, a1)[d]
                        dve.wait_ge(s["sig"], 4 * p + 2 * d + 1)
                        if p:
                            dve.wait_ge(s["exps"], 4 * p)
                        nc.vector.tensor_tensor_scan(a["cum"][:, back(d)], keep[:, d, back(d)], a["sg"][:, back(d)], 0.0,
                                                     ALU.mult, ALU.add).then_inc(s["cum"], 1)
                    elif n in (4, 12):
                        d = n // 12
                        a = (a0, a1)[d]
                        dve.wait_ge(s["cum"], 2 * p + d + 1)
                        dve.wait_ge(s["sig"], 4 * p + 2 * d + 2)
                        nc.vector.tensor_scalar(a["sg"], a["aa"], pr.param("k_a")(p), pr.c["one_minus_ka"][:, p:p + 1],
                                                ALU.mult, ALU.add).then_inc(s["prep"], 1)
                        dve.wait_ge(s["prep"], 4 * p + 2 * d + 1)
                        nc.vector.tensor_tensor(a["sg"], a["sg"], k, ALU.mult).then_inc(s["prep"], 1)
                    elif n == 13:
                        dve.wait_ge(s["rinv"], p + 1)
                        nc.vector.tensor_tensor(kk[:, :], kkr[:, :], rinv[:, :], ALU.mult).then_inc(s["kk"], 1)
                        dve.wait_ge(s["kk"], p + 1)
                        dve.wait_ge(s["prep"], 4 * p + 4)
                        for d, a in both(p):
                            nc.vector.tensor_tensor(a["aa"], kk[:, :], a["aa"], ALU.mult).then_inc(s["bk"], 1)
                    elif n == 15:
                        for d, a in both(p):
                            dve.wait_ge(s["exps"], 4 * p + 2 * d + 2)
                            dve.wait_ge(s["bk"], 2 * p + d + 1)
                            nc.vector.tensor_tensor(chunks(a["Rt"]), chunks(r), inc(a, d), ALU.mult).then_inc(s["scaled"], 1)
                            nc.vector.tensor_tensor(chunks(a["Kt"]), chunks(kk[:, :]), ex(a, d), ALU.mult).then_inc(s["scaled"], 1)
                            nc.vector.tensor_tensor(a["Kh"], a["sg"], a["pinv"], ALU.mult).then_inc(s["scaled"], 1)
                            nc.vector.tensor_tensor(a["Bh"], a["aa"], a["pinv"], ALU.mult).then_inc(s["scaled"], 1)
                        if p:
                            dve.wait_ge(s["bsum"], p)
                        nc.vector.tensor_tensor(ks[:, :], a0["sg"], a1["sg"], ALU.add).then_inc(s["ksum"], 1)
                        dve.wait_ge(s["ksum"], p + 1)
                        nc.vector.scalar_tensor_tensor(ks[:, :], ks[:, :], pr.param("r_k")(p), r, ALU.mult, ALU.mult)\
                            .then_inc(s["bonus"], 1)
                    elif n == 17:
                        dve.wait_ge(s["bsum"], p + 1)
                        dve.wait_ge(s["kkr"], p + 1)
                        nc.vector.tensor_tensor(k, pr.bank[2], v, ALU.mult).then_inc(s["bout"], 1)

                def mask(p, n):
                    d, key = n % 2, GRAMS[n // 2][0]
                    out = pr.pair[2 - d] if key == "L" else pr.pair[1]
                    which = strict if key in ("L", "M") else incl
                    dve.wait_ge(s["gram"], 8 * p + n + 1)
                    nc.vector.tensor_tensor(dirs[d][0]["mats"][key][:, :, :], out[:, :].rearrange("p (q t) -> p q t", q=8),
                                            which[:, d:d + 1, :].to_broadcast([P, 8, P]), ALU.mult).then_inc(s["mask"], 1)

                def beside(p, n):
                    if 6 <= n < 12:
                        mask(p, n - 4)
                    if p + 1 < RT:
                        prepare(p + 1, n)

                dve.wait_ge(s["const"], 80)
                for d in range(2):
                    for j in range(2):
                        nc.vector.memset(dirs[d][j]["pin"][:, :, (CH if d else 0):(CH if d else 0) + 1], 1.0).then_inc(s["ones"], 1)
                dve.wait_ge(s["ones"], 4)
                for n in range(STEPS):
                    prepare(0, n)
                for p in range(RT):
                    if p:
                        dve.wait_ge(s["y"], p)
                    for d, a in both(p):
                        mask(p, d)
                        dve.wait_ge(s["mask"], 8 * p + d + 1)
                        nc.vector.tensor_tensor(a["Y"], a["mats"]["L"][:, :, :], pair[:, d:d + 1, :].to_broadcast([P, 8, P]),
                                                ALU.mult).then_inc(s["ybegin"], 1)
                        dve.wait_ge(s["ybegin"], 2 * p + d + 1)
                        nc.vector.tensor_tensor(a["Y"], c["ident"].unsqueeze(1).to_broadcast([P, 8, P]), a["Y"],
                                                ALU.subtract).then_inc(s["y0"], 1)
                    for lev in range(1, 6):
                        u = 5 * p + lev - 1
                        for d, a in both(p):
                            dve.wait_ge(s["m1"], 2 * u + d + 1)
                            nc.vector.tensor_tensor(a["M1"], pr.bank[d].rearrange("p (q t) -> p q t", q=8),
                                                    level[:, 5 * d + lev - 1:5 * d + lev, :].to_broadcast([P, 8, 64]), ALU.mult)\
                                .then_inc(s["m1out"], 1)
                        beside(p, 3 * lev - 3)
                        for d, a in both(p):
                            dve.wait_ge(s["px"], 2 * u + d + 1)
                            w = 2 ** lev
                            x = half_cols(a["X"], lev, d)
                            nc.vector.tensor_tensor(x, x, pr.bank[d].rearrange("p (q n w) -> p q n w", q=8, w=w),
                                                    ALU.subtract).then_inc(s["xsub"], 1)
                        beside(p, 3 * lev - 2)
                        beside(p, 3 * lev - 1)
                    if p + 1 < RT:
                        prepare(p + 1, 15)
                    for d, a in both(p):
                        dve.wait_ge(s["phi"], 2 * p + d + 1)
                        for hh in range(2):
                            h = slice(64 * hh, 64 * hh + 64)
                            nc.vector.tensor_tensor(a["Phi"][h, :, h].rearrange("p (a b) t -> p a b t", a=2),
                                                    pr.pair[0][h, :].rearrange("p (a x) -> p a x", a=2)[:, :, 0:256]
                                                    .rearrange("p a (b t) -> p a b t", b=4),
                                                    c["ident64"][h, :].unsqueeze(1).unsqueeze(1).to_broadcast([64, 2, 4, 64]),
                                                    ALU.add).then_inc(s["phiout"], 1)
                        dve.wait_ge(s["psi"], 2 * p + d + 1)
                        dve.wait_ge(s["zzero"], 4 * (2 * p + d + 1))
                        for hh in range(2):
                            h = slice(64 * hh, 64 * hh + 64)
                            psi = pr.pair[3][h, :].rearrange("p (cc x) -> p cc x", cc=2)[:, :, 0:256]\
                                .rearrange("p cc (b t) -> p b cc t", b=4)
                            for cc in range(2):
                                lo_b, hi_b = (0, 4 if cc == 0 else 3) if d == 0 else (0 if cc == 1 else 1, 4)
                                step = 1 if d == 0 else -1
                                slots = a["Z"][h, 2 * lo_b + cc + step:2 * (hi_b - 1) + cc + step + 1:2, h]
                                ends = a["pin"][h, 2 * lo_b + cc:2 * (hi_b - 1) + cc + 1:2, CH * (1 - d):CH * (1 - d) + 1]
                                last = nc.vector.tensor_tensor(slots, psi[:, lo_b:hi_b, cc, :],
                                                               ends.to_broadcast([64, hi_b - lo_b, 64]), ALU.mult)
                                last.then_inc(s["psiout"], 1)
                    for d, a in both(p):
                        dve.wait_ge(s["rb"], 2 * p + d + 1)
                        dve.wait_ge(s["gram"], 8 * (p + 1))
                        nc.vector.tensor_tensor(a["Rb"], a["Rt"], pr.bank[2 + d], ALU.add).then_inc(s["rbout"], 1)
                    for i in range(NCH - 1):
                        for d, a in both(p):
                            at, nxt = ORDER[d][i], ORDER[d][i + 1]
                            dve.wait_ge(s["step"], 14 * p + 2 * i + d + 1)
                            if i == 0:
                                dve.wait_ge(s["psiout"], 4 * (2 * p + d + 1))
                            nc.vector.scalar_tensor_tensor(a["Z"][:, nxt, :], pr.bank[4 + d][:, (i % 4) * P:(i % 4 + 1) * P],
                                                           a["pin"][:, at, CH * (1 - d):CH * (1 - d) + 1], a["Z"][:, nxt, :],
                                                           ALU.mult, ALU.add).then_inc(s["zout"], 1)
                    if p + 1 < RT:
                        prepare(p + 1, 17)
        pr.release(s)




def rwkv_out_block(pr, U, g2, y_hi, y_lo):
    nc, c = pr.nc, pr.c
    with ExitStack() as ctx:
        sq, rstd, gate = (pr.tile("ro_" + k, [P, 2, T], F32, ctx) for k in ("sq", "rstd", "gate"))
        sg = pr.tile("ro_sg", [P, T], F32, ctx)
        s = pr.stage_sems("ro_", ("sg", "mean", "centred", "sq", "var", "log", "rstd", "g", "gate", "y", "hi", "lo"))
        with nc.Block() as block:
            @block.sync
            def _(sp):
                pr.stream(sp, pr.taken + RAW_SLOTS)

            @block.tensor
            def _(pe):
                for p in range(RT + 1):
                    if p < RT:
                        if p >= 2:
                            pe.wait_ge(s["centred"], p - 1)
                        nc.tensor.matmul(pr.bank[p % 2], c["head_mean"], U[:, p, :], start=True, stop=True)\
                            .then_inc(s["mean"], 1)
                        if p == 0:
                            pe.wait_ge(s["sg"], 1)
                        if p >= 2:
                            pe.wait_ge(s["gate"], p - 1)
                        nc.tensor.matmul(pr.bank[4 + p % 2], g2[:, p * P:(p + 1) * P], sg[:, :], start=True, stop=True)\
                            .then_inc(s["g"], 1)
                    if p >= 1:
                        pe.wait_ge(s["sq"], p)
                        if p >= 3:
                            pe.wait_ge(s["log"], p - 2)
                        nc.tensor.matmul(pr.bank[2 + (p - 1) % 2], c["head_mean"], sq[:, (p - 1) % 2, :], start=True, stop=True)\
                            .then_inc(s["var"], 1)

            @block.scalar
            def _(act):
                nc.scalar.activation(sg[:, :], U[:, 14, :], ACT.Sigmoid).then_inc(s["sg"], 1)
                for p in range(RT):
                    act.wait_ge(s["centred"], p + 1)
                    if p >= 2:
                        act.wait_ge(s["var"], p - 1)
                    nc.scalar.activation(sq[:, p % 2, :], U[:, p, :], ACT.Square).then_inc(s["sq"], 1)
                    act.wait_ge(s["g"], p + 1)
                    if p >= 2:
                        act.wait_ge(s["y"], 3 * (p - 1))
                    nc.scalar.copy(gate[:, p % 2, :], pr.bank[4 + p % 2]).then_inc(s["gate"], 1)
                    act.wait_ge(s["var"], p + 1)
                    nc.scalar.activation(rstd[:, p % 2, :], pr.bank[2 + p % 2], ACT.Ln, bias=pr.eps(1)).then_inc(s["log"], 1)
                    act.wait_ge(s["log"], p + 1)
                    nc.scalar.activation(rstd[:, p % 2, :], rstd[:, p % 2, :], ACT.Exp, scale=-0.5).then_inc(s["rstd"], 1)
                    act.wait_ge(s["y"], 3 * (p + 1))
                    nc.scalar.copy(y_hi[:, p, :], U[:, p, :]).then_inc(s["hi"], 1)

            @block.vector
            def _(dve):
                for p in range(RT):
                    y = U[:, p, :]
                    dve.wait_ge(s["mean"], p + 1)
                    nc.vector.tensor_tensor(y, y, pr.bank[p % 2], ALU.subtract).then_inc(s["centred"], 1)
                    dve.wait_ge(s["rstd"], p + 1)
                    nc.vector.scalar_tensor_tensor(y, y, pr.param("ln_w")(p), rstd[:, p % 2, :], ALU.mult, ALU.mult)\
                        .then_inc(s["y"], 1)
                    dve.wait_ge(s["y"], 3 * p + 1)
                    nc.vector.scalar_tensor_tensor(y, U[:, 4 + p, :], pr.param("ln_b")(p), y, ALU.add, ALU.add)\
                        .then_inc(s["y"], 1)
                    dve.wait_ge(s["y"], 3 * p + 2)
                    nc.vector.tensor_tensor(y, y, gate[:, p % 2, :], ALU.mult).then_inc(s["y"], 1)
                    dve.wait_ge(s["hi"], p + 1)
                    nc.vector.tensor_tensor(y_lo[:, p, :], y, y_hi[:, p, :].bitcast(F32), ALU.subtract).then_inc(s["lo"], 1)
        pr.release(s)


class Modulation:

    def __init__(self, pr, ctx, cc, spread):
        self.pr, self.cc, self.spread = pr, cc, spread
        self.w = pr.tile("mod_w", [P, MOD_SLOTS, D], F32, ctx)
        self.acc = pr.tile("mod_acc", [P, 2, 2, D], F32, ctx)
        self.landed = [pr.sem(f"mod_landed{i}") for i in range(MOD_SLOTS)]
        self.added, self.reduced, self.made = pr.sem("mod_added"), pr.sem("mod_reduced"), pr.sem("mod_made")

    def load(self, pool):
        for i in range(MOD_PARTS * KT):
            if i >= MOD_SLOTS:
                pool.wait_ge(self.added, 2 * (i - MOD_SLOTS + 1))
            pool.dma_start(self.w[:, i % MOD_SLOTS, :], self.pr.dram["w_mod"][i]).then_inc(self.landed[i % MOD_SLOTS], 16)

    def add(self, dve, n):
        total = 2 * MOD_PARTS * KT
        for j in range(min(total, total * n // self.spread), min(total, total * (n + 1) // self.spread)):
            i, column = divmod(j, 2)
            part, k = divmod(i, KT)
            acc, w, c = self.acc[:, part % 2, column, :], self.w[:, i % MOD_SLOTS, :], self.cc[:, column, k:k + 1]
            dve.wait_ge(self.landed[i % MOD_SLOTS], 16 * (i // MOD_SLOTS + 1))
            if k == 0:
                if part >= 2:
                    dve.wait_ge(self.reduced, part - 1)
                self.pr.nc.vector.tensor_scalar(acc, w, c, None, ALU.mult).then_inc(self.added, 1)
            else:
                dve.wait_ge(self.added, j - 1)
                self.pr.nc.vector.scalar_tensor_tensor(acc, w, c, acc, ALU.mult, ALU.add).then_inc(self.added, 1)

    def reduce(self, pe, part):
        pe.wait_ge(self.added, 2 * KT * (part + 1))
        for column in range(2):
            for m in range(KT):
                at = MOD_PARTS * KT * column + KT * part + m
                last = self.pr.nc.tensor.matmul(self.pr.bank[6][:, at:at + 1], self.acc[:, part % 2, column, m * P:(m + 1) * P],
                                                self.pr.c["ones"][:, 0:1], start=True, stop=True)
        last.then_inc(self.reduced, 1)

    def finish(self, dve):
        pr, nc = self.pr, self.pr.nc
        n = MOD_PARTS * KT
        dve.wait_ge(self.reduced, MOD_PARTS)
        nc.vector.tensor_tensor(pr.mod[:, :, :], pr.bank[6][:, 0:2 * n].rearrange("p (two n) -> p two n", two=2),
                                pr.param_cols("b_mod").unsqueeze(1).to_broadcast([P, 2, n]), ALU.add).then_inc(self.made, 1)
        dve.wait_ge(self.made, 1)
        for i, (column, part, gain) in enumerate(((0, 1, "norm1"), (1, 1, "norm1"), (0, 4, "norm2"))):
            nc.vector.scalar_tensor_tensor(pr.gains[:, i, :], pr.mod[:, column, KT * part:KT * (part + 1)], 1.0,
                                           pr.param_cols(gain), ALU.add, ALU.mult).then_inc(self.made, 1)


def retention_block(pr, V, W, out_hi, out_lo, o, sq):
    nc, c = pr.nc, pr.c
    H = RET_HEADS
    with ExitStack() as ctx:
        t = lambda name, shape: pr.tile("rt_" + name, shape, F32, ctx)
        table, turned, rot_sb = t("table", [P, 2, T]), t("turned", [P, 2, T]), t("rot", [P, P])
        vN, kcN, vcN = t("v_tokens", [P, TB, T]), t("kc_tokens", [P, CTX_T, T]), t("vc_tokens", [P, CTX_T, T])
        rel, strip, strip_b = t("rel", [P, 4, 896]), t("strip", [P, 2, 896]), t("strip_b", [P, 896])
        steps, ctx_steps = t("steps", [P, 2, T]), t("ctx_steps", [P, 2, CTX_T])
        kcd = t("kc_decayed", [P, 2, CTX_T, P])
        dq = t("q_decayed", [P, 2, T])
        S = t("scores", [P, 2, TB, T])
        state = t("state", [P, 2, P])
        sm = t("small", [P, 6, 8])
        cw = t("ctx_weight", [P, 8, CTX_T])
        rstd = turned
        s = pr.stage_sems("rt_", ("in", "rot", "sin", "cos", "roped", "tr", "trout", "rate", "lg", "cw", "kcd", "state", "stateout",
              "e1", "e2", "dq", "strip", "score", "sout", "o", "oout", "mean", "centred", "sq", "var", "log", "rstd",
              "silu", "y", "hi", "lo"))
        with nc.Block() as block:
            @block.sync
            def _(sp):
                for dst, key, a in ((table, "rope_ret", 2), (rel, "rel", 4), (steps, "steps", 2), (ctx_steps, "ctx_steps", 2)):
                    sp.dma_start(dst[:, :, :], pr.dram[key].rearrange("p (a t) -> p a t", a=a)).then_inc(s["in"], 16)
                sp.dma_start(rot_sb[:, :], pr.dram["rot_ret"]).then_inc(s["in"], 16)
                pr.stream(sp, pr.taken + RAW_SLOTS)

            @block.tensor
            def _(pe):
                pe.wait_ge(s["in"], 80)
                for i in range(8):
                    if i >= 2:
                        pe.wait_ge(s["sin"], i - 1)
                    nc.tensor.matmul(pr.bank[i % 2], rot_sb[:, :], V[:, i, :], start=True, stop=True).then_inc(s["rot"], 1)
                srcs = [(V, 8, b) for b in range(TB)] + [(W, 0, b) for b in range(CTX_T)] + [(W, 4, b) for b in range(CTX_T)]
                for i, (src, first, b) in enumerate(srcs):
                    if i >= 2:
                        pe.wait_ge(s["trout"], i - 1)
                    for j in range(4):
                        last = nc.tensor.transpose(pr.bank[2 + i % 2][:, j * P:(j + 1) * P],
                                                   src[:, first + j, b * P:(b + 1) * P], c["ident"])
                    last.then_inc(s["tr"], 1)
                pe.wait_ge(s["roped"], 8)
                pe.wait_ge(s["trout"], 8)
                for h in range(H):
                    for d in range(2):
                        pe.wait_ge(s["kcd"], 2 * (2 * h + d + 1))
                        if d == 0 and h:
                            pe.wait_ge(s["stateout"], 2 * h)
                        for b in range(CTX_T):
                            last = nc.tensor.matmul(pr.bank[7][:, d * P:(d + 1) * P], kcd[:, d, b, :],
                                                    vcN[:, b, h * P:(h + 1) * P], start=(b == 0), stop=(b == CTX_T - 1))
                        last.then_inc(s["state"], 1)
                    for j in range(TB):
                        n = TB * h + j
                        if n >= 2:
                            pe.wait_ge(s["sout"], n - 1)
                        nc.tensor.matmul(pr.bank[n % 2], V[:, 4 + h, j * P:(j + 1) * P], V[:, h, :], start=True, stop=True)\
                            .then_inc(s["score"], 1)
                    if h >= 2:
                        pe.wait_ge(s["oout"], h - 1)
                    out = pr.bank[2 + h % 2]
                    for j in range(TB):
                        pe.wait_ge(s["sout"], TB * h + j + 1)
                        nc.tensor.matmul(out, vN[:, j, h * P:(h + 1) * P], S[:, h % 2, j, :], start=(j == 0), stop=False)
                    pe.wait_ge(s["stateout"], 2 * h + 2)
                    pe.wait_ge(s["dq"], 2 * h + 2)
                    for d in range(2):
                        last = nc.tensor.matmul(out, state[:, d, :], dq[:, d, :], start=False, stop=(d == 1))
                    last.then_inc(s["o"], 1)
                    pe.wait_ge(s["oout"], h + 1)
                    if h >= 2:
                        pe.wait_ge(s["centred"], h - 1)
                    nc.tensor.matmul(pr.bank[4 + h % 2], c["ones"], o[:, h % 2, :], start=True, stop=True).then_inc(s["mean"], 1)
                    pe.wait_ge(s["sq"], h + 1)
                    if h:
                        pe.wait_ge(s["log"], h)
                    nc.tensor.matmul(pr.bank[6], c["ones"], sq[:, h % 2, :], start=True, stop=True).then_inc(s["var"], 1)

            @block.scalar
            def _(act):
                nc.scalar.activation(sm[:, 0, :], pr.param_cols("rate"), ACT.Exp).then_inc(s["rate"], 1)
                act.wait_ge(s["lg"], 1)
                nc.scalar.activation(sm[:, 2, :], sm[:, 1, :], ACT.Ln).then_inc(s["rate"], 1)
                act.wait_ge(s["in"], 80)
                act.wait_ge(s["lg"], 5)
                for d in range(2):
                    for h in range(H):
                        nc.scalar.activation(cw[:, 4 * d + h, :], ctx_steps[:, d, :], ACT.Exp, scale=sm[:, 5, 4 * d + h:4 * d + h + 1])\
                            .then_inc(s["cw"], 1)
                for i in range(8):
                    act.wait_ge(s["tr"], i + 1)
                    dst = vN[:, i, :] if i < 4 else kcN[:, i - 4, :] if i < 6 else vcN[:, i - 6, :]
                    nc.scalar.copy(dst, pr.bank[2 + i % 2]).then_inc(s["trout"], 1)
                for h in range(H):
                    for d in range(2):
                        lg = sm[:, 5, 4 * d + h:4 * d + h + 1]
                        if h:
                            act.wait_ge(s["strip"], 3 * h)
                        nc.scalar.activation(strip[:, 1, :] if d == 0 else strip_b[:, :], rel[:, d, :], ACT.Exp, scale=lg)\
                            .then_inc(s["e1"], 1)
                    for d in range(2):
                        lg = sm[:, 5, 4 * d + h:4 * d + h + 1]
                        if h:
                            act.wait_ge(s["o"], h)
                        nc.scalar.activation(dq[:, d, :], steps[:, d, :], ACT.Exp, scale=lg).then_inc(s["e2"], 1)
                    for d in range(2):
                        act.wait_ge(s["state"], 2 * h + 2)
                        nc.scalar.copy(state[:, d, :], pr.bank[7][:, d * P:(d + 1) * P]).then_inc(s["stateout"], 1)
                    act.wait_ge(s["o"], h + 1)
                    if h >= 2:
                        act.wait_ge(s["lo"], h - 1)
                    nc.scalar.copy(o[:, h % 2, :], pr.bank[2 + h % 2]).then_inc(s["oout"], 1)
                    act.wait_ge(s["centred"], h + 1)
                    nc.scalar.activation(sq[:, h % 2, :], o[:, h % 2, :], ACT.Square).then_inc(s["sq"], 1)
                    nc.scalar.activation(V[:, 12 + h, :], V[:, 12 + h, :], ACT.Silu).then_inc(s["silu"], 1)
                    act.wait_ge(s["var"], h + 1)
                    nc.scalar.activation(rstd[:, h % 2, :], pr.bank[6], ACT.Ln, scale=1.0 / P, bias=pr.eps(0)).then_inc(s["log"], 1)
                    act.wait_ge(s["log"], h + 1)
                    nc.scalar.activation(rstd[:, h % 2, :], rstd[:, h % 2, :], ACT.Exp, scale=-0.5).then_inc(s["rstd"], 1)
                    act.wait_ge(s["y"], 2 * h + 2)
                    nc.scalar.copy(out_hi[:, h, :], o[:, h % 2, :]).then_inc(s["hi"], 1)

            @block.vector
            def _(dve):
                dve.wait_ge(s["rate"], 1)
                nc.vector.tensor_scalar(sm[:, 1, :], sm[:, 0, :], -1.0, 1.0, ALU.mult, ALU.add).then_inc(s["lg"], 1)
                dve.wait_ge(s["lg"], 1)
                nc.vector.scalar_tensor_tensor(sm[:, 3, :], sm[:, 1, :], -1.0, sm[:, 0, :], ALU.add, ALU.add).then_inc(s["lg"], 1)
                nc.vector.reciprocal(sm[:, 4, :], sm[:, 1, :]).then_inc(s["lg"], 1)
                dve.wait_ge(s["lg"], 3)
                nc.vector.tensor_tensor(sm[:, 3, :], sm[:, 3, :], sm[:, 4, :], ALU.mult).then_inc(s["lg"], 1)
                dve.wait_ge(s["lg"], 4)
                dve.wait_ge(s["rate"], 2)
                nc.vector.tensor_tensor(sm[:, 5, :], sm[:, 2, :], sm[:, 3, :], ALU.subtract).then_inc(s["lg"], 1)
                dve.wait_ge(s["in"], 80)
                for i in range(8):
                    dve.wait_ge(s["rot"], i + 1)
                    if i >= 2:
                        dve.wait_ge(s["roped"], i - 1)
                    nc.vector.tensor_tensor(turned[:, i % 2, :], pr.bank[i % 2], table[:, 1, :], ALU.mult).then_inc(s["sin"], 1)
                    nc.vector.tensor_tensor(V[:, i, :], V[:, i, :], table[:, 0, :], ALU.mult).then_inc(s["cos"], 1)
                    dve.wait_ge(s["sin"], i + 1)
                    dve.wait_ge(s["cos"], i + 1)
                    nc.vector.tensor_tensor(V[:, i, :], V[:, i, :], turned[:, i % 2, :], ALU.add).then_inc(s["roped"], 1)
                dve.wait_ge(s["roped"], 8)
                for h in range(H):
                    dve.wait_ge(s["trout"], 6)
                    dve.wait_ge(s["cw"], 8)
                    for d in range(2):
                        if h:
                            dve.wait_ge(s["state"], 2 * h)
                        for b in range(CTX_T):
                            nc.vector.tensor_scalar(kcd[:, d, b, :], kcN[:, b, h * P:(h + 1) * P], cw[:, 4 * d + h, b:b + 1],
                                                    None, ALU.mult).then_inc(s["kcd"], 1)
                    dve.wait_ge(s["e1"], 2 * h + 2)
                    if h:
                        dve.wait_ge(s["strip"], 3 * h)
                    if h:
                        dve.wait_ge(s["sout"], TB * h)
                    nc.vector.tensor_tensor(strip[:, 0, :], strip[:, 1, :], rel[:, 2, :], ALU.mult).then_inc(s["strip"], 1)
                    nc.vector.tensor_tensor(strip_b[:, :], strip_b[:, :], rel[:, 3, :], ALU.mult).then_inc(s["strip"], 1)
                    dve.wait_ge(s["strip"], 3 * h + 2)
                    nc.vector.tensor_tensor(strip[:, 0, :], strip[:, 0, :], strip_b[:, :], ALU.add).then_inc(s["strip"], 1)
                    for d in range(2):
                        dve.wait_ge(s["e2"], 2 * h + d + 1)
                        nc.vector.tensor_tensor(dq[:, d, :], V[:, h, :], dq[:, d, :], ALU.mult).then_inc(s["dq"], 1)
                    dve.wait_ge(s["strip"], 3 * h + 3)
                    for j in range(TB):
                        n = TB * h + j
                        dve.wait_ge(s["score"], n + 1)
                        if h >= 2:
                            dve.wait_ge(s["o"], h - 1)
                        at = 384 - P * j
                        nc.vector.tensor_tensor(S[:, h % 2, j, :], pr.bank[n % 2], strip[:, 0, at:at + T], ALU.mult)\
                            .then_inc(s["sout"], 1)
                    x = o[:, h % 2, :]
                    dve.wait_ge(s["mean"], h + 1)
                    nc.vector.scalar_tensor_tensor(x, pr.bank[4 + h % 2], -1.0 / P, x, ALU.mult, ALU.add).then_inc(s["centred"], 1)
                    dve.wait_ge(s["rstd"], h + 1)
                    nc.vector.scalar_tensor_tensor(x, x, pr.param("gn_g")(h), rstd[:, h % 2, :], ALU.mult, ALU.mult)\
                        .then_inc(s["y"], 1)
                    dve.wait_ge(s["y"], 2 * h + 1)
                    dve.wait_ge(s["silu"], h + 1)
                    nc.vector.tensor_tensor(x, x, V[:, 12 + h, :], ALU.mult).then_inc(s["y"], 1)
                    dve.wait_ge(s["hi"], h + 1)
                    nc.vector.tensor_tensor(out_lo[:, h, :], x, out_hi[:, h, :].bitcast(F32), ALU.subtract).then_inc(s["lo"], 1)
        pr.release(s)




def gqa_block(pr, A, B, out_hi, out_lo):
    nc, c = pr.nc, pr.c
    with ExitStack() as ctx:
        t = lambda name, shape: pr.tile("at_" + name, shape, F32, ctx)
        table, turned, rot_sb = t("table", [P, 2, T]), t("turned", [P, 2, T]), t("rot", [P, P])
        sq, rstd = t("sq", [P, 2, T]), t("rstd", [P, 2, T])
        vN = t("v_tokens", [P, KEY_T, P])
        prob, probT = t("prob", [P, 3, KEYS]), t("probT", [P, 2, KEYS])
        oN = t("o_tokens", [P, 2, TB, P])
        small, qgain = t("small", [P, 4, 4]), t("qgain", [P, 1])
        s = pr.stage_sems("at_", ("in", "qgain", "sq", "mean", "log", "rstd", "normed", "rot", "sin", "cos", "roped", "vtr", "vout",
              "score", "negmax", "exp", "tr", "tra", "trv", "pv", "inv", "oout", "otr", "hi", "lo"))
        items = [(A[:, i, :], T) for i in range(5)] + [(B[:, 0, :], TC)]
        units = [(i, q, g) for i in range(ATT_TILES) for q in range(TB) for g in range(2)]
        U = len(units)
        with nc.Block() as block:
            @block.sync
            def _(sp):
                sp.dma_start(table[:, :, :], pr.dram["rope_att"].rearrange("p (a t) -> p a t", a=2)).then_inc(s["in"], 16)
                sp.dma_start(rot_sb[:, :], pr.dram["rot_att"]).then_inc(s["in"], 16)
                pr.stream(sp, pr.taken + RAW_SLOTS)

            @block.tensor
            def _(pe):
                pe.wait_ge(s["in"], 32)
                for b in range(KEY_T):
                    src = B[:, 1, b * P:(b + 1) * P] if b < CTX_T else A[:, 5, (b - CTX_T) * P:(b - CTX_T + 1) * P]
                    last = nc.tensor.transpose(pr.pair[3][:, b * P:(b + 1) * P], src, c["ident"])
                last.then_inc(s["vtr"], 1)
                for n, (x, w) in enumerate(items):
                    pe.wait_ge(s["sq"], n + 1)
                    if n >= 2:
                        pe.wait_ge(s["log"], n - 1)
                    nc.tensor.matmul(pr.bank[n % 2][:, 0:w], c["head_mean"], sq[:, n % 2, 0:w], start=True, stop=True)\
                        .then_inc(s["mean"], 1)
                for n in range(5):
                    pe.wait_ge(s["normed"], n + 1)
                    if n >= 2:
                        pe.wait_ge(s["sin"], n - 1)
                    nc.tensor.matmul(pr.bank[2 + n % 2], rot_sb[:, :], A[:, n, :], start=True, stop=True).then_inc(s["rot"], 1)
                pe.wait_ge(s["roped"], 5)
                pe.wait_ge(s["normed"], 6)
                pe.wait_ge(s["vout"], 1)
                for n in range(U + 3):
                    if n < U:
                        i, q, g = units[n]
                        h = slice(64 * g, 64 * g + 64)
                        if n >= 2:
                            pe.wait_ge(s["exp"], n - 1)
                        query = A[h, i, q * P:(q + 1) * P]
                        nc.tensor.matmul(pr.pair[n % 2][:, 256:512], query, B[h, 0, :], start=True, stop=True)
                        nc.tensor.matmul(pr.pair[n % 2][:, 512:1024], query, A[h, 4, :], start=True, stop=True)\
                            .then_inc(s["score"], 1)
                    if 1 <= n <= U:
                        m = n - 1
                        pe.wait_ge(s["exp"], m + 1)
                        if m:
                            pe.wait_ge(s["tra"], m)
                            pe.wait_ge(s["trv"], m)
                        for k in range(KEY_T):
                            last = nc.tensor.transpose(pr.pair[2][:, k * P:(k + 1) * P], prob[:, m % 3, k * P:(k + 1) * P], c["ident"])
                        last.then_inc(s["tr"], 1)
                    if 2 <= n <= U + 1:
                        m = n - 2
                        i, q, g = units[m]
                        pe.wait_ge(s["tra"], m + 1)
                        pe.wait_ge(s["trv"], m + 1)
                        if m >= 2:
                            pe.wait_ge(s["oout"], m - 1)
                        if m % 8 == 1 and m > 8:
                            pe.wait_ge(s["lo"], m // 8)
                        for k in range(KEY_T):
                            last = nc.tensor.matmul(pr.bank[6 + m % 2][:, 0:64], probT[:, m % 2, k * P:(k + 1) * P],
                                                    vN[:, k, 64 * g:64 * g + 64], start=(k == 0), stop=(k == KEY_T - 1))
                        last.then_inc(s["pv"], 1)
                    if n >= 3 and (n - 2) % 8 == 0:
                        i = (n - 2) // 8 - 1
                        pe.wait_ge(s["oout"], 8 * (i + 1))
                        if i:
                            pe.wait_ge(s["lo"], i)
                        for q in range(TB):
                            last = nc.tensor.transpose(pr.bank[7][:, q * P:(q + 1) * P], oN[:, i % 2, q, :], c["ident"])
                        last.then_inc(s["otr"], 1)

            @block.scalar
            def _(act):
                for n, (x, w) in enumerate(items):
                    if n >= 2:
                        act.wait_ge(s["mean"], n - 1)
                    nc.scalar.activation(sq[:, n % 2, 0:w], x, ACT.Square).then_inc(s["sq"], 1)
                    act.wait_ge(s["mean"], n + 1)
                    if n >= 2:
                        act.wait_ge(s["normed"], n - 1)
                    nc.scalar.activation(rstd[:, n % 2, 0:w], pr.bank[n % 2][:, 0:w], ACT.Ln, bias=pr.eps(0)).then_inc(s["log"], 1)
                    act.wait_ge(s["log"], n + 1)
                    nc.scalar.activation(rstd[:, n % 2, 0:w], rstd[:, n % 2, 0:w], ACT.Exp, scale=-0.5).then_inc(s["rstd"], 1)
                act.wait_ge(s["vtr"], 1)
                nc.scalar.copy(vN[:, :, :], pr.pair[3][:, 0:KEYS].rearrange("p (k t) -> p k t", k=KEY_T)).then_inc(s["vout"], 1)
                for n in range(U + 2):
                    if n < U:
                        act.wait_ge(s["negmax"], n + 1)
                        if n >= 3:
                            act.wait_ge(s["tr"], n - 2)
                        nc.scalar.activation(prob[:, n % 3, :], pr.pair[n % 2][:, 256:1024], ACT.Exp,
                                             bias=small[:, n % 4, 0:1], accum_out=small[:, n % 4, 1:2]).then_inc(s["exp"], 1)
                    if 1 <= n <= U:
                        m = n - 1
                        act.wait_ge(s["tr"], m + 1)
                        if m >= 2:
                            act.wait_ge(s["pv"], m - 1)
                        nc.scalar.copy(probT[:, m % 2, 0:T], pr.pair[2][:, 0:T]).then_inc(s["tra"], 1)
                    if n >= 2 and (n - 1) % 8 == 0:
                        i = (n - 1) // 8 - 1
                        act.wait_ge(s["otr"], i + 1)
                        nc.scalar.copy(out_hi[:, i, :], pr.bank[7]).then_inc(s["hi"], 1)

            @block.vector
            def _(dve):
                dve.wait_ge(s["in"], 32)
                nc.vector.tensor_scalar(qgain[:, :], pr.param("q_norm")(0), ATT_SCALE, None, ALU.mult).then_inc(s["qgain"], 1)
                dve.wait_ge(s["qgain"], 1)
                for n, (x, w) in enumerate(items):
                    dve.wait_ge(s["rstd"], n + 1)
                    nc.vector.scalar_tensor_tensor(x, x, qgain[:, :] if n < 4 else pr.param("k_norm")(0),
                                                   rstd[:, n % 2, 0:w], ALU.mult, ALU.mult).then_inc(s["normed"], 1)
                for i in range(5):
                    dve.wait_ge(s["rot"], i + 1)
                    if i >= 2:
                        dve.wait_ge(s["roped"], i - 1)
                    nc.vector.tensor_tensor(turned[:, i % 2, :], pr.bank[2 + i % 2], table[:, 1, :], ALU.mult).then_inc(s["sin"], 1)
                    nc.vector.tensor_tensor(A[:, i, :], A[:, i, :], table[:, 0, :], ALU.mult).then_inc(s["cos"], 1)
                    dve.wait_ge(s["sin"], i + 1)
                    dve.wait_ge(s["cos"], i + 1)
                    nc.vector.tensor_tensor(A[:, i, :], A[:, i, :], turned[:, i % 2, :], ALU.add).then_inc(s["roped"], 1)
                for n in range(U + 2):
                    if n < U:
                        dve.wait_ge(s["score"], n + 1)
                        if n >= 4:
                            dve.wait_ge(s["oout"], n - 3)
                        nc.vector.tensor_reduce(small[:, n % 4, 0:1], pr.pair[n % 2][:, 256:1024], AX_X, ALU.max, negate=True)\
                            .then_inc(s["negmax"], 1)
                    if 1 <= n <= U:
                        m = n - 1
                        dve.wait_ge(s["tr"], m + 1)
                        if m >= 2:
                            dve.wait_ge(s["pv"], m - 1)
                        nc.vector.tensor_copy(probT[:, m % 2, T:KEYS], pr.pair[2][:, T:KEYS]).then_inc(s["trv"], 1)
                        dve.wait_ge(s["exp"], m + 1)
                        nc.vector.reciprocal(small[:, m % 4, 2:3], small[:, m % 4, 1:2]).then_inc(s["inv"], 1)
                    if n >= 2:
                        m = n - 2
                        i, q, g = units[m]
                        dve.wait_ge(s["pv"], m + 1)
                        dve.wait_ge(s["inv"], m + 1)
                        if m >= 16:
                            dve.wait_ge(s["otr"], m // 8 - 1)
                        nc.vector.tensor_scalar(oN[:, i % 2, q, 64 * g:64 * g + 64], pr.bank[6 + m % 2][:, 0:64],
                                                small[:, m % 4, 2:3], None, ALU.mult).then_inc(s["oout"], 1)
                        if m % 8 == 7:
                            dve.wait_ge(s["hi"], i + 1)
                            nc.vector.tensor_tensor(out_lo[:, i, :], pr.bank[7], out_hi[:, i, :].bitcast(F32), ALU.subtract)\
                                .then_inc(s["lo"], 1)
        pr.release(s)




def bass_two_blocks(nc, dram, out):
    with ExitStack() as ctx:
        pr = Program(nc, ctx, dram)
        stored = pr.sem("out_stored")
        h_spill = nc.dram_tensor("h_spill", (2, P, KT * T), F32, kind="Internal").ap()
        params = pr.tile("params", [P, N_PARAMS])
        derived = pr.tile("derived", [P, 24])
        consts = pr.tile("consts", [P, 4 * P + 64 + 6])
        pr.c = {"ident": consts[:, 0:P], "ones": consts[:, P:2 * P], "head_ones": consts[:, 2 * P:3 * P],
                "head_mean": consts[:, 3 * P:4 * P], "ident64": consts[:, 4 * P:4 * P + 64],
                "own_weight": derived[:, 0:15], "one_minus_ka": derived[:, 15:19], "subln_scaled": derived[:, 19:20]}
        pr.eps = lambda i: consts[:, 4 * P + 64 + i:4 * P + 65 + i]
        pr.param_cols = lambda name: params[:, PARAM_COLS[name][0]:sum(PARAM_COLS[name])]
        pr.param = lambda name: (lambda i: params[:, PARAM_COLS[name][0] + i:PARAM_COLS[name][0] + i + 1])
        pr.mod = pr.tile("mod", [P, 2, 48])
        pr.gains = pr.tile("gains", [P, 3, 8])
        silu_c = pr.tile("silu_c", [P, 2, 8])
        x = pr.tile("x", [P, KT, T])
        o_spill = nc.dram_tensor("o_spill", (2, P, 4 * T), F32, kind="Internal").ap()
        y_spill = nc.dram_tensor("y_spill", (2, P, 4 * T), F32, kind="Internal").ap()
        x_view = lambda ap: ap.rearrange("(k p) t -> p k t", p=P)
        with ExitStack() as first_half:
            with ExitStack() as rwkv_scope:
                U = pr.tile("rwkv_in", [P, R_TILES, T], F32, rwkv_scope)
                w_lora = pr.tile("w_lora", [P, 2, RW], F32, rwkv_scope)
                g2 = pr.tile("g2", [P, RW], F32, rwkv_scope)
                with ExitStack() as in_scope:
                    hi = pr.tile("w_hi", [P, SPLIT_SLOTS, 1024], F32R, in_scope)
                    lo = pr.tile("w_lo", [P, SPLIT_SLOTS, 1024], F32R, in_scope)
                    h_hi = pr.tile("h_hi", [P, KT, T], F32R, in_scope)
                    h_lo = pr.tile("h_lo", [P, KT, T], F32R, in_scope)
                    with ExitStack() as x_scope:
                        buf = pr.tile("norm_buf0", [P, KT, T], F32, x_scope)
                        rstd = pr.tile("norm_rstd0", [P, 2, T], F32, x_scope)
                        loaded, made, x_in = pr.sem("consts_in"), pr.sem("derived_made"), pr.sem("x_in")
                        with nc.Block() as block:
                            @block.sync
                            def _(sp):
                                sp.dma_start(x[:, :, :], x_view(dram["x"])).then_inc(x_in, 16)
                                sp.dma_start(params[:, :], dram["params"]).then_inc(loaded, 16)
                                sp.dma_start(consts[:, :], dram["consts"]).then_inc(loaded, 16)
                                pr.stream(sp, RAW_SLOTS)
                                sp.dma_start(w_lora[:, :, :], dram["w_lora"].rearrange("p (a n) -> p a n", a=2)).then_inc(loaded, 16)
                                sp.dma_start(g2[:, :], dram["g2"]).then_inc(loaded, 16)
                                sp.wait_ge(x_in, 16)
                                sp.wait_ge(loaded, 64)

                            @block.vector
                            def _(dve):
                                dve.wait_ge(loaded, 64)
                                nc.vector.tensor_tensor(derived[:, 0:15], pr.param_cols("mu_prev"), pr.param_cols("mu_next"),
                                                        ALU.add).then_inc(made, 1)
                                dve.wait_ge(made, 1)
                                nc.vector.tensor_scalar(derived[:, 0:15], derived[:, 0:15], -1.0, 1.0, ALU.mult, ALU.add).then_inc(made, 1)
                                nc.vector.tensor_scalar(derived[:, 15:19], pr.param_cols("k_a"), -1.0, 1.0, ALU.mult, ALU.add)\
                                    .then_inc(made, 1)
                                nc.vector.tensor_scalar(derived[:, 19:20], pr.param("subln")(0), 1.0 - LAMBDA_INIT, None, ALU.mult)\
                                    .then_inc(made, 1)
                        norm_block(pr, {"sq": buf, "rstd": rstd, "y": buf}, lambda k: x[:, k, :], h_hi, h_lo, pr.param("norm_mix"))
                    spilled = pr.sem("h_spilled")
                    h_parts = split_parts(h_hi, h_lo, KT)
                    o_hi, o_lo = pr.tile("o_hi", [P, 4, T], F32R, in_scope), pr.tile("o_lo", [P, 4, T], F32R, in_scope)
                    with ExitStack() as da_scope:
                        Q = pr.tile("da_in", [P, 12, T], F32, da_scope)
                        evac = pr.sem("da_in_out")
                        gemm_block(pr, hi, lo, [Job(pr.taken + n, h_parts) for n in range(12)],
                                   copy_out(pr, evac, lambda n: Q[:, n, :], scale=lambda n: 64 ** -0.5 if n < 4 else 1.0),
                                   nothing, evac, lambda n: n + 1)
                        da_attention_block(pr, Q, U, o_hi, o_lo)
                    pad = pr.tile("shift_pad", [P, 2, T + 2], F32, in_scope)
                    s_act, s_dve, s_zero = pr.sem("shift_act"), pr.sem("shift_dve"), pr.sem("pad_zeroed")

                    def shift_act(act, n, bank, done):
                        act.wait_ge(pr.job_done, done)
                        if n >= 2:
                            act.wait_ge(s_dve, 2 * (n - 1))
                        nc.scalar.copy(pad[:, n % 2, 1:T + 1], bank).then_inc(s_act, 1)
                        nc.scalar.mul(U[:, n, :], bank, pr.c["own_weight"][:, n:n + 1]).then_inc(s_act, 1)

                    def shift_dve(dve, n, bank, done):
                        if n == 0:
                            for j in range(2):
                                nc.vector.memset(pad[:, j, 0:1], 0.0).then_inc(s_zero, 1)
                                nc.vector.memset(pad[:, j, T + 1:T + 2], 0.0).then_inc(s_zero, 1)
                            dve.wait_ge(s_zero, 4)
                        dve.wait_ge(s_act, 2 * n + 2)
                        nc.vector.scalar_tensor_tensor(U[:, n, :], pad[:, n % 2, 0:T], pr.param("mu_prev")(n), U[:, n, :],
                                                       ALU.mult, ALU.add).then_inc(s_dve, 1)
                        dve.wait_ge(s_dve, 2 * n + 1)
                        nc.vector.scalar_tensor_tensor(U[:, n, :], pad[:, n % 2, 2:T + 2], pr.param("mu_next")(n), U[:, n, :],
                                                       ALU.mult, ALU.add).then_inc(s_dve, 1)

                    with nc.Block() as block:
                        @block.sync
                        def _(sp):
                            sp.dma_start(h_spill[0], h_hi[:, :, :].bitcast(F32).rearrange("p k t -> p (k t)")).then_inc(spilled, 16)
                            sp.dma_start(h_spill[1], h_lo[:, :, :].bitcast(F32).rearrange("p k t -> p (k t)")).then_inc(spilled, 16)
                            sp.dma_start(o_spill[0], o_hi[:, :, :].bitcast(F32).rearrange("p k t -> p (k t)")).then_inc(spilled, 16)
                            sp.dma_start(o_spill[1], o_lo[:, :, :].bitcast(F32).rearrange("p k t -> p (k t)")).then_inc(spilled, 16)
                    gemm_block(pr, hi, lo, [Job(pr.taken + n, h_parts) for n in range(R_TILES)], shift_act, shift_dve,
                               s_act, lambda n: 2 * n + 2)
                    tanhed = pr.sem("tanhed")
                    with nc.Block() as block:
                        @block.scalar
                        def _(act):
                            nc.scalar.activation(U[:, 12, :], U[:, 12, :], ACT.Tanh).then_inc(tanhed, 1)
                            for i, key in enumerate(("c", "c_ctx")):
                                nc.scalar.activation(silu_c[:, i, :], pr.param_cols(key), ACT.Silu).then_inc(tanhed, 1)

                        @block.sync
                        def _(sp):
                            sp.wait_ge(spilled, 64)
                rwkv_block(pr, U, w_lora, x)
                y_hi, y_lo = pr.tile("y_hi", [P, 4, T], F32R, rwkv_scope), pr.tile("y_lo", [P, 4, T], F32R, rwkv_scope)
                rwkv_out_block(pr, U, g2, y_hi, y_lo)
                with nc.Block() as block:
                    @block.sync
                    def _(sp):
                        sp.dma_start(y_spill[0], y_hi[:, :, :].bitcast(F32).rearrange("p k t -> p (k t)")).then_inc(spilled, 16)
                        sp.dma_start(y_spill[1], y_lo[:, :, :].bitcast(F32).rearrange("p k t -> p (k t)")).then_inc(spilled, 16)
                        sp.wait_ge(spilled, 96)
        ahead_sq, rstd = pr.tile("norm_sq", [P, 2, T]), pr.tile("norm_rstd", [P, 2, T])
        ahead = NormAhead(pr, ahead_sq, rstd)
        with ExitStack() as scope:
            hi, lo = (pr.tile(f"w_{k}1", [P, SPLIT_SLOTS, 1024], F32R, scope) for k in ("hi", "lo"))
            h_hi, h_lo = pr.tile("h_hi1", [P, KT, T], F32R, scope), pr.tile("h_lo1", [P, KT, T], F32R, scope)
            with ExitStack() as merge_scope:
                o_hi, o_lo = pr.tile("o_hi1", [P, 4, T], F32R, merge_scope), pr.tile("o_lo1", [P, 4, T], F32R, merge_scope)
                y_hi, y_lo = pr.tile("y_hi1", [P, 4, T], F32R, merge_scope), pr.tile("y_lo1", [P, 4, T], F32R, merge_scope)
                m_hi = pr.tile("m_hi", [P, KT, T], F32R, merge_scope)
                m_lo = pr.tile("m_lo", [P, KT, T], F32R, merge_scope)
                sig, part = pr.tile("sig", [P, 2, T], F32, merge_scope), pr.tile("part", [P, 2, 2, T], F32, merge_scope)
                back = pr.sem("h_back")
                with nc.Block() as block:
                    @block.sync
                    def _(sp):
                        sp.dma_start(h_hi[:, :, :].bitcast(F32).rearrange("p k t -> p (k t)"), h_spill[0]).then_inc(back, 16)
                        sp.dma_start(h_lo[:, :, :].bitcast(F32).rearrange("p k t -> p (k t)"), h_spill[1]).then_inc(back, 16)
                        sp.dma_start(o_hi[:, :, :].bitcast(F32).rearrange("p k t -> p (k t)"), o_spill[0]).then_inc(back, 16)
                        sp.dma_start(o_lo[:, :, :].bitcast(F32).rearrange("p k t -> p (k t)"), o_spill[1]).then_inc(back, 16)
                        sp.dma_start(y_hi[:, :, :].bitcast(F32).rearrange("p k t -> p (k t)"), y_spill[0]).then_inc(back, 16)
                        sp.dma_start(y_lo[:, :, :].bitcast(F32).rearrange("p k t -> p (k t)"), y_spill[1]).then_inc(back, 16)
                        sp.dma_start(x[:, :, :], x_view(dram["x"])).then_inc(back, 16)
                        sp.wait_ge(back, 112)
                evac, g_sig, g_part, g_sum, g_hi, g_lo = (pr.sem("merge_" + k) for k in ("out", "sig", "part", "sum", "hi", "lo"))

                def merge_act(act, n, bank, done):
                    tile, j = divmod(n, 4)
                    act.wait_ge(pr.job_done, done)
                    if j in (0, 2):
                        e = 2 * tile + j // 2
                        if e >= 2:
                            act.wait_ge(g_part, e - 1)
                        nc.scalar.activation(sig[:, e % 2, :], bank, ACT.Sigmoid).then_inc(g_sig, 1)
                    if j == 3:
                        act.wait_ge(g_sum, tile + 1)
                        nc.scalar.copy(m_hi[:, tile, :], part[:, tile % 2, 0, :]).then_inc(g_hi, 1)

                def merge_dve(dve, n, bank, done):
                    tile, j = divmod(n, 4)
                    if j in (1, 3):
                        e = 2 * tile + j // 2
                        dve.wait_ge(pr.job_done, done)
                        dve.wait_ge(g_sig, e + 1)
                        if tile >= 2:
                            dve.wait_ge(g_lo, tile - 1)
                        nc.vector.tensor_tensor(part[:, tile % 2, j // 2, :], bank, sig[:, e % 2, :], ALU.mult).then_inc(g_part, 1)
                    if j == 3:
                        dve.wait_ge(g_part, 2 * tile + 2)
                        nc.vector.tensor_tensor(part[:, tile % 2, 0, :], part[:, tile % 2, 0, :], part[:, tile % 2, 1, :], ALU.add)\
                            .then_inc(g_sum, 1)
                        dve.wait_ge(g_hi, tile + 1)
                        nc.vector.tensor_tensor(m_lo[:, tile, :], part[:, tile % 2, 0, :], m_hi[:, tile, :].bitcast(F32), ALU.subtract)\
                            .then_inc(g_lo, 1)

                def merge_wait(pe, n):
                    if n >= BANKS:
                        old = n - BANKS
                        e = 2 * (old // 4) + (old % 4) // 2
                        pe.wait_ge(g_sig if old % 2 == 0 else g_part, e + 1)

                moving = (split_parts(h_hi, h_lo, KT), split_parts(y_hi, y_lo, 4), split_parts(h_hi, h_lo, KT), split_parts(o_hi, o_lo, 4))
                gemm_block(pr, hi, lo, [Job(pr.taken + n, moving[n % 4]) for n in range(32)], merge_act, merge_dve,
                           evac, None, pe_wait=merge_wait)
                residual_gemm(pr, hi, lo, x, split_parts(m_hi, m_lo, KT), "out1",
                              ahead=ahead.begin(x, pr.param("norm_ffn"), h_hi, h_lo))
            modulation = Modulation(pr, scope, silu_c, spread=60)
            ff_stage(pr, hi, lo, x, split_parts(h_hi, h_lo, KT), "ff1", modulation=modulation,
                     rstd=rstd[:, 1, :], ahead=ahead.begin(x, pr.param("norm_ple"), h_hi, h_lo))
            with ExitStack() as s2:
                p_raw = pr.tile("p_raw", [P, 2, T], F32, s2)
                p_hi, p_lo = pr.tile("p_hi", [P, 2, T], F32R, s2), pr.tile("p_lo", [P, 2, T], F32R, s2)
                ple_stage(pr, hi, lo, x, split_parts(h_hi, h_lo, KT), p_raw, p_hi, p_lo, modulation, rstd[:, 1, :], ahead.begin(x))
        with ExitStack() as scope:
            a_hi, a_lo = pr.tile("a_hi", [P, KT, T], F32R, scope), pr.tile("a_lo", [P, KT, T], F32R, scope)
            with ExitStack() as s1:
                A, B = pr.tile("att_in", [P, 6, T], F32, s1), pr.tile("att_ctx", [P, 2, TC], F32, s1)
                with ExitStack() as s2:
                    V, W = pr.tile("ret_in", [P, 16, T], F32, s2), pr.tile("ret_ctx", [P, 8, TC], F32, s2)
                    with ExitStack() as s3:
                        hi, lo = (pr.tile(f"w_{k}3", [P, SPLIT_SLOTS, 1024], F32R, s3) for k in ("hi", "lo"))
                        c_hi, c_lo = pr.tile("c_hi", [P, KT, TC], F32R, s3), pr.tile("c_lo", [P, KT, TC], F32R, s3)
                        with ExitStack() as s4:
                            buf = pr.tile("norm_buf5", [P, KT, T], F32, s4)
                            rstd5 = pr.tile("norm_rstd5", [P, 2, T], F32, s4)
                            norm_block(pr, {"sq": buf, "rstd": rstd5, "y": buf}, lambda k: x[:, k, :], a_hi, a_lo,
                                       lambda k: pr.gains[:, 0, k:k + 1], bias=lambda k: pr.mod[:, 0, k:k + 1],
                                       before=(pr.param("norm_final"), rstd[:, 1, :]))
                            ctx_in = pr.sem("ctx_in")
                            with nc.Block() as block:
                                @block.sync
                                def _(sp):
                                    sp.dma_start(buf[:, :, 0:TC], x_view(dram["ctx"])).then_inc(ctx_in, 16)
                                    sp.wait_ge(ctx_in, 16)
                            norm_block(pr, {"sq": buf[:, :, TC:T], "rstd": rstd5, "y": buf[:, :, TC:T]}, lambda k: buf[:, k, 0:TC],
                                       c_hi, c_lo, lambda k: pr.gains[:, 1, k:k + 1], width=TC,
                                       bias=lambda k: pr.mod[:, 1, k:k + 1])
                        lat, con = split_parts(a_hi, a_lo, KT), split_parts(c_hi, c_lo, KT)
                        jobs, dests = [], []
                        for n in range(22):
                            scale = RET_SCALE if 4 <= n < 8 else 1.0
                            jobs.append(Job(pr.taken + n, lat))
                            dests.append((V[:, n, :] if n < 16 else A[:, n - 16, :], scale))
                            if 4 <= n < 12 or n >= 20:
                                jobs.append(Job(pr.taken + n, con, TC))
                                dests.append((W[:, n - 4, :] if n < 12 else B[:, n - 20, :], scale))
                        evac = pr.sem("in2_out")
                        gemm_block(pr, hi, lo, jobs, copy_out(pr, evac, lambda n: dests[n][0], scale=lambda n: dests[n][1]),
                                   nothing, evac, lambda n: n + 1)
                    retention_block(pr, V, W, a_hi, a_lo, ahead_sq, rstd)
                gqa_block(pr, A, B, a_hi[:, 4:8, :], a_lo[:, 4:8, :])
            hi, lo = (pr.tile(f"w_{k}4", [P, SPLIT_SLOTS, 1024], F32R, scope) for k in ("hi", "lo"))
            residual_gemm(pr, hi, lo, x, split_parts(a_hi, a_lo, KT), "out2", lambda n: pr.mod[:, 0, 16 + n:17 + n],
                          ahead=ahead.begin(x))
            with ExitStack() as s2:
                buf = pr.tile("norm_buf6", [P, KT, T], F32, s2)
                norm_block(pr, {"sq": None, "rstd": rstd, "y": buf}, lambda k: x[:, k, :], a_hi, a_lo,
                           lambda k: pr.gains[:, 2, k:k + 1], bias=lambda k: pr.mod[:, 0, 24 + k:25 + k], known=True)
            ff_stage(pr, hi, lo, x, split_parts(a_hi, a_lo, KT), "ff2", lambda n: pr.mod[:, 0, 40 + n:41 + n],
                     ahead=ahead.begin(x))
            normed = pr.sem("out_normed")
            with nc.Block() as block:
                @block.vector
                def _(dve):
                    for k in range(KT):
                        nc.vector.scalar_tensor_tensor(x[:, k, :], x[:, k, :], pr.param("final2")(k), rstd[:, 1, :],
                                                       ALU.mult, ALU.mult).then_inc(normed, 1)

                @block.sync
                def _(sp):
                    for k in range(0, KT, 2):
                        sp.wait_ge(normed, k + 2)
                        sp.dma_start(x_view(out)[:, k:k + 2, :], x[:, k:k + 2, :]).then_inc(stored, 16)
                    sp.wait_ge(stored, 16 * KT // 2)
        assert pr.taken == len(TILES) == pr.streamed


def residual_gemm(pr, hi, lo, x, moving, name, gate=None, ahead=None):
    nc = pr.nc
    evac = pr.sem(name + "_out")

    def add(dve, n, bank, done):
        dve.wait_ge(pr.job_done, done)
        if gate is None:
            nc.vector.tensor_tensor(x[:, n, :], x[:, n, :], bank, ALU.add).then_inc(evac, 1)
        else:
            nc.vector.scalar_tensor_tensor(x[:, n, :], bank, gate(n), x[:, n, :], ALU.mult, ALU.add).then_inc(evac, 1)

        ahead.dve(dve, n)

    gemm_block(pr, hi, lo, [Job(pr.taken + n, moving) for n in range(KT)],
               lambda act, n, bank, done: ahead.act(act, n, evac, n + 1), add, evac, lambda n: n + 1,
               pe_wait=lambda pe, n: ahead.pe(pe, n - 3) if n >= 3 else None,
               pe_after=lambda pe: [ahead.pe(pe, n) for n in range(KT - 3, KT)], act_after=ahead.finish)


def ff_stage(pr, hi, lo, x, moving, name, gate=None, modulation=None, rstd=None, ahead=None):
    nc = pr.nc
    with ExitStack() as ctx:
        f_hi = pr.tile(name + "_f_hi", [P, 2, KT, T], F32R, ctx)
        f_lo = pr.tile(name + "_f_lo", [P, 2, KT, T], F32R, ctx)
        act_buf, sq_buf = pr.tile(name + "_relu", [P, 2, T], F32, ctx), pr.tile(name + "_sq", [P, 2, T], F32, ctx)
        relu_made, sq_made, f_hi_made, f_lo_made, added = (pr.sem(f"{name}_{k}") for k in ("relu", "sq", "hi", "lo", "added"))
        order = [(kind, g, j) for kind, g in ff_order() for j in range(8)]
        ups = [sum(k == "up" for k, _, _ in order[:n]) for n in range(len(order) + 1)]
        downs = [n - u for n, u in enumerate(ups)]
        jobs = [Job(pr.taken + n, moving if kind == "up" else
                    [(f_hi[:, g % 2, k, :], f_lo[:, g % 2, k, :]) for k in range(KT)]) for n, (kind, g, j) in enumerate(order)]
        base = pr.jobs
        last_down = {g: max(n for n, (k, gg, _) in enumerate(order) if k == "down" and gg == g) for g in range(FF_GROUPS)}

        def act_step(act, n, bank, done):
            kind, g, j = order[n]
            if kind == "up":
                u = ups[n]
                act.wait_ge(relu_made, u + 1)
                if u >= 2:
                    act.wait_ge(f_lo_made, u - 1)
                nc.scalar.activation(sq_buf[:, u % 2, :], act_buf[:, u % 2, :], ACT.Square).then_inc(sq_made, 1)
                act.wait_ge(sq_made, u + 1)
                if g >= 2:
                    act.wait_ge(pr.job_done, base + last_down[g - 2] + 1)
                nc.scalar.copy(f_hi[:, g % 2, j, :], sq_buf[:, u % 2, :]).then_inc(f_hi_made, 1)
            elif g == FF_GROUPS - 1:
                ahead.act(act, j, added, downs[n] + 1)

        def dve_step(dve, n, bank, done):
            kind, g, j = order[n]
            dve.wait_ge(pr.job_done, done)
            if kind == "up":
                u = ups[n]
                if u >= 2:
                    dve.wait_ge(sq_made, u - 1)
                if rstd is None:
                    nc.vector.tensor_scalar(act_buf[:, u % 2, :], bank, 0.0, None, ALU.max).then_inc(relu_made, 1)
                else:
                    nc.vector.scalar_tensor_tensor(act_buf[:, u % 2, :], bank, 0.0, rstd, ALU.max, ALU.mult).then_inc(relu_made, 1)
                dve.wait_ge(f_hi_made, u + 1)
                nc.vector.tensor_tensor(f_lo[:, g % 2, j, :], sq_buf[:, u % 2, :], f_hi[:, g % 2, j, :].bitcast(F32), ALU.subtract)\
                    .then_inc(f_lo_made, 1)
            else:
                if g:
                    dve.wait_ge(added, downs[n] - 7)
                if gate is None:
                    nc.vector.tensor_tensor(x[:, j, :], x[:, j, :], bank, ALU.add).then_inc(added, 1)
                else:
                    nc.vector.scalar_tensor_tensor(x[:, j, :], bank, gate(j), x[:, j, :], ALU.mult, ALU.add).then_inc(added, 1)
                if g == FF_GROUPS - 1:
                    ahead.dve(dve, j)
            if modulation is not None:
                modulation.add(dve, n)

        due = [(r + 1) * modulation.spread // MOD_PARTS + 3 for r in range(MOD_PARTS)] if modulation else []

        def pe_wait(pe, n):
            kind, g, j = order[n]
            if n >= BANKS:
                old = order[n - BANKS][0]
                if old == "up":
                    pe.wait_ge(relu_made, ups[n - BANKS] + 1)
                else:
                    pe.wait_ge(added, downs[n - BANKS] + 1)
            if kind == "down" and j == 0:
                pe.wait_ge(f_lo_made, 8 * (g + 1))
            if modulation is not None and n in due:
                modulation.reduce(pe, due.index(n))
            if n >= len(order) - 5:
                ahead.pe(pe, n - len(order) + 5)

        gemm_block(pr, hi, lo, jobs, act_step, dve_step, added, None, pe_wait=pe_wait,
                   pool_step=modulation.load if modulation else None,
                   pe_after=lambda pe: [ahead.pe(pe, n) for n in range(KT - 3, KT)], act_after=ahead.finish)


def ple_stage(pr, hi, lo, x, moving, p_raw, p_hi, p_lo, modulation, rstd, ahead):
    nc = pr.nc
    s_in, s_hi, s_lo, s_gate, s_sig, s_mul, s_add = (pr.sem("ple_" + k) for k in ("in", "hi", "lo", "gate", "sig", "mul", "add"))
    with ExitStack() as ctx:
        sig = pr.tile("ple_sig", [P, 2, T], F32, ctx)
        with nc.Block() as block:
            @block.sync
            def _(sp):
                sp.dma_start(p_raw[:, :, :], pr.dram["p"].rearrange("(k p) t -> p k t", p=P)).then_inc(s_in, 16)

            @block.scalar
            def _(act):
                act.wait_ge(s_in, 16)
                nc.scalar.copy(p_hi[:, :, :], p_raw[:, :, :]).then_inc(s_hi, 1)

            @block.vector
            def _(dve):
                dve.wait_ge(s_hi, 1)
                nc.vector.tensor_tensor(p_lo[:, :, :], p_raw[:, :, :], p_hi[:, :, :].bitcast(F32), ALU.subtract).then_inc(s_lo, 1)
                modulation.finish(dve)

        def act_step(act, n, bank, done):
            tile, j = divmod(n, 2)
            if j == 0:
                act.wait_ge(s_gate, tile + 1)
                nc.scalar.activation(sig[:, tile % 2, :], sig[:, tile % 2, :], ACT.Sigmoid).then_inc(s_sig, 1)
            else:
                ahead.act(act, tile, s_add, tile + 1)

        def dve_step(dve, n, bank, done):
            tile, j = divmod(n, 2)
            dve.wait_ge(pr.job_done, done)
            if j == 0:
                if tile >= 2:
                    dve.wait_ge(s_add, tile - 1)
                nc.vector.tensor_tensor(sig[:, tile % 2, :], bank, rstd, ALU.mult).then_inc(s_gate, 1)
            else:
                dve.wait_ge(s_sig, tile + 1)
                nc.vector.tensor_tensor(sig[:, tile % 2, :], bank, sig[:, tile % 2, :], ALU.mult).then_inc(s_mul, 1)
                dve.wait_ge(s_mul, tile + 1)
                nc.vector.tensor_tensor(x[:, tile, :], x[:, tile, :], sig[:, tile % 2, :], ALU.add).then_inc(s_add, 1)

        def pe_wait(pe, n):
            if n >= BANKS:
                tile, j = divmod(n - BANKS, 2)
                pe.wait_ge(s_mul if j else s_gate, tile + 1)
                if j:
                    ahead.pe(pe, tile)

        gemm_block(pr, hi, lo, [Job(pr.taken + n, moving if n % 2 == 0 else split_parts(p_hi, p_lo, 2)) for n in range(16)],
                   act_step, dve_step, s_add, None, pe_wait=pe_wait,
                   pe_after=lambda pe: [ahead.pe(pe, n) for n in range(KT - 2, KT)], act_after=ahead.finish)


def columns(v):
    return np.asarray(v, np.float32).reshape(-1, P).T


def weight_tiles(w):
    k, n = w.shape
    kt = min(k // P, 8)
    w = w.reshape(k // (kt * P), kt, P, n // P, P)
    return np.ascontiguousarray(w.transpose(0, 3, 2, 1, 4)).reshape(-1, P, kt * P)


def lay_out(inputs):
    a = {k: np.asarray(v) for k, v in inputs.items()}
    first = lambda k: a[k][0]
    w_in = first("w_in")
    heads = np.concatenate([np.r_[64 * i:64 * i + 64, 64 * (i + 4):64 * (i + 4) + 64] for i in range(4)])
    in2 = np.r_[0:2048, 2048 + heads, 2560:2816]
    out2 = np.r_[0:512, 512 + heads]
    dup = lambda v: np.concatenate([v, v])
    pad = lambda v: np.concatenate([v, np.zeros(64, np.float32)])
    vectors = {
        "norm_mix": first("norm_mix"), "mu_prev": first("shift_mu_prev"), "mu_next": first("shift_mu_next"),
        "w0": first("rwkv_w0").reshape(-1), "a0": first("rwkv_a0").reshape(-1), "k_k": first("rwkv_k_k"),
        "k_a": first("rwkv_k_a"), "r_k": first("rwkv_r_k").reshape(-1), "ln_w": first("rwkv_ln_w"),
        "ln_b": first("rwkv_ln_b"), "subln": first("da_subln_w"), "norm_ffn": first("norm_ffn"),
        "norm_ple": first("norm_ple"), "norm_final": a["norm_final"], "b_mod": first("b_mod_2"),
        "norm1": first("norm1_g_2"), "norm2": first("norm2_g_2"), "gn_g": first("ret_gn_g_2"),
        "q_norm": dup(first("q_norm_g_2")), "k_norm": dup(first("k_norm_g_2")), "final2": a["final_norm_g_2"],
        "c": a["c_2"][0], "c_ctx": a["c_ctx_2"],
        "lam": np.concatenate([pad(first(k)) for k in ("da_lq1", "da_lk1", "da_lq2", "da_lk2")]),
        "rate": np.repeat(first("ret_log_rate_2").reshape(-1), P),
    }
    consts = shape_constants()
    out = {
        "x": a["x"][0].T, "ctx": a["ctx_2"][0].T, "p": a["p"][0, 0].T,
        "params": np.concatenate([columns(vectors[k]) for k in PARAM_COLS], 1),
        "consts": np.concatenate([consts.pop(k) for k in ("ident", "ones", "head_ones", "head_mean", "ident64", "eps")], 1),
        "w_lora": np.concatenate([first("rwkv_w2").reshape(P, -1), first("rwkv_a2").reshape(P, -1)], 1),
        "g2": first("rwkv_g2"),
        "w_rwkv": weight_tiles(w_in[:, 0:1920]), "w_da": weight_tiles(w_in[:, 1920:3456]),
        "w_gate": weight_tiles(w_in[:, 3456:5504]), "w_mod": first("w_mod_2").reshape(KT, P, MOD_PARTS, D).transpose(2, 0, 1, 3).reshape(-1, P, D),
        "w_rwkv_o": weight_tiles(first("rwkv_w_o")), "w_da_o": weight_tiles(first("da_w_o")),
        "w_out": weight_tiles(first("w_out")), "w_ff1": weight_tiles(first("w_ff1")), "w_ff2": weight_tiles(first("w_ff2")),
        "w_ple_gate": weight_tiles(first("w_ple_gate")), "w_ple_proj": weight_tiles(first("w_ple_proj")),
        "w_in2": weight_tiles(first("w_in_2")[:, in2]), "w_out2": weight_tiles(first("w_out_2")[out2]),
        "w_ff1_2": weight_tiles(first("w_ff1_2")), "w_ff2_2": weight_tiles(first("w_ff2_2")),
        **consts,
    }
    return {k: np.ascontiguousarray(v) for k, v in out.items()}


def kernel(**inputs):
    import concourse.bacc as bacc
    from concourse.bass_utils import run_bass_kernel_spmd

    nc = bacc.Bacc("TRN2", target_bir_lowering=False, num_devices=1)
    arrays = lay_out(inputs)
    dram = {k: nc.dram_tensor(f"in_{k}", v.shape, F32, kind="ExternalInput").ap() for k, v in arrays.items()}
    out = nc.dram_tensor("out", (D, T), F32, kind="ExternalOutput").ap()
    bass_two_blocks(nc, dram, out)
    results = run_bass_kernel_spmd(nc, [{f"in_{k}": v for k, v in arrays.items()}], core_ids=[0])
    return np.ascontiguousarray(results.results[0]["out"].T)[None]
```

```python
from contextlib import ExitStack

import numpy as np

import concourse.bass as bass
from concourse import mybir

F32 = mybir.dt.float32
F32R = mybir.dt.float32r
ALU = mybir.AluOpType
ACT = mybir.ActivationFunctionType
AX_X = mybir.AxisListType.X

P = 128
D = 1024
T = 512
TC = 256
KT = D // P
TB = T // P

RW = 512
RT = RW // P
CH = 64
NCH = T // CH
R_TILES = 15
DA_HEADS = 4
FF_GROUPS = 4
RMS_EPS = 1e-6
GN_EPS = 64e-5
SUBLN_EPS = 1e-5
LAMBDA_INIT = 0.8 - 0.6
DECAY_RATE = float(np.exp(-0.5))

RET_HEADS = 4
RET_SCALE = 128 ** -0.5
ATT_TILES = 4
ATT_SCALE = 64 ** -0.5
KEYS = TC + T
CTX_T = TC // P
KEY_T = KEYS // P

PARAM_COLS = {}
_at = 0
for _name, _n in (("norm_mix", 8), ("mu_prev", 15), ("mu_next", 15), ("w0", 8), ("a0", 8), ("k_k", 4),
                  ("k_a", 4), ("r_k", 4), ("ln_w", 4), ("ln_b", 4), ("subln", 1), ("norm_ffn", 8),
                  ("norm_ple", 8), ("norm_final", 8), ("b_mod", 48), ("norm1", 8), ("norm2", 8),
                  ("gn_g", 4), ("q_norm", 1), ("k_norm", 1), ("final2", 8), ("c", 8), ("c_ctx", 8),
                  ("lam", 4), ("rate", 8)):
    PARAM_COLS[_name] = (_at, _n)
    _at += _n
N_PARAMS = _at


def rope_rotation(half):
    width = 2 * half[1]
    out = np.zeros((P, P), np.float32)
    for base in range(0, P, half[0]):
        for m in range(half[1]):
            out[base + m + half[1], base + m] = -1.0
            out[base + m, base + m + half[1]] = 1.0
    assert width <= half[0]
    return out


def shape_constants():
    f = np.float32
    i = np.arange(P)
    same_chunk = (i[:, None] // CH) == (i[None, :] // CH)
    out = {
        "ident": np.eye(P, dtype=f),
        "ones": np.ones((P, P), f),
        "head_ones": ((i[:, None] // 64) == (i[None, :] // 64)).astype(f),
        "head_mean": ((i[:, None] // 64) == (i[None, :] // 64)).astype(f) / f(64),
        "ident64": (i[:, None] % 64 == np.arange(64)[None, :]).astype(f),
        "rot_da": rope_rotation((64, 8)),
        "rot_att": rope_rotation((64, 32)),
        "rot_ret": rope_rotation((128, 64)),
    }
    t = np.arange(T)
    out["keep"] = np.concatenate([np.broadcast_to((t % CH != first).astype(f), (P, T))
                                  for first in (0, CH - 1)], 1)
    before = [i[:, None] < i[None, :], i[:, None] > i[None, :]]
    out["strict"] = np.concatenate([(b & same_chunk).astype(f) for b in before], 1)
    out["incl"] = np.concatenate([((b | (i[:, None] == i[None, :])) & same_chunk).astype(f) for b in before], 1)
    pair = (i[:, None] // 2) == (i[None, :] // 2)
    out["pair"] = np.concatenate([(b & pair).astype(f) for b in before], 1)
    levels = []
    for d in range(2):
        for s in (2, 4, 8, 16, 32):
            cols = i[(i // s) % 2 == d]
            rows = (i // s) % 2 == 1 - d
            levels.append((rows[:, None] & ((i[:, None] // (2 * s)) == (cols[None, :] // (2 * s)))).astype(f))
    out["level"] = np.concatenate(levels, 1)
    out["eps"] = np.broadcast_to(np.array([RMS_EPS, GN_EPS, SUBLN_EPS, 10 * np.log(2.0), 0.0, 1.0], f), (P, 6))

    def per_channel(cos, sin):
        return np.concatenate([np.asarray(cos, f).T, np.asarray(sin, f).T], 1)

    pos = np.arange(T, dtype=f)
    inv = f(500000.0) ** (-np.arange(0, 16, 2, dtype=f) / f(16))
    ang = pos[:, None] * inv[None, :]
    cos, sin = np.ones((T, 64), f), np.zeros((T, 64), f)
    cos[:, 0:8] = cos[:, 8:16] = np.cos(ang)
    sin[:, 0:8] = sin[:, 8:16] = np.sin(ang)
    out["rope_da"] = per_channel(np.tile(cos, (1, 2)), np.tile(sin, (1, 2)))
    fr = f(10000.0) ** (-np.arange(64, dtype=f) / f(64))
    ang = pos[:, None] * fr
    out["rope_ret"] = per_channel(np.tile(np.cos(ang), (1, 2)), np.tile(np.sin(ang), (1, 2)))
    af = f(10000.0) ** (-np.arange(16, dtype=f) / f(16))
    row, col = (t // 64).astype(f), (t % 64).astype(f)
    ang = np.concatenate([row[:, None] * af, col[:, None] * af], -1)
    out["rope_att"] = per_channel(np.tile(np.cos(ang), (1, 4)), np.tile(np.sin(ang), (1, 4)))
    rel = (np.arange(896)[None, :] - 384 - i[:, None]).astype(f)
    out["rel"] = np.concatenate([np.maximum(rel, 0), np.maximum(-rel, 0), (rel >= 0).astype(f), (rel <= 0).astype(f)], 1)
    out["steps"] = np.concatenate([np.broadcast_to(pos + 1, (P, T)), np.broadcast_to(T - pos, (P, T))], 1)
    l = i[:, None] + P * np.arange(CTX_T)[None, :]
    out["ctx_steps"] = np.concatenate([TC - 1 - l, l], 1)
    return {k: np.ascontiguousarray(v, dtype=f) for k, v in out.items()}


CONST_SHAPES = {k: v.shape for k, v in shape_constants().items()}


STREAM = ([("w_da", 0, 12, 8, True), ("w_rwkv", 0, 15, 8, True)]
          + [e for n in range(8) for e in (("w_gate", n, 1, 8, True), ("w_rwkv_o", n, 1, 4, True),
                                           ("w_gate", 8 + n, 1, 8, True), ("w_da_o", n, 1, 4, True))]
          + [("w_out", 0, 8, 8, True)])


def ff_order():
    out = [("up", 0)]
    for g in range(1, FF_GROUPS):
        out += [("up", g), ("down", g - 1)]
    return out + [("down", FF_GROUPS - 1)]


def ff_stream(up, down):
    return [(up if kind == "up" else down, 8 * g, 8, 8, True) for kind, g in ff_order()]


STREAM += ff_stream("w_ff1", "w_ff2")
STREAM += [e for n in range(8) for e in (("w_ple_gate", n, 1, 8, True), ("w_ple_proj", n, 1, 2, True))]
STREAM += [("w_in2", 0, 22, 8, True), ("w_out2", 0, 8, 8, True)]
STREAM += ff_stream("w_ff1_2", "w_ff2_2")
TILES = [(name, first + j, kt, split) for name, first, n, kt, split in STREAM for j in range(n)]
WEIGHTS = {name: (max(t for m, t, _, _ in TILES if m == name) + 1, kt) for name, _, kt, _ in TILES}

RAW_SLOTS = 4
SPLIT_SLOTS = 3
AHEAD = 2
MOD_PARTS = 6
MOD_SLOTS = 2
BANKS = 4


class Job:

    def __init__(self, weight, moving, width=T):
        self.weight, self.moving, self.width = weight, moving, width


class Program:

    def __init__(self, nc, ctx, dram):
        self.nc, self.ctx, self.dram = nc, ctx, dram
        self.pair = [ctx.enter_context(nc.psum_tensor(f"pair{i}", [P, 1024], F32)) for i in range(4)]
        self.bank = [self.pair[i // 2][:, 512 * (i % 2):512 * (i % 2) + 512] for i in range(8)]
        self.raw = self.tile("w_raw", [P, RAW_SLOTS, 1024])
        self.raw_landed = [self.sem(f"raw_landed{i}") for i in range(RAW_SLOTS)]
        self.hi_made, self.lo_made = self.sem("w_hi_made"), self.sem("w_lo_made")
        self.job_done = self.sem("job_done")
        self.norm_sems = [self.sem("norm_" + k) for k in ("sq", "sum", "log", "rstd", "y", "hi", "lo", "x")]
        self.norms = self.norms_split = self.norm_sums = self.norm_befores = 0
        self.streamed = 0
        self.taken = 0
        self.jobs = 0
        self.splits = 0
        self.split_no = {}
        self.last_job = {}
        self.split_slot = {}

    def sem(self, name):
        return self.ctx.enter_context(self.nc.semaphore(name))

    def stage_sems(self, prefix, names):
        return {k: self.nc.alloc_semaphore(name=prefix + k) for k in names}

    def release(self, sems):
        self.nc.clear_and_free_semaphores(list(sems.values()))
        self.nc.all_engine_barrier()

    def tile(self, name, shape, dtype=F32, ctx=None):
        return (ctx or self.ctx).enter_context(self.nc.sbuf_tensor(name, shape, dtype))

    def plan(self, jobs):
        self.first_job = self.jobs
        self.first_tile = self.taken
        for job in jobs:
            if job.weight not in self.last_job:
                assert job.weight == self.taken
                self.taken += 1
                if TILES[job.weight][3]:
                    self.split_slot[self.splits] = job.weight
                    self.splits += 1
                    self.split_no[job.weight] = self.splits
            self.jobs += 1
            self.last_job[job.weight] = self.jobs

    def stream(self, sp, until):
        for w in range(self.streamed, min(until, len(TILES))):
            name, tile, kt, split = TILES[w]
            old = w - RAW_SLOTS
            if old >= 0 and TILES[old][3]:
                sp.wait_ge(self.lo_made, self.split_no[old])
            elif old >= 0:
                sp.wait_ge(self.job_done, self.last_job[old])
            sp.dma_start(self.raw[:, w % RAW_SLOTS, 0:kt * P], self.dram[name][tile])\
                .then_inc(self.raw_landed[w % RAW_SLOTS], 16)
        self.streamed = max(self.streamed, min(until, len(TILES)))

    def landed(self, w):
        return self.raw_landed[w % RAW_SLOTS], 16 * (w // RAW_SLOTS + 1)


def gemm_block(pr, hi, lo, jobs, act_step, dve_step, evac_sem, evac_at, pe_wait=None,
               bank0=0, pool_step=None, pe_after=None, act_after=None):
    nc = pr.nc
    pr.plan(jobs)
    first, tiles = pr.first_job, range(pr.first_tile, pr.taken)
    of_tile = {w: [n for n, job in enumerate(jobs) if job.weight == w] for w in tiles}

    def bank(n):
        return pr.bank[bank0 + n % BANKS]

    with nc.Block() as block:
        @block.sync
        def _(sp):
            pr.stream(sp, pr.taken + RAW_SLOTS)

        @block.tensor
        def _(pe):
            for n, job in enumerate(jobs):
                w = job.weight
                kt = TILES[w][2]
                slot = (pr.split_no[w] - 1) % SPLIT_SLOTS
                if n == of_tile[w][0]:
                    pe.wait_ge(pr.lo_made, pr.split_no[w])
                if n >= BANKS and evac_at is not None:
                    pe.wait_ge(evac_sem, evac_at(n - BANKS))
                if pe_wait is not None:
                    pe_wait(pe, n)
                out = bank(n)[:, 0:job.width]
                for k in range(kt):
                    w_hi, w_lo = hi[:, slot, k * P:(k + 1) * P], lo[:, slot, k * P:(k + 1) * P]
                    x_hi, x_lo = job.moving[k]
                    nc.tensor.matmul(out, w_hi, x_hi, start=(k == 0), stop=False)
                    nc.tensor.matmul(out, w_hi, x_lo, start=False, stop=False)
                    last = nc.tensor.matmul(out, w_lo, x_hi, start=False, stop=(k == kt - 1))
                last.then_inc(pr.job_done, 1)
            if pe_after is not None:
                pe_after(pe)

        @block.gpsimd
        def _(pool):
            if pool_step is not None:
                pool_step(pool)

        @block.scalar
        def _(act):
            for i in range(len(tiles) + AHEAD):
                if i < len(tiles):
                    w = tiles[i]
                    s = pr.split_no[w] - 1
                    act.wait_ge(*pr.landed(w))
                    if s >= SPLIT_SLOTS:
                        act.wait_ge(pr.job_done, pr.last_job[pr.split_slot[s - SPLIT_SLOTS]])
                    cols = TILES[w][2] * P
                    nc.scalar.copy(hi[:, s % SPLIT_SLOTS, 0:cols], pr.raw[:, w % RAW_SLOTS, 0:cols])\
                        .then_inc(pr.hi_made, 1)
                if i >= AHEAD:
                    for n in of_tile[tiles[i - AHEAD]]:
                        act_step(act, n, bank(n), first + n + 1)
            if act_after is not None:
                act_after(act)

        @block.vector
        def _(dve):
            for i in range(len(tiles) + AHEAD):
                if i < len(tiles):
                    w = tiles[i]
                    s = pr.split_no[w] - 1
                    cols = TILES[w][2] * P
                    dve.wait_ge(*pr.landed(w))
                    dve.wait_ge(pr.hi_made, s + 1)
                    if s >= SPLIT_SLOTS:
                        dve.wait_ge(pr.job_done, pr.last_job[pr.split_slot[s - SPLIT_SLOTS]])
                    nc.vector.tensor_tensor(lo[:, s % SPLIT_SLOTS, 0:cols], pr.raw[:, w % RAW_SLOTS, 0:cols],
                                            hi[:, s % SPLIT_SLOTS, 0:cols].bitcast(F32), ALU.subtract)\
                        .then_inc(pr.lo_made, 1)
                if i >= AHEAD:
                    for n in of_tile[tiles[i - AHEAD]]:
                        dve_step(dve, n, bank(n), first + n + 1)


def copy_out(pr, evac, dest, func=ACT.Copy, scale=1.0):
    def act_step(act, n, bank, done):
        act.wait_ge(pr.job_done, done)
        out = dest(n)
        pr.nc.scalar.activation(out, bank[:, 0:out.shape[-1]], func, scale=scale(n) if callable(scale) else scale)\
            .then_inc(evac, 1)
    return act_step


def nothing(*_):
    pass


class NormAhead:

    def __init__(self, pr, sq, rstd):
        self.pr, self.sq, self.rstd, self.uses, self.splits = pr, sq, rstd, -1, 0
        self.sq_made, self.summed, self.log_made, self.rstd_made, self.hi_made, self.lo_made = (
            pr.sem("ahead_" + k) for k in ("sq", "sum", "log", "rstd", "hi", "lo"))

    def begin(self, x, gain=None, x_hi=None, x_lo=None):
        self.x, self.gain, self.x_hi, self.x_lo = x, gain, x_hi, x_lo
        self.uses += 1
        self.base = KT * self.uses
        self.split_base = KT * self.splits
        self.splits += gain is not None
        return self

    def act(self, act, tile, finished, count):
        nc, at = self.pr.nc, self.base + tile
        act.wait_ge(finished, count)
        if at >= 2:
            act.wait_ge(self.summed, at - 1)
        nc.scalar.activation(self.sq[:, tile % 2, :], self.x[:, tile, :], ACT.Square).then_inc(self.sq_made, 1)
        if self.gain is not None:
            nc.scalar.activation(self.x_hi[:, tile, :], self.x[:, tile, :], ACT.Copy, scale=self.gain(tile)).then_inc(self.hi_made, 1)

    def dve(self, dve, tile):
        if self.gain is not None:
            dve.wait_ge(self.hi_made, self.split_base + tile + 1)
            self.pr.nc.vector.scalar_tensor_tensor(self.x_lo[:, tile, :], self.x[:, tile, :], self.gain(tile),
                                                   self.x_hi[:, tile, :].bitcast(F32), ALU.mult, ALU.subtract)\
                .then_inc(self.lo_made, 1)

    def pe(self, pe, tile):
        pe.wait_ge(self.sq_made, self.base + tile + 1)
        if tile == 0 and self.uses:
            pe.wait_ge(self.log_made, self.uses)
        self.pr.nc.tensor.matmul(self.pr.bank[7], self.pr.c["ones"], self.sq[:, tile % 2, :], start=(tile == 0),
                                 stop=(tile == KT - 1)).then_inc(self.summed, 1)

    def finish(self, act):
        nc = self.pr.nc
        act.wait_ge(self.summed, self.base + KT)
        nc.scalar.activation(self.rstd[:, 0, :], self.pr.bank[7], ACT.Ln, scale=1.0 / D, bias=self.pr.eps(0)).then_inc(self.log_made, 1)
        act.wait_ge(self.log_made, self.uses + 1)
        nc.scalar.activation(self.rstd[:, 1, :], self.rstd[:, 0, :], ACT.Exp, scale=-0.5).then_inc(self.rstd_made, 1)


def norm_block(pr, scratch, x, x_hi, x_lo, gain, width=T, bias=None, out=None, known=False, before=None,
               ready=None):
    nc = pr.nc
    sq, rstd, y = scratch["sq"], scratch["rstd"], scratch["y"]
    sq_made, sum_done, log_made, rstd_made, y_made, hi_made, lo_made, x_made = pr.norm_sems
    q, q_sum, q_x = pr.norms, pr.norm_sums, pr.norm_befores
    split = pr.norms_split
    pr.norms += 1
    pr.norm_sums += not known
    pr.norm_befores += before is not None
    pr.norms_split += out is None
    total = pr.bank[7][:, 0:width]
    with nc.Block() as block:
        @block.sync
        def _(sp):
            pr.stream(sp, pr.taken + RAW_SLOTS)

        @block.tensor
        def _(pe):
            if not known:
                for k in range(KT):
                    pe.wait_ge(sq_made, KT * q_sum + k + 1)
                    last = nc.tensor.matmul(total, pr.c["ones"], sq[:, k, 0:width], start=(k == 0), stop=(k == KT - 1))
                last.then_inc(sum_done, 1)

        @block.scalar
        def _(act):
            if not known:
                for k in range(KT):
                    if ready:
                        ready(act, k)
                    if before:
                        act.wait_ge(x_made, KT * q_x + k + 1)
                    nc.scalar.activation(sq[:, k, 0:width], x(k), ACT.Square).then_inc(sq_made, 1)
                act.wait_ge(sum_done, q_sum + 1)
                nc.scalar.activation(rstd[:, 0, 0:width], total, ACT.Ln, scale=1.0 / D, bias=pr.eps(0)).then_inc(log_made, 1)
                act.wait_ge(log_made, q_sum + 1)
                nc.scalar.activation(rstd[:, 1, 0:width], rstd[:, 0, 0:width], ACT.Exp, scale=-0.5).then_inc(rstd_made, 1)
            if out is None:
                for k in range(KT):
                    act.wait_ge(y_made, KT * q + k + 1)
                    nc.scalar.activation(x_hi[:, k, 0:width], y[:, k, 0:width], ACT.Identity,
                                         bias=bias(k) if bias else pr.eps(4)).then_inc(hi_made, 1)

        @block.vector
        def _(dve):
            if before:
                for k in range(KT):
                    nc.vector.scalar_tensor_tensor(x(k), x(k), before[0](k), before[1], ALU.mult, ALU.mult).then_inc(x_made, 1)
            if not known:
                dve.wait_ge(rstd_made, q_sum + 1)
            for k in range(KT + 1):
                if k < KT:
                    if ready:
                        ready(dve, k)
                    nc.vector.scalar_tensor_tensor(y[:, k, 0:width] if out is None else out(k), x(k), gain(k),
                                                   rstd[:, 1, 0:width], ALU.mult, ALU.mult).then_inc(y_made, 1)
                if k >= 1 and out is None:
                    dve.wait_ge(y_made, KT * q + k)
                    dve.wait_ge(hi_made, KT * split + k)
                    nc.vector.scalar_tensor_tensor(x_lo[:, k - 1, 0:width], y[:, k - 1, 0:width],
                                                   bias(k - 1) if bias else 0.0,
                                                   x_hi[:, k - 1, 0:width].bitcast(F32), ALU.add, ALU.subtract)\
                        .then_inc(lo_made, 1)


def split_parts(x_hi, x_lo, n):
    return [(x_hi[:, k, :], x_lo[:, k, :]) for k in range(n)]


def da_attention_block(pr, U, room, out_hi, out_lo):
    nc, c = pr.nc, pr.c
    with ExitStack() as ctx:
        t = lambda name, shape, dtype=F32: pr.tile("da_" + name, shape, dtype, ctx)
        table, turned, rot_sb = room[:, 4:6, :], room[:, 6:8, :], t("rot", [P, P])
        vN = room[:, 0:4, :]
        prob = room[:, 8:12, :].rearrange("p (a b) t -> p a b t", a=2)
        probT = t("probT", [P, 2, TB, T])
        oT = t("oT", [P, 4, T])
        small = t("small", [P, 2, 8])
        lam = t("lam", [P, 8])
        s = pr.stage_sems("da_", ("table_in", "rot_done", "sin_made", "cos_made", "roped", "v_done", "v_out", "score", "negmax",
              "exp", "inv", "scaled", "diff", "tr_done", "tr_out", "pv_done", "o_out", "lam_in", "lam_sum",
              "lam_exp", "lam_made", "sq", "sum", "log", "rstd", "y", "hi", "lo"))
        units = [(h, q) for h in range(DA_HEADS) for q in range(TB)]
        with nc.Block() as block:
            @block.sync
            def _(sp):
                sp.dma_start(table[:, :, :], pr.dram["rope_da"].rearrange("p (a t) -> p a t", a=2))\
                    .then_inc(s["table_in"], 16)
                sp.dma_start(rot_sb[:, :], pr.dram["rot_da"]).then_inc(s["table_in"], 16)
                pr.stream(sp, pr.taken + RAW_SLOTS)

            @block.tensor
            def _(pe):
                pe.wait_ge(s["table_in"], 32)
                for i in range(8):
                    if i >= 2:
                        pe.wait_ge(s["sin_made"], i - 1)
                    nc.tensor.matmul(pr.bank[i % 2], rot_sb[:, :], U[:, i, :], start=True, stop=True)\
                        .then_inc(s["rot_done"], 1)
                for b in range(TB):
                    if b >= 2:
                        pe.wait_ge(s["v_out"], b - 1)
                    for j in range(4):
                        last = nc.tensor.transpose(pr.bank[2 + b % 2][:, j * P:(j + 1) * P],
                                                   U[:, 8 + j, b * P:(b + 1) * P], c["ident"])
                    last.then_inc(s["v_done"], 1)
                pe.wait_ge(s["lam_in"], 2)
                nc.tensor.matmul(pr.bank[4][:, 0:2], c["ones"], lam[:, 0:2], start=True, stop=True)\
                    .then_inc(s["lam_sum"], 1)
                pe.wait_ge(s["roped"], 8)
                pe.wait_ge(s["v_out"], TB)
                pe.wait_ge(s["lam_exp"], 1)
                for i in range(len(units) + 2):
                    if i < len(units):
                        h, q = units[i]
                        if i >= 2:
                            pe.wait_ge(s["exp"], 2 * (i - 1))
                        for m in range(2):
                            last = nc.tensor.matmul(pr.bank[2 * (i % 2) + m],
                                                    U[64 * m:64 * m + 64, h, q * P:(q + 1) * P],
                                                    U[64 * m:64 * m + 64, 4 + h, :], start=True, stop=True)
                        last.then_inc(s["score"], 1)
                    if i >= 2:
                        j = i - 2
                        h, q = units[j]
                        pe.wait_ge(s["diff"], j + 1)
                        if j >= 2:
                            pe.wait_ge(s["tr_out"], j - 1)
                        for k in range(TB):
                            last = nc.tensor.transpose(pr.bank[4 + j % 2][:, k * P:(k + 1) * P],
                                                       prob[:, j % 2, 0, k * P:(k + 1) * P], c["ident"])
                        last.then_inc(s["tr_done"], 1)
                        if q == TB - 1:
                            pe.wait_ge(s["tr_out"], j + 1)
                            if h >= 2:
                                pe.wait_ge(s["o_out"], h - 1)
                            for k in range(TB):
                                last = nc.tensor.matmul(pr.bank[6 + h % 2], vN[:, k, h * P:(h + 1) * P],
                                                        probT[:, h % 2, k, :], start=(k == 0), stop=(k == TB - 1))
                            last.then_inc(s["pv_done"], 1)
                for h in range(DA_HEADS):
                    pe.wait_ge(s["sq"], h + 1)
                    nc.tensor.matmul(pr.bank[h], c["ones"], room[:, 4 + h, :], start=True, stop=True)\
                        .then_inc(s["sum"], 1)

            @block.scalar
            def _(act):
                for b in range(TB):
                    act.wait_ge(s["v_done"], b + 1)
                    nc.scalar.copy(vN[:, b, :], pr.bank[2 + b % 2]).then_inc(s["v_out"], 1)
                act.wait_ge(s["lam_sum"], 1)
                nc.scalar.activation(lam[:, 2:4], pr.bank[4][:, 0:2], ACT.Exp).then_inc(s["lam_exp"], 1)
                for i in range(len(units) + 2):
                    if i < len(units):
                        for m in range(2):
                            act.wait_ge(s["negmax"], 2 * i + m + 1)
                            if i >= 2:
                                act.wait_ge(s["tr_done"], i - 1)
                            nc.scalar.activation(prob[:, i % 2, m, :], pr.bank[2 * (i % 2) + m], ACT.Exp,
                                                 bias=small[:, i % 2, m:m + 1],
                                                 accum_out=small[:, i % 2, 2 + m:3 + m]).then_inc(s["exp"], 1)
                    if i >= 2:
                        j = i - 2
                        h, q = units[j]
                        act.wait_ge(s["tr_done"], j + 1)
                        if h >= 2:
                            act.wait_ge(s["pv_done"], h - 1)
                        nc.scalar.copy(probT[:, h % 2, :, q * P:(q + 1) * P],
                                       pr.bank[4 + j % 2].rearrange("p (k t) -> p k t", k=TB)).then_inc(s["tr_out"], 1)
                        if q == TB - 1:
                            act.wait_ge(s["pv_done"], h + 1)
                            nc.scalar.copy(oT[:, h, :], pr.bank[6 + h % 2]).then_inc(s["o_out"], 1)
                for h in range(DA_HEADS):
                    act.wait_ge(s["o_out"], h + 1)
                    nc.scalar.activation(room[:, 4 + h, :], oT[:, h, :], ACT.Square).then_inc(s["sq"], 1)
                for h in range(DA_HEADS):
                    act.wait_ge(s["sum"], h + 1)
                    nc.scalar.activation(prob[:, h // 2, h % 2, :], pr.bank[h], ACT.Ln, scale=1.0 / P, bias=pr.eps(2))\
                        .then_inc(s["log"], 1)
                for h in range(DA_HEADS):
                    act.wait_ge(s["log"], h + 1)
                    nc.scalar.activation(prob[:, h // 2, h % 2, :], prob[:, h // 2, h % 2, :], ACT.Exp, scale=-0.5)\
                        .then_inc(s["rstd"], 1)
                for h in range(DA_HEADS):
                    act.wait_ge(s["y"], h + 1)
                    nc.scalar.copy(out_hi[:, h, :], oT[:, h, :]).then_inc(s["hi"], 1)

            @block.vector
            def _(dve):
                dve.wait_ge(s["table_in"], 32)
                for i in range(8):
                    dve.wait_ge(s["rot_done"], i + 1)
                    if i >= 2:
                        dve.wait_ge(s["roped"], i - 1)
                    nc.vector.tensor_tensor(turned[:, i % 2, :], pr.bank[i % 2], table[:, 1, :], ALU.mult)\
                        .then_inc(s["sin_made"], 1)
                    nc.vector.tensor_tensor(U[:, i, :], U[:, i, :], table[:, 0, :], ALU.mult)\
                        .then_inc(s["cos_made"], 1)
                    dve.wait_ge(s["sin_made"], i + 1)
                    dve.wait_ge(s["cos_made"], i + 1)
                    nc.vector.tensor_tensor(U[:, i, :], U[:, i, :], turned[:, i % 2, :], ALU.add)\
                        .then_inc(s["roped"], 1)
                lp = pr.param("lam")
                for m in range(2):
                    nc.vector.tensor_tensor(lam[:, m:m + 1], lp(2 * m), lp(2 * m + 1), ALU.mult).then_inc(s["lam_in"], 1)
                dve.wait_ge(s["lam_exp"], 1)
                nc.vector.tensor_tensor(lam[:, 4:5], lam[:, 3:4], lam[:, 2:3], ALU.subtract).then_inc(s["lam_made"], 1)
                dve.wait_ge(s["lam_made"], 1)
                nc.vector.tensor_scalar_add(lam[:, 5:6], lam[:, 4:5], -LAMBDA_INIT).then_inc(s["lam_made"], 1)
                dve.wait_ge(s["lam_made"], 2)

                for i in range(len(units) + 1):
                    if i < len(units):
                        dve.wait_ge(s["score"], i + 1)
                        if i >= 2:
                            dve.wait_ge(s["diff"], i - 1)
                        for m in range(2):
                            nc.vector.tensor_reduce(small[:, i % 2, m:m + 1], pr.bank[2 * (i % 2) + m], AX_X,
                                                    ALU.max, negate=True).then_inc(s["negmax"], 1)
                    if i >= 1:
                        j = i - 1
                        w = small[:, j % 2, :]
                        dve.wait_ge(s["exp"], 2 * j + 2)
                        nc.vector.reciprocal(w[:, 4:6], w[:, 2:4]).then_inc(s["inv"], 1)
                        dve.wait_ge(s["inv"], 2 * j + 1)
                        nc.vector.tensor_tensor(w[:, 6:7], w[:, 5:6], lam[:, 5:6], ALU.mult).then_inc(s["inv"], 1)
                        nc.vector.tensor_scalar(prob[:, j % 2, 0, :], prob[:, j % 2, 0, :], w[:, 4:5], None, ALU.mult)\
                            .then_inc(s["scaled"], 1)
                        dve.wait_ge(s["inv"], 2 * j + 2)
                        dve.wait_ge(s["scaled"], j + 1)
                        nc.vector.scalar_tensor_tensor(prob[:, j % 2, 0, :], prob[:, j % 2, 1, :], w[:, 6:7],
                                                       prob[:, j % 2, 0, :], ALU.mult, ALU.add).then_inc(s["diff"], 1)
                for h in range(DA_HEADS):
                    dve.wait_ge(s["rstd"], h + 1)
                    nc.vector.scalar_tensor_tensor(oT[:, h, :], oT[:, h, :], pr.c["subln_scaled"],
                                                   prob[:, h // 2, h % 2, :], ALU.mult, ALU.mult).then_inc(s["y"], 1)
                for h in range(DA_HEADS):
                    dve.wait_ge(s["hi"], h + 1)
                    nc.vector.tensor_tensor(out_lo[:, h, :], oT[:, h, :], out_hi[:, h, :].bitcast(F32), ALU.subtract)\
                        .then_inc(s["lo"], 1)
        pr.release(s)


def rwkv_block(pr, U, w_lora, room):
    nc, c = pr.nc, pr.c
    L_KINDS = ("L", "A1", "M", "A2")
    with ExitStack() as ctx:
        t = lambda name, shape: pr.tile("rw_" + name, shape, F32, ctx)
        keep, strict, incl, pair = (t(k, [P, 2, w]) for k, w in (("keep", T), ("strict", P), ("incl", P), ("pair", P)))
        level = t("level", [P, 10, 64])
        kkr, kk, ks, rinv = t("kkr", [P, T]), t("kk", [P, T]), t("ks", [P, T]), t("rinv", [P, T])
        v_tokens = t("vN", [P, 2, TB, P])
        dirs = []
        for d in range(2):
            td = lambda name, shape: t(f"{name}{d}", shape)
            right = td("right", [P, 8, P])
            scr, kb, kh, rt = td("scr", [P, 4 * T]), td("kb", [P, 2, 2, T]), td("kh", [P, 2, T]), td("rt", [P, 2, T])
            pin = td("pin", [P, 2, NCH, CH + 1])
            mats = {k: td("m" + k, [P, 8, P]) for k in L_KINDS}
            fixed = dict(
                cum=room[:, 4 * d, :], sg=room[:, 4 * d + 1, :], aa=room[:, 4 * d + 2, :], pinv=room[:, 4 * d + 3, :],
                X=scr[:, 0:1024].rearrange("p (q t) -> p q t", q=8), Y=scr[:, 1024:2048].rearrange("p (q t) -> p q t", q=8),
                R=right, M1=right[:, :, 0:64], BhN=td("bhn", [P, TB, P]), KhN=td("khn", [P, TB, P]),
                mats=mats, Phi=mats["L"], Z=mats["M"])
            dirs.append([dict(fixed, pin=pin[:, j], Kt=kb[:, j, 0, :], Bh=kb[:, j, 1, :], Kh=kh[:, j, :], Rb=kh[:, j, :],
                              Rt=rt[:, j, :], N=kb[:, j, :, :].rearrange("p a (q t) -> p (a q) t", t=P)) for j in range(2)])
        both = lambda p: [(d, dirs[d][p % 2]) for d in range(2)]
        STEPS = 18
        Y_BANKS = (6, 7, 0, 1)
        TR_BANKS = (0, 1, 6, 7, 0, 1)
        GRAMS = [("L", "Bh", "Kt"), ("M", "Kh", "Kt"), ("A1", "Bh", "Rt"), ("A2", "Kh", "Rt")]
        names = ("const", "kkr", "kksq", "kksum", "kkmax", "kklog", "rinv", "kk", "lora", "sig", "ones", "prep", "cum", "bk", "exps",
                 "vtr", "vout", "tr", "trout", "gram", "mask", "ybegin", "y0", "xtr", "xout", "m1", "m1out", "px", "xsub",
                 "ytr", "yout", "mv", "mvout", "n", "nout", "phizero", "zzero", "phi", "phiout", "psi", "psiout",
                 "rb", "rbout", "step", "zout", "y", "yo", "ksum", "bonus", "bsum", "bout", "scaled")
        s = pr.stage_sems("rw_", names)

        def ex(a, d):
            return a["pin"][:, :, d:d + CH]

        def inc(a, d):
            return a["pin"][:, :, 1 - d:1 - d + CH]

        def chunks(x):
            return x.rearrange("p (n t) -> p n t", n=NCH)

        def half_cols(x, lev, d):
            return x.rearrange("p q (n two w) -> p q n two w", two=2, w=2 ** lev)[:, :, :, d, :]

        ORDER = [list(range(NCH)), list(range(NCH))[::-1]]
        heads = [(hh, b) for hh in range(2) for b in range(TB)]

        with nc.Block() as block:
            @block.sync
            def _(sp):
                for dst, key in ((keep, "keep"), (strict, "strict"), (incl, "incl"), (pair, "pair")):
                    sp.dma_start(dst[:, :, :], pr.dram[key].rearrange("p (a t) -> p a t", a=2)).then_inc(s["const"], 16)
                sp.dma_start(level[:, :, :], pr.dram["level"].rearrange("p (a t) -> p a t", a=10)).then_inc(s["const"], 16)
                pr.stream(sp, pr.taken + RAW_SLOTS)

            @block.gpsimd
            def _(pool):
                for p in range(RT):
                    for d, a in both(p):
                        pool.wait_ge(s["mv"], 2 * p + d + 1)
                        for hh in range(2):
                            nc.gpsimd.memset(a["Phi"][64 * hh:64 * hh + 64, :, 64 - 64 * hh:128 - 64 * hh], 0.0)\
                                .then_inc(s["phizero"], 1)
                            nc.gpsimd.memset(a["Z"][64 * hh:64 * hh + 64, :, 64 - 64 * hh:128 - 64 * hh], 0.0)\
                                .then_inc(s["zzero"], 1)
                            nc.gpsimd.memset(a["Z"][64 * hh:64 * hh + 64, ORDER[d][0], 64 * hh:64 * hh + 64], 0.0)\
                                .then_inc(s["zzero"], 1)

            @block.tensor
            def _(pe):
                def gram(p, n):
                    d, (key, left, right) = n % 2, GRAMS[n // 2]
                    a = dirs[d][p % 2]
                    out = pr.pair[2 - d] if key == "L" else pr.pair[1]
                    for hh, b in heads:
                        rows, cols, q = slice(64 * hh, 64 * hh + 64), slice(b * P, (b + 1) * P), hh * TB + b
                        last = nc.tensor.matmul(out[:, q * P:(q + 1) * P], a[left][rows, cols], a[right][rows, cols],
                                                start=True, stop=True)
                    last.then_inc(s["gram"], 1)

                def prepare(p, n):
                    if n == 0:
                        nc.tensor.matmul(pr.bank[3], w_lora[0:64, 0, p * P:(p + 1) * P], U[0:64, 12, :],
                                         start=True, stop=True).then_inc(s["lora"], 1)
                    elif n == 1:
                        pe.wait_ge(s["kksq"], p + 1)
                        nc.tensor.matmul(pr.bank[2], c["head_ones"], kk[:, :], start=True, stop=True).then_inc(s["kksum"], 1)
                    elif n == 2:
                        pe.wait_ge(s["sig"], 4 * p + 1)
                        nc.tensor.matmul(pr.bank[3], w_lora[0:64, 1, p * P:(p + 1) * P], U[0:64, 13, :],
                                         start=True, stop=True).then_inc(s["lora"], 1)
                    elif n == 3:
                        pe.wait_ge(s["kkmax"], p + 1)
                        nc.tensor.matmul(pr.bank[2], w_lora[64:128, 0, p * P:(p + 1) * P], U[64:128, 12, :],
                                         start=True, stop=True).then_inc(s["lora"], 1)
                    elif n == 4:
                        pe.wait_ge(s["sig"], 4 * p + 2)
                        nc.tensor.matmul(pr.bank[3], w_lora[64:128, 1, p * P:(p + 1) * P], U[64:128, 13, :],
                                         start=True, stop=True).then_inc(s["lora"], 1)
                    elif n == 5:
                        pe.wait_ge(s["sig"], 4 * p + 3)
                        for b in range(TB):
                            last = nc.tensor.transpose(pr.bank[2][:, b * P:(b + 1) * P], U[:, 8 + p, b * P:(b + 1) * P], c["ident"])
                        last.then_inc(s["vtr"], 1)
                    elif n == 16:
                        pe.wait_ge(s["vout"], p + 1)
                        pe.wait_ge(s["bonus"], p + 1)
                        nc.tensor.matmul(pr.bank[2], c["head_ones"], ks[:, :], start=True, stop=True).then_inc(s["bsum"], 1)

                def beside(p, n):
                    if 6 <= n < 12:
                        if n == 6 and p + 1 < RT:
                            pe.wait_ge(s["vout"], p + 2)
                            pe.wait_ge(s["sig"], 4 * p + 8)
                        elif n > 6:
                            pe.wait_ge(s["mask"], 8 * p + n - 4)
                        gram(p, n - 4)
                    elif p + 1 < RT:
                        prepare(p + 1, n)

                for n in range(STEPS):
                    prepare(0, n)
                for p in range(RT):
                    if p:
                        pe.wait_ge(s["zout"], 14 * p)
                    pe.wait_ge(s["scaled"], 8 * (p + 1))
                    gram(p, 0)
                    pe.wait_ge(s["bout"], p + 1)
                    gram(p, 1)
                    if p:
                        pe.wait_ge(s["yo"], 2 * p)
                    for d, a in both(p):
                        for j, key in enumerate(("Kt", "Bh", "Kh")):
                            i = 3 * d + j
                            if i >= 4:
                                pe.wait_ge(s["trout"], 6 * p + i - 3)
                            for b in range(TB):
                                last = nc.tensor.transpose(pr.bank[TR_BANKS[i]][:, b * P:(b + 1) * P],
                                                           a[key][:, b * P:(b + 1) * P], c["ident"])
                            last.then_inc(s["tr"], 1)
                    pe.wait_ge(s["trout"], 6 * (p + 1))
                    for d, a in both(p):
                        pe.wait_ge(s["y0"], 2 * p + d + 1)
                        for q in range(8):
                            last = nc.tensor.transpose(pr.pair[2 + d][:, q * P:(q + 1) * P], a["Y"][:, q, :], c["ident"])
                        last.then_inc(s["xtr"], 1)
                    pe.wait_ge(s["xout"], 2 * p + 2)
                    pe.wait_ge(s["mask"], 8 * p + 2)
                    for lev in range(1, 6):
                        u = 5 * p + lev - 1
                        for d, a in both(p):
                            for q in range(8):
                                last = nc.tensor.matmul(pr.bank[d][:, q * 64:(q + 1) * 64], a["mats"]["L"][:, q, :],
                                                        half_cols(a["X"], lev, d)[:, q], start=True, stop=True)
                            last.then_inc(s["m1"], 1)
                        beside(p, 3 * lev - 3)
                        for d, a in both(p):
                            pe.wait_ge(s["m1out"], 2 * u + d + 1)
                            if lev > 1:
                                pe.wait_ge(s["yout"], 2 * (u - 1) + d + 1)
                            for q in range(8):
                                last = nc.tensor.matmul(pr.bank[d][:, q * 64:(q + 1) * 64], a["Y"][:, q, :],
                                                        a["M1"][:, q, :], start=True, stop=True)
                            last.then_inc(s["px"], 1)
                        beside(p, 3 * lev - 2)
                        for d, a in both(p):
                            pe.wait_ge(s["xsub"], 2 * u + d + 1)
                            for q in range(8):
                                last = nc.tensor.transpose(pr.pair[2 + d][:, q * P:(q + 1) * P], a["X"][:, q, :], c["ident"])
                            last.then_inc(s["ytr"], 1)
                        beside(p, 3 * lev - 1)
                    vN = v_tokens[:, p % 2]
                    pe.wait_ge(s["mask"], 8 * (p + 1))
                    for d, a in both(p):
                        for hh, b in heads:
                            q = hh * TB + b
                            last = nc.tensor.matmul(pr.bank[d][:, q * 64:(q + 1) * 64], a["mats"]["M"][:, q, :],
                                                    vN[:, b, 64 * hh:64 * hh + 64], start=True, stop=True)
                        last.then_inc(s["mv"], 1)
                    for d, a in both(p):
                        pe.wait_ge(s["mvout"], 2 * p + d + 1)
                        pe.wait_ge(s["yout"], 2 * (5 * p + 4) + d + 1)
                        for hh, b in heads:
                            q = hh * TB + b
                            out = pr.pair[1 + d][:, q * P:(q + 1) * P]
                            last = nc.tensor.matmul(out, a["Y"][:, q, :], a["R"][:, q, :], start=True, stop=True)
                        last.then_inc(s["n"], 1)
                    for d, a in both(p):
                        pe.wait_ge(s["nout"], 2 * p + d + 1)
                        if d == 1:
                            pe.wait_ge(s["phiout"], 2 * (2 * p) + 2)
                        for cc in range(2):
                            r = slice(64 * cc, 64 * cc + 64)
                            for hh, b in heads:
                                last = nc.tensor.matmul(pr.pair[0][64 * hh:64 * hh + 64, 512 * cc + 64 * b:512 * cc + 64 * b + 64],
                                                        a["N"][r, hh * TB + b, 64:128], a["BhN"][r, b, 64 * hh:64 * hh + 64],
                                                        start=True, stop=True)
                        last.then_inc(s["phi"], 1)
                        if d == 1:
                            pe.wait_ge(s["psiout"], 4 * (2 * p) + 4)
                        for cc in range(2):
                            r = slice(64 * cc, 64 * cc + 64)
                            for hh, b in heads:
                                h = slice(64 * hh, 64 * hh + 64)
                                out = pr.pair[3][h, 512 * cc + 64 * b:512 * cc + 64 * b + 64]
                                nc.tensor.matmul(out, a["KhN"][r, b, h], vN[r, b, h], start=True, stop=False)
                                last = nc.tensor.matmul(out, a["BhN"][r, b, h], a["N"][r, hh * TB + b, 0:64],
                                                        start=False, stop=True)
                        last.then_inc(s["psi"], 1)
                        for hh, b in heads:
                            last = nc.tensor.matmul(pr.bank[2 + d][64 * hh:64 * hh + 64, b * P:(b + 1) * P],
                                                    a["N"][:, hh * TB + b, 64:128], a["mats"]["A1"][:, hh * TB + b, :],
                                                    start=True, stop=True)
                        last.then_inc(s["rb"], 1)
                    pe.wait_ge(s["phiout"], 4 * (p + 1))
                    pe.wait_ge(s["psiout"], 8 * (p + 1))
                    fixed_parts = [(b, hh, d, a, k) for b in range(TB) for hh in range(2) for d, a in both(p) for k in range(2)]
                    for i in range(NCH - 1):
                        for d, a in both(p):
                            at = ORDER[d][i]
                            if i == 0:
                                pe.wait_ge(s["phizero"], 2 * (2 * p + d + 1))
                                pe.wait_ge(s["zzero"], 4 * (2 * p + d + 1))
                            else:
                                pe.wait_ge(s["zout"], 14 * p + 2 * (i - 1) + d + 1)
                            out = pr.bank[4 + d][:, (i % 4) * P:(i % 4 + 1) * P]
                            nc.tensor.matmul(out, a["Phi"][:, 4 * (at % 2) + at // 2, :], a["Z"][:, at, :],
                                             start=True, stop=True).then_inc(s["step"], 1)
                        for b, hh, d, a, k in fixed_parts[5 * i:5 * (i + 1)]:
                            q, h = hh * TB + b, slice(64 * hh, 64 * hh + 64)
                            left, right = ((vN[:, b, h], a["mats"]["A2"]), (a["N"][:, q, 0:64], a["mats"]["A1"]))[k]
                            nc.tensor.matmul(pr.bank[Y_BANKS[b]][h, 0:P], left, right[:, q, :],
                                             start=(d == 0 and k == 0), stop=False, skip_group_check=True)
                    pe.wait_ge(s["rbout"], 2 * p + 2)
                    if p + 1 < RT:
                        prepare(p + 1, 16)
                    pe.wait_ge(s["zout"], 14 * p + 14)
                    for b in range(TB):
                        for d, a in both(p):
                            for cc in range(2):
                                last = nc.tensor.matmul(pr.bank[Y_BANKS[b]][:, 64 * cc:64 * cc + 64], a["Z"][:, 2 * b + cc, :],
                                                        a["Rb"][:, (2 * b + cc) * CH:(2 * b + cc + 1) * CH],
                                                        start=False, stop=(d == 1), skip_group_check=True)
                    last.then_inc(s["y"], 1)

            @block.scalar
            def _(act):
                def sigmoid(p, n):
                    d, m = divmod(n, 2)
                    key, prm = (("sg", "w0"), ("aa", "a0"))[m]
                    act.wait_ge(s["lora"], 4 * p + n + 1)
                    if p:
                        act.wait_ge(s["scaled"], 8 * p)
                        act.wait_ge(s["ksum"], p)
                    nc.scalar.activation(dirs[d][0][key], pr.bank[2 if n == 2 else 3], ACT.Sigmoid, bias=pr.param(prm)(4 * d + p))\
                        .then_inc(s["sig"], 1)

                def prepare(p, n):
                    if n == 0:
                        act.wait_ge(s["kkr"], p + 1)
                        if p:
                            act.wait_ge(s["scaled"], 8 * p)
                        nc.scalar.activation(kk[:, :], kkr[:, :], ACT.Square).then_inc(s["kksq"], 1)
                        sigmoid(p, 0)
                    elif n in (2, 3, 4):
                        sigmoid(p, n - 1)
                    elif n == 5:
                        act.wait_ge(s["vtr"], p + 1)
                        if p >= 2:
                            act.wait_ge(s["y"], p - 1)
                        nc.scalar.copy(v_tokens[:, p % 2], pr.bank[2].rearrange("p (b t) -> p b t", b=TB)).then_inc(s["vout"], 1)
                    elif n == 6:
                        act.wait_ge(s["kkmax"], p + 1)
                        nc.scalar.activation(rinv[:, :], rinv[:, :], ACT.Ln, scale=2.0 ** 20).then_inc(s["kklog"], 1)
                    elif n == 9:
                        act.wait_ge(s["kklog"], p + 1)
                        nc.scalar.activation(rinv[:, :], rinv[:, :], ACT.Exp, scale=-0.5, bias=pr.eps(3)).then_inc(s["rinv"], 1)
                    elif n in (10, 12):
                        d, a = both(p)[n // 12]
                        act.wait_ge(s["cum"], 2 * p + d + 1)
                        if p >= 2:
                            act.wait_ge(s["zout"], 14 * (p - 1))
                            act.wait_ge(s["psiout"], 8 * (p - 1))
                        if p:
                            act.wait_ge(s["scaled"], 8 * p)
                        nc.scalar.activation(inc(a, d), chunks(a["cum"]), ACT.Exp, scale=-DECAY_RATE).then_inc(s["exps"], 1)
                        nc.scalar.activation(a["pinv"], a["cum"], ACT.Exp, scale=DECAY_RATE).then_inc(s["exps"], 1)

                for n in range(STEPS):
                    prepare(0, n)
                for p in range(RT):
                    if p:
                        act.wait_ge(s["y"], p)
                    for d, a in both(p):
                        for j, key in enumerate(("KtN", "BhN", "KhN")):
                            act.wait_ge(s["tr"], 6 * p + 3 * d + j + 1)
                            bank = pr.bank[TR_BANKS[3 * d + j]]
                            if key == "KtN":
                                dst, src = a["R"].rearrange("p (hh b) t -> p hh b t", hh=2)[:, :, :, 64:128],\
                                    bank.rearrange("p (b hh t) -> p hh b t", b=TB, hh=2)
                            else:
                                dst, src = a[key][:, :, :], bank.rearrange("p (b t) -> p b t", b=TB)
                            nc.scalar.copy(dst, src).then_inc(s["trout"], 1)
                    for d, a in both(p):
                        act.wait_ge(s["xtr"], 2 * p + d + 1)
                        nc.scalar.copy(a["X"], pr.pair[2 + d][:, :].rearrange("p (q t) -> p q t", q=8)).then_inc(s["xout"], 1)
                    for lev in range(1, 6):
                        u = 5 * p + lev - 1
                        for n in range(3 * lev - 3, 3 * lev):
                            if n % 3 == 2:
                                for d, a in both(p):
                                    act.wait_ge(s["ytr"], 2 * u + d + 1)
                                    nc.scalar.copy(a["Y"], pr.pair[2 + d][:, :].rearrange("p (q t) -> p q t", q=8))\
                                        .then_inc(s["yout"], 1)
                            if p + 1 < RT:
                                prepare(p + 1, n)
                    for d, a in both(p):
                        act.wait_ge(s["mv"], 2 * p + d + 1)
                        nc.scalar.copy(a["M1"], pr.bank[d].rearrange("p (q t) -> p q t", q=8)).then_inc(s["mvout"], 1)
                    for d, a in both(p):
                        act.wait_ge(s["n"], 2 * p + d + 1)
                        act.wait_ge(s["gram"], 8 * (p + 1))
                        nc.scalar.mul(a["N"], pr.pair[1 + d][:, :].rearrange("p (q t) -> p q t", q=8), -1.0).then_inc(s["nout"], 1)
                    act.wait_ge(s["y"], p + 1)
                    for j in range(2):
                        nc.scalar.copy(U[:, p, 256 * j:256 * j + 256].rearrange("p (b t) -> p b t", b=2),
                                       pr.pair[3 - 3 * j][:, :].rearrange("p (b t) -> p b t", b=2)[:, :, 0:P]).then_inc(s["yo"], 1)

            @block.vector
            def _(dve):
                def back(d):
                    return slice(None, None, -1) if d else slice(None)

                def prepare(p, n):
                    r, k, v = (U[:, 4 * j + p, :] for j in range(3))
                    (_, a0), (_, a1) = both(p)
                    if n == 0:
                        if p:
                            dve.wait_ge(s["kk"], p)
                            dve.wait_ge(s["kksq"], p)
                        nc.vector.tensor_scalar(kkr[:, :], k, pr.param("k_k")(p), None, ALU.mult).then_inc(s["kkr"], 1)
                    elif n == 2:
                        dve.wait_ge(s["kksum"], p + 1)
                        nc.vector.tensor_scalar(rinv[:, :], pr.bank[2], 1e-24, None, ALU.max).then_inc(s["kkmax"], 1)
                    elif n in (3, 5):
                        d = (n - 3) // 2
                        a = (a0, a1)[d]
                        dve.wait_ge(s["sig"], 4 * p + 2 * d + 1)
                        if p:
                            dve.wait_ge(s["exps"], 4 * p)
                        nc.vector.tensor_tensor_scan(a["cum"][:, back(d)], keep[:, d, back(d)], a["sg"][:, back(d)], 0.0,
                                                     ALU.mult, ALU.add).then_inc(s["cum"], 1)
                    elif n in (4, 12):
                        d = n // 12
                        a = (a0, a1)[d]
                        dve.wait_ge(s["cum"], 2 * p + d + 1)
                        dve.wait_ge(s["sig"], 4 * p + 2 * d + 2)
                        nc.vector.tensor_scalar(a["sg"], a["aa"], pr.param("k_a")(p), pr.c["one_minus_ka"][:, p:p + 1],
                                                ALU.mult, ALU.add).then_inc(s["prep"], 1)
                        dve.wait_ge(s["prep"], 4 * p + 2 * d + 1)
                        nc.vector.tensor_tensor(a["sg"], a["sg"], k, ALU.mult).then_inc(s["prep"], 1)
                    elif n == 13:
                        dve.wait_ge(s["rinv"], p + 1)
                        nc.vector.tensor_tensor(kk[:, :], kkr[:, :], rinv[:, :], ALU.mult).then_inc(s["kk"], 1)
                        dve.wait_ge(s["kk"], p + 1)
                        dve.wait_ge(s["prep"], 4 * p + 4)
                        for d, a in both(p):
                            nc.vector.tensor_tensor(a["aa"], kk[:, :], a["aa"], ALU.mult).then_inc(s["bk"], 1)
                    elif n == 15:
                        for d, a in both(p):
                            dve.wait_ge(s["exps"], 4 * p + 2 * d + 2)
                            dve.wait_ge(s["bk"], 2 * p + d + 1)
                            nc.vector.tensor_tensor(chunks(a["Rt"]), chunks(r), inc(a, d), ALU.mult).then_inc(s["scaled"], 1)
                            nc.vector.tensor_tensor(chunks(a["Kt"]), chunks(kk[:, :]), ex(a, d), ALU.mult).then_inc(s["scaled"], 1)
                            nc.vector.tensor_tensor(a["Kh"], a["sg"], a["pinv"], ALU.mult).then_inc(s["scaled"], 1)
                            nc.vector.tensor_tensor(a["Bh"], a["aa"], a["pinv"], ALU.mult).then_inc(s["scaled"], 1)
                        if p:
                            dve.wait_ge(s["bsum"], p)
                        nc.vector.tensor_tensor(ks[:, :], a0["sg"], a1["sg"], ALU.add).then_inc(s["ksum"], 1)
                        dve.wait_ge(s["ksum"], p + 1)
                        nc.vector.scalar_tensor_tensor(ks[:, :], ks[:, :], pr.param("r_k")(p), r, ALU.mult, ALU.mult)\
                            .then_inc(s["bonus"], 1)
                    elif n == 17:
                        dve.wait_ge(s["bsum"], p + 1)
                        dve.wait_ge(s["kkr"], p + 1)
                        nc.vector.tensor_tensor(k, pr.bank[2], v, ALU.mult).then_inc(s["bout"], 1)

                def mask(p, n):
                    d, key = n % 2, GRAMS[n // 2][0]
                    out = pr.pair[2 - d] if key == "L" else pr.pair[1]
                    which = strict if key in ("L", "M") else incl
                    dve.wait_ge(s["gram"], 8 * p + n + 1)
                    nc.vector.tensor_tensor(dirs[d][0]["mats"][key][:, :, :], out[:, :].rearrange("p (q t) -> p q t", q=8),
                                            which[:, d:d + 1, :].to_broadcast([P, 8, P]), ALU.mult).then_inc(s["mask"], 1)

                def beside(p, n):
                    if 6 <= n < 12:
                        mask(p, n - 4)
                    if p + 1 < RT:
                        prepare(p + 1, n)

                dve.wait_ge(s["const"], 80)
                for d in range(2):
                    for j in range(2):
                        nc.vector.memset(dirs[d][j]["pin"][:, :, (CH if d else 0):(CH if d else 0) + 1], 1.0).then_inc(s["ones"], 1)
                dve.wait_ge(s["ones"], 4)
                for n in range(STEPS):
                    prepare(0, n)
                for p in range(RT):
                    if p:
                        dve.wait_ge(s["y"], p)
                    for d, a in both(p):
                        mask(p, d)
                        dve.wait_ge(s["mask"], 8 * p + d + 1)
                        nc.vector.tensor_tensor(a["Y"], a["mats"]["L"][:, :, :], pair[:, d:d + 1, :].to_broadcast([P, 8, P]),
                                                ALU.mult).then_inc(s["ybegin"], 1)
                        dve.wait_ge(s["ybegin"], 2 * p + d + 1)
                        nc.vector.tensor_tensor(a["Y"], c["ident"].unsqueeze(1).to_broadcast([P, 8, P]), a["Y"],
                                                ALU.subtract).then_inc(s["y0"], 1)
                    for lev in range(1, 6):
                        u = 5 * p + lev - 1
                        for d, a in both(p):
                            dve.wait_ge(s["m1"], 2 * u + d + 1)
                            nc.vector.tensor_tensor(a["M1"], pr.bank[d].rearrange("p (q t) -> p q t", q=8),
                                                    level[:, 5 * d + lev - 1:5 * d + lev, :].to_broadcast([P, 8, 64]), ALU.mult)\
                                .then_inc(s["m1out"], 1)
                        beside(p, 3 * lev - 3)
                        for d, a in both(p):
                            dve.wait_ge(s["px"], 2 * u + d + 1)
                            w = 2 ** lev
                            x = half_cols(a["X"], lev, d)
                            nc.vector.tensor_tensor(x, x, pr.bank[d].rearrange("p (q n w) -> p q n w", q=8, w=w),
                                                    ALU.subtract).then_inc(s["xsub"], 1)
                        beside(p, 3 * lev - 2)
                        beside(p, 3 * lev - 1)
                    if p + 1 < RT:
                        prepare(p + 1, 15)
                    for d, a in both(p):
                        dve.wait_ge(s["phi"], 2 * p + d + 1)
                        for hh in range(2):
                            h = slice(64 * hh, 64 * hh + 64)
                            nc.vector.tensor_tensor(a["Phi"][h, :, h].rearrange("p (a b) t -> p a b t", a=2),
                                                    pr.pair[0][h, :].rearrange("p (a x) -> p a x", a=2)[:, :, 0:256]
                                                    .rearrange("p a (b t) -> p a b t", b=4),
                                                    c["ident64"][h, :].unsqueeze(1).unsqueeze(1).to_broadcast([64, 2, 4, 64]),
                                                    ALU.add).then_inc(s["phiout"], 1)
                        dve.wait_ge(s["psi"], 2 * p + d + 1)
                        dve.wait_ge(s["zzero"], 4 * (2 * p + d + 1))
                        for hh in range(2):
                            h = slice(64 * hh, 64 * hh + 64)
                            psi = pr.pair[3][h, :].rearrange("p (cc x) -> p cc x", cc=2)[:, :, 0:256]\
                                .rearrange("p cc (b t) -> p b cc t", b=4)
                            for cc in range(2):
                                lo_b, hi_b = (0, 4 if cc == 0 else 3) if d == 0 else (0 if cc == 1 else 1, 4)
                                step = 1 if d == 0 else -1
                                slots = a["Z"][h, 2 * lo_b + cc + step:2 * (hi_b - 1) + cc + step + 1:2, h]
                                ends = a["pin"][h, 2 * lo_b + cc:2 * (hi_b - 1) + cc + 1:2, CH * (1 - d):CH * (1 - d) + 1]
                                last = nc.vector.tensor_tensor(slots, psi[:, lo_b:hi_b, cc, :],
                                                               ends.to_broadcast([64, hi_b - lo_b, 64]), ALU.mult)
                                last.then_inc(s["psiout"], 1)
                    for d, a in both(p):
                        dve.wait_ge(s["rb"], 2 * p + d + 1)
                        dve.wait_ge(s["gram"], 8 * (p + 1))
                        nc.vector.tensor_tensor(a["Rb"], a["Rt"], pr.bank[2 + d], ALU.add).then_inc(s["rbout"], 1)
                    for i in range(NCH - 1):
                        for d, a in both(p):
                            at, nxt = ORDER[d][i], ORDER[d][i + 1]
                            dve.wait_ge(s["step"], 14 * p + 2 * i + d + 1)
                            if i == 0:
                                dve.wait_ge(s["psiout"], 4 * (2 * p + d + 1))
                            nc.vector.scalar_tensor_tensor(a["Z"][:, nxt, :], pr.bank[4 + d][:, (i % 4) * P:(i % 4 + 1) * P],
                                                           a["pin"][:, at, CH * (1 - d):CH * (1 - d) + 1], a["Z"][:, nxt, :],
                                                           ALU.mult, ALU.add).then_inc(s["zout"], 1)
                    if p + 1 < RT:
                        prepare(p + 1, 17)
        pr.release(s)




def rwkv_out_block(pr, U, g2, y_hi, y_lo):
    nc, c = pr.nc, pr.c
    with ExitStack() as ctx:
        sq = U[:, 8:8 + RT, :]
        rstd, gate = (pr.tile("ro_" + k, [P, RT, T], F32, ctx) for k in ("rstd", "gate"))
        sg = pr.tile("ro_sg", [P, T], F32, ctx)
        s = pr.stage_sems("ro_", ("sg", "mean", "centred", "sq", "var", "log", "rstd", "g", "gate", "y", "hi", "lo"))
        with nc.Block() as block:
            @block.sync
            def _(sp):
                pr.stream(sp, pr.taken + RAW_SLOTS)

            @block.tensor
            def _(pe):
                for p in range(RT):
                    nc.tensor.matmul(pr.bank[p], c["head_mean"], U[:, p, :], start=True, stop=True).then_inc(s["mean"], 1)
                pe.wait_ge(s["sg"], 1)
                for p in range(RT):
                    nc.tensor.matmul(pr.bank[4 + p], g2[:, p * P:(p + 1) * P], sg[:, :], start=True, stop=True)\
                        .then_inc(s["g"], 1)
                for p in range(RT):
                    pe.wait_ge(s["centred"], p + 1)
                    pe.wait_ge(s["sq"], p + 1)
                    nc.tensor.matmul(pr.bank[p], c["head_mean"], sq[:, p, :], start=True, stop=True).then_inc(s["var"], 1)

            @block.scalar
            def _(act):
                nc.scalar.activation(sg[:, :], U[:, 14, :], ACT.Sigmoid).then_inc(s["sg"], 1)
                for p in range(RT):
                    act.wait_ge(s["centred"], p + 1)
                    nc.scalar.activation(sq[:, p, :], U[:, p, :], ACT.Square).then_inc(s["sq"], 1)
                for p in range(RT):
                    act.wait_ge(s["g"], p + 1)
                    nc.scalar.copy(gate[:, p, :], pr.bank[4 + p]).then_inc(s["gate"], 1)
                for p in range(RT):
                    act.wait_ge(s["var"], p + 1)
                    nc.scalar.activation(rstd[:, p, :], pr.bank[p], ACT.Ln, bias=pr.eps(1)).then_inc(s["log"], 1)
                for p in range(RT):
                    act.wait_ge(s["log"], p + 1)
                    nc.scalar.activation(rstd[:, p, :], rstd[:, p, :], ACT.Exp, scale=-0.5).then_inc(s["rstd"], 1)
                for p in range(RT):
                    act.wait_ge(s["y"], 3 * (p + 1))
                    nc.scalar.copy(y_hi[:, p, :], U[:, p, :]).then_inc(s["hi"], 1)

            @block.vector
            def _(dve):
                for p in range(RT):
                    dve.wait_ge(s["mean"], p + 1)
                    nc.vector.tensor_tensor(U[:, p, :], U[:, p, :], pr.bank[p], ALU.subtract).then_inc(s["centred"], 1)
                for p in range(RT):
                    y = U[:, p, :]
                    dve.wait_ge(s["rstd"], p + 1)
                    nc.vector.scalar_tensor_tensor(y, y, pr.param("ln_w")(p), rstd[:, p, :], ALU.mult, ALU.mult)\
                        .then_inc(s["y"], 1)
                    dve.wait_ge(s["y"], 3 * p + 1)
                    nc.vector.scalar_tensor_tensor(y, U[:, 4 + p, :], pr.param("ln_b")(p), y, ALU.add, ALU.add)\
                        .then_inc(s["y"], 1)
                    dve.wait_ge(s["y"], 3 * p + 2)
                    dve.wait_ge(s["gate"], p + 1)
                    nc.vector.tensor_tensor(y, y, gate[:, p, :], ALU.mult).then_inc(s["y"], 1)
                for p in range(RT):
                    dve.wait_ge(s["hi"], p + 1)
                    nc.vector.tensor_tensor(y_lo[:, p, :], U[:, p, :], y_hi[:, p, :].bitcast(F32), ALU.subtract).then_inc(s["lo"], 1)
        pr.release(s)


class Modulation:

    def __init__(self, pr, room, cc, spread):
        self.pr, self.cc, self.spread = pr, cc, spread
        n = MOD_SLOTS * D // T
        self.w = room[:, 0:n, :].rearrange("p (s a) t -> p s (a t)", s=MOD_SLOTS)
        self.acc = room[:, n:n + 4 * D // T, :].rearrange("p (i c a) t -> p i c (a t)", i=2, c=2)
        self.landed = [pr.sem(f"mod_landed{i}") for i in range(MOD_SLOTS)]
        self.added, self.reduced, self.made = pr.sem("mod_added"), pr.sem("mod_reduced"), pr.sem("mod_made")

    def load(self, pool):
        for i in range(MOD_PARTS * KT):
            if i >= MOD_SLOTS:
                pool.wait_ge(self.added, 2 * (i - MOD_SLOTS + 1))
            pool.dma_start(self.w[:, i % MOD_SLOTS, :], self.pr.dram["w_mod"][i]).then_inc(self.landed[i % MOD_SLOTS], 16)

    def add(self, dve, n):
        total = 2 * MOD_PARTS * KT
        for j in range(min(total, total * n // self.spread), min(total, total * (n + 1) // self.spread)):
            i, column = divmod(j, 2)
            part, k = divmod(i, KT)
            acc, w, c = self.acc[:, part % 2, column, :], self.w[:, i % MOD_SLOTS, :], self.cc[:, column, k:k + 1]
            dve.wait_ge(self.landed[i % MOD_SLOTS], 16 * (i // MOD_SLOTS + 1))
            if k == 0:
                if part >= 2:
                    dve.wait_ge(self.reduced, part - 1)
                self.pr.nc.vector.tensor_scalar(acc, w, c, None, ALU.mult).then_inc(self.added, 1)
            else:
                dve.wait_ge(self.added, j - 1)
                self.pr.nc.vector.scalar_tensor_tensor(acc, w, c, acc, ALU.mult, ALU.add).then_inc(self.added, 1)

    def reduce(self, pe, part):
        pe.wait_ge(self.added, 2 * KT * (part + 1))
        for column in range(2):
            for m in range(KT):
                at = MOD_PARTS * KT * column + KT * part + m
                last = self.pr.nc.tensor.matmul(self.pr.bank[6][:, at:at + 1], self.acc[:, part % 2, column, m * P:(m + 1) * P],
                                                self.pr.c["ones"][:, 0:1], start=True, stop=True)
        last.then_inc(self.reduced, 1)

    def finish(self, dve):
        pr, nc = self.pr, self.pr.nc
        n = MOD_PARTS * KT
        dve.wait_ge(self.reduced, MOD_PARTS)
        nc.vector.tensor_tensor(pr.mod[:, :, :], pr.bank[6][:, 0:2 * n].rearrange("p (two n) -> p two n", two=2),
                                pr.param_cols("b_mod").unsqueeze(1).to_broadcast([P, 2, n]), ALU.add).then_inc(self.made, 1)
        dve.wait_ge(self.made, 1)
        for i, (column, part, gain) in enumerate(((0, 1, "norm1"), (1, 1, "norm1"), (0, 4, "norm2"))):
            nc.vector.scalar_tensor_tensor(pr.gains[:, i, :], pr.mod[:, column, KT * part:KT * (part + 1)], 1.0,
                                           pr.param_cols(gain), ALU.add, ALU.mult).then_inc(self.made, 1)


def retention_block(pr, V, W, out_hi, out_lo, o, sq):
    nc, c = pr.nc, pr.c
    H = RET_HEADS
    with ExitStack() as ctx:
        t = lambda name, shape: pr.tile("rt_" + name, shape, F32, ctx)
        table, turned, rot_sb = t("table", [P, 2, T]), t("turned", [P, 2, T]), t("rot", [P, P])
        vN, kcN, vcN = t("v_tokens", [P, TB, T]), t("kc_tokens", [P, CTX_T, T]), t("vc_tokens", [P, CTX_T, T])
        rel, strip, strip_b = t("rel", [P, 4, 896]), t("strip", [P, 2, 896]), t("strip_b", [P, 896])
        steps, ctx_steps = t("steps", [P, 2, T]), t("ctx_steps", [P, 2, CTX_T])
        kcd = t("kc_decayed", [P, 2, CTX_T, P])
        dq = t("q_decayed", [P, 2, T])
        S = t("scores", [P, 2, TB, T])
        state = t("state", [P, 2, P])
        sm = t("small", [P, 6, 8])
        cw = t("ctx_weight", [P, 8, CTX_T])
        rstd = turned
        s = pr.stage_sems("rt_", ("rope_in", "in", "rot", "sin", "cos", "roped", "tr", "trout", "rate", "lg", "cw", "kcd", "state", "stateout",
              "e1", "e2", "dq", "strip", "score", "sout", "o", "oout", "mean", "centred", "sq", "var", "log", "rstd",
              "silu", "y", "hi", "lo"))
        with nc.Block() as block:
            @block.sync
            def _(sp):
                sp.dma_start(table[:, :, :], pr.dram["rope_ret"].rearrange("p (a t) -> p a t", a=2)).then_inc(s["rope_in"], 16)
                sp.dma_start(rot_sb[:, :], pr.dram["rot_ret"]).then_inc(s["rope_in"], 16)
                for dst, key, a in ((rel, "rel", 4), (steps, "steps", 2), (ctx_steps, "ctx_steps", 2)):
                    sp.dma_start(dst[:, :, :], pr.dram[key].rearrange("p (a t) -> p a t", a=a)).then_inc(s["in"], 16)
                pr.stream(sp, pr.taken + RAW_SLOTS)

            @block.tensor
            def _(pe):
                pe.wait_ge(s["rope_in"], 32)
                for i in range(8):
                    if i >= 2:
                        pe.wait_ge(s["sin"], i - 1)
                    nc.tensor.matmul(pr.bank[i % 2], rot_sb[:, :], V[:, i, :], start=True, stop=True).then_inc(s["rot"], 1)
                srcs = [(V, 8, b) for b in range(TB)] + [(W, 0, b) for b in range(CTX_T)] + [(W, 4, b) for b in range(CTX_T)]
                for i, (src, first, b) in enumerate(srcs):
                    if i >= 2:
                        pe.wait_ge(s["trout"], i - 1)
                    for j in range(4):
                        last = nc.tensor.transpose(pr.bank[2 + i % 2][:, j * P:(j + 1) * P],
                                                   src[:, first + j, b * P:(b + 1) * P], c["ident"])
                    last.then_inc(s["tr"], 1)
                pe.wait_ge(s["roped"], 8)
                pe.wait_ge(s["trout"], 8)
                for h in range(H + 1):
                    j = h - 1
                    if h:
                        pe.wait_ge(s["oout"], j + 1)
                        if j >= 2:
                            pe.wait_ge(s["centred"], j - 1)
                        nc.tensor.matmul(pr.bank[4 + j % 2], c["ones"], o[:, j % 2, :], start=True, stop=True).then_inc(s["mean"], 1)
                    if h < H:
                        for d in range(2):
                            pe.wait_ge(s["kcd"], 2 * (2 * h + d + 1))
                            if d == 0 and h:
                                pe.wait_ge(s["stateout"], 2 * h)
                            for b in range(CTX_T):
                                last = nc.tensor.matmul(pr.bank[7][:, d * P:(d + 1) * P], kcd[:, d, b, :],
                                                        vcN[:, b, h * P:(h + 1) * P], start=(b == 0), stop=(b == CTX_T - 1))
                            last.then_inc(s["state"], 1)
                        for i in range(TB):
                            n = TB * h + i
                            if n >= 2:
                                pe.wait_ge(s["sout"], n - 1)
                            nc.tensor.matmul(pr.bank[n % 2], V[:, 4 + h, i * P:(i + 1) * P], V[:, h, :], start=True, stop=True)\
                                .then_inc(s["score"], 1)
                    if h:
                        pe.wait_ge(s["sq"], j + 1)
                        if j:
                            pe.wait_ge(s["log"], j)
                        nc.tensor.matmul(pr.bank[6], c["ones"], sq[:, j % 2, :], start=True, stop=True).then_inc(s["var"], 1)
                    if h < H:
                        if h >= 2:
                            pe.wait_ge(s["oout"], h - 1)
                        out = pr.bank[2 + h % 2]
                        for i in range(TB):
                            pe.wait_ge(s["sout"], TB * h + i + 1)
                            nc.tensor.matmul(out, vN[:, i, h * P:(h + 1) * P], S[:, h % 2, i, :], start=(i == 0), stop=False)
                        pe.wait_ge(s["stateout"], 2 * h + 2)
                        pe.wait_ge(s["dq"], 2 * h + 2)
                        for d in range(2):
                            last = nc.tensor.matmul(out, state[:, d, :], dq[:, d, :], start=False, stop=(d == 1))
                        last.then_inc(s["o"], 1)

            @block.scalar
            def _(act):
                for h in range(H):
                    nc.scalar.activation(V[:, 12 + h, :], V[:, 12 + h, :], ACT.Silu).then_inc(s["silu"], 1)
                nc.scalar.activation(sm[:, 0, :], pr.param_cols("rate"), ACT.Exp).then_inc(s["rate"], 1)
                act.wait_ge(s["lg"], 1)
                nc.scalar.activation(sm[:, 2, :], sm[:, 1, :], ACT.Ln).then_inc(s["rate"], 1)
                act.wait_ge(s["in"], 48)
                act.wait_ge(s["lg"], 5)
                for d in range(2):
                    for h in range(H):
                        nc.scalar.activation(cw[:, 4 * d + h, :], ctx_steps[:, d, :], ACT.Exp, scale=sm[:, 5, 4 * d + h:4 * d + h + 1])\
                            .then_inc(s["cw"], 1)
                for i in range(8):
                    act.wait_ge(s["tr"], i + 1)
                    dst = vN[:, i, :] if i < 4 else kcN[:, i - 4, :] if i < 6 else vcN[:, i - 6, :]
                    nc.scalar.copy(dst, pr.bank[2 + i % 2]).then_inc(s["trout"], 1)
                for h in range(H + 1):
                    j = h - 1
                    if h < H:
                        for d in range(2):
                            if h:
                                act.wait_ge(s["strip"], 3 * h)
                            nc.scalar.activation(strip[:, 1, :] if d == 0 else strip_b[:, :], rel[:, d, :], ACT.Exp,
                                                 scale=sm[:, 5, 4 * d + h:4 * d + h + 1]).then_inc(s["e1"], 1)
                        for d in range(2):
                            if h:
                                act.wait_ge(s["o"], h)
                            nc.scalar.activation(dq[:, d, :], steps[:, d, :], ACT.Exp,
                                                 scale=sm[:, 5, 4 * d + h:4 * d + h + 1]).then_inc(s["e2"], 1)
                        for d in range(2):
                            act.wait_ge(s["state"], 2 * h + 2)
                            nc.scalar.copy(state[:, d, :], pr.bank[7][:, d * P:(d + 1) * P]).then_inc(s["stateout"], 1)
                    if h:
                        act.wait_ge(s["centred"], j + 1)
                        nc.scalar.activation(sq[:, j % 2, :], o[:, j % 2, :], ACT.Square).then_inc(s["sq"], 1)
                        act.wait_ge(s["var"], j + 1)
                        nc.scalar.activation(rstd[:, j % 2, :], pr.bank[6], ACT.Ln, scale=1.0 / P, bias=pr.eps(0)).then_inc(s["log"], 1)
                        act.wait_ge(s["log"], j + 1)
                        nc.scalar.activation(rstd[:, j % 2, :], rstd[:, j % 2, :], ACT.Exp, scale=-0.5).then_inc(s["rstd"], 1)
                    if h < H:
                        act.wait_ge(s["o"], h + 1)
                        if h >= 2:
                            act.wait_ge(s["lo"], h - 1)
                        nc.scalar.copy(o[:, h % 2, :], pr.bank[2 + h % 2]).then_inc(s["oout"], 1)
                    if h:
                        act.wait_ge(s["y"], 2 * j + 2)
                        nc.scalar.copy(out_hi[:, j, :], o[:, j % 2, :]).then_inc(s["hi"], 1)

            @block.vector
            def _(dve):
                dve.wait_ge(s["rate"], 1)
                nc.vector.tensor_scalar(sm[:, 1, :], sm[:, 0, :], -1.0, 1.0, ALU.mult, ALU.add).then_inc(s["lg"], 1)
                dve.wait_ge(s["lg"], 1)
                nc.vector.scalar_tensor_tensor(sm[:, 3, :], sm[:, 1, :], -1.0, sm[:, 0, :], ALU.add, ALU.add).then_inc(s["lg"], 1)
                nc.vector.reciprocal(sm[:, 4, :], sm[:, 1, :]).then_inc(s["lg"], 1)
                dve.wait_ge(s["lg"], 3)
                nc.vector.tensor_tensor(sm[:, 3, :], sm[:, 3, :], sm[:, 4, :], ALU.mult).then_inc(s["lg"], 1)
                dve.wait_ge(s["lg"], 4)
                dve.wait_ge(s["rate"], 2)
                nc.vector.tensor_tensor(sm[:, 5, :], sm[:, 2, :], sm[:, 3, :], ALU.subtract).then_inc(s["lg"], 1)
                dve.wait_ge(s["rope_in"], 32)
                for i in range(8):
                    dve.wait_ge(s["rot"], i + 1)
                    if i >= 2:
                        dve.wait_ge(s["roped"], i - 1)
                    nc.vector.tensor_tensor(turned[:, i % 2, :], pr.bank[i % 2], table[:, 1, :], ALU.mult).then_inc(s["sin"], 1)
                    nc.vector.tensor_tensor(V[:, i, :], V[:, i, :], table[:, 0, :], ALU.mult).then_inc(s["cos"], 1)
                    dve.wait_ge(s["sin"], i + 1)
                    dve.wait_ge(s["cos"], i + 1)
                    nc.vector.tensor_tensor(V[:, i, :], V[:, i, :], turned[:, i % 2, :], ALU.add).then_inc(s["roped"], 1)
                dve.wait_ge(s["roped"], 8)
                for h in range(H + 1):
                    j = h - 1
                    if h < H:
                        dve.wait_ge(s["trout"], 6)
                        dve.wait_ge(s["cw"], 8)
                        for d in range(2):
                            if h:
                                dve.wait_ge(s["state"], 2 * h)
                            for b in range(CTX_T):
                                nc.vector.tensor_scalar(kcd[:, d, b, :], kcN[:, b, h * P:(h + 1) * P], cw[:, 4 * d + h, b:b + 1],
                                                        None, ALU.mult).then_inc(s["kcd"], 1)
                    if h:
                        x = o[:, j % 2, :]
                        dve.wait_ge(s["mean"], j + 1)
                        nc.vector.scalar_tensor_tensor(x, pr.bank[4 + j % 2], -1.0 / P, x, ALU.mult, ALU.add).then_inc(s["centred"], 1)
                    if h < H:
                        dve.wait_ge(s["e1"], 2 * h + 2)
                        dve.wait_ge(s["in"], 48)
                        if h:
                            dve.wait_ge(s["strip"], 3 * h)
                            dve.wait_ge(s["sout"], TB * h)
                        nc.vector.tensor_tensor(strip[:, 0, :], strip[:, 1, :], rel[:, 2, :], ALU.mult).then_inc(s["strip"], 1)
                        nc.vector.tensor_tensor(strip_b[:, :], strip_b[:, :], rel[:, 3, :], ALU.mult).then_inc(s["strip"], 1)
                        dve.wait_ge(s["strip"], 3 * h + 2)
                        nc.vector.tensor_tensor(strip[:, 0, :], strip[:, 0, :], strip_b[:, :], ALU.add).then_inc(s["strip"], 1)
                        dve.wait_ge(s["strip"], 3 * h + 3)
                        for i in range(TB):
                            n = TB * h + i
                            dve.wait_ge(s["score"], n + 1)
                            if h >= 2:
                                dve.wait_ge(s["o"], h - 1)
                            at = 384 - P * i
                            nc.vector.tensor_tensor(S[:, h % 2, i, :], pr.bank[n % 2], strip[:, 0, at:at + T], ALU.mult)\
                                .then_inc(s["sout"], 1)
                        for d in range(2):
                            dve.wait_ge(s["e2"], 2 * h + d + 1)
                            nc.vector.tensor_tensor(dq[:, d, :], V[:, h, :], dq[:, d, :], ALU.mult).then_inc(s["dq"], 1)
                    if h:
                        dve.wait_ge(s["rstd"], j + 1)
                        nc.vector.scalar_tensor_tensor(x, x, pr.param("gn_g")(j), rstd[:, j % 2, :], ALU.mult, ALU.mult)\
                            .then_inc(s["y"], 1)
                        dve.wait_ge(s["y"], 2 * j + 1)
                        dve.wait_ge(s["silu"], j + 1)
                        nc.vector.tensor_tensor(x, x, V[:, 12 + j, :], ALU.mult).then_inc(s["y"], 1)
                        dve.wait_ge(s["hi"], j + 1)
                        nc.vector.tensor_tensor(out_lo[:, j, :], x, out_hi[:, j, :].bitcast(F32), ALU.subtract).then_inc(s["lo"], 1)
        pr.release(s)




def gqa_block(pr, A, B, out_hi, out_lo):
    nc, c = pr.nc, pr.c
    with ExitStack() as ctx:
        t = lambda name, shape: pr.tile("at_" + name, shape, F32, ctx)
        table, turned, rot_sb = t("table", [P, 2, T]), t("turned", [P, 2, T]), t("rot", [P, P])
        sq, rstd = t("sq", [P, 6, T]), t("rstd", [P, 6, T])
        vN = t("v_tokens", [P, KEY_T, P])
        prob, probT = t("prob", [P, 3, KEYS]), t("probT", [P, 2, KEYS])
        small, qgain = t("small", [P, 4, 4]), t("qgain", [P, 1])
        s = pr.stage_sems("at_", ("in", "qgain", "sq", "mean", "log", "rstd", "normed", "rot", "sin", "cos", "roped", "vtr", "vout",
              "score", "negmax", "exp", "tr", "tra", "trv", "pv", "inv", "scaled", "hi", "lo"))
        items = [(A[:, i, :], T) for i in range(5)] + [(B[:, 0, :], TC)]
        units = [(i, q, g) for i in range(ATT_TILES) for q in range(TB) for g in range(2)]
        U = len(units)
        with nc.Block() as block:
            @block.sync
            def _(sp):
                sp.dma_start(table[:, :, :], pr.dram["rope_att"].rearrange("p (a t) -> p a t", a=2)).then_inc(s["in"], 16)
                sp.dma_start(rot_sb[:, :], pr.dram["rot_att"]).then_inc(s["in"], 16)
                pr.stream(sp, pr.taken + RAW_SLOTS)

            @block.tensor
            def _(pe):
                for b in range(KEY_T):
                    src = B[:, 1, b * P:(b + 1) * P] if b < CTX_T else A[:, 5, (b - CTX_T) * P:(b - CTX_T + 1) * P]
                    last = nc.tensor.transpose(pr.pair[3][:, b * P:(b + 1) * P], src, c["ident"])
                last.then_inc(s["vtr"], 1)
                for n, (x, w) in enumerate(items):
                    pe.wait_ge(s["sq"], n + 1)
                    nc.tensor.matmul(pr.bank[n][:, 0:w], c["head_mean"], sq[:, n, 0:w], start=True, stop=True)\
                        .then_inc(s["mean"], 1)
                pe.wait_ge(s["log"], 6)
                for n in range(5):
                    pe.wait_ge(s["normed"], n + 1)
                    if n == 0:
                        pe.wait_ge(s["in"], 32)
                    if n >= 2:
                        pe.wait_ge(s["sin"], n - 1)
                    nc.tensor.matmul(pr.bank[2 + n % 2], rot_sb[:, :], A[:, n, :], start=True, stop=True).then_inc(s["rot"], 1)
                pe.wait_ge(s["roped"], 5)
                pe.wait_ge(s["normed"], 6)
                pe.wait_ge(s["vout"], 1)
                for n in range(U + 3):
                    if n < U:
                        i, q, g = units[n]
                        h = slice(64 * g, 64 * g + 64)
                        if n >= 2:
                            pe.wait_ge(s["exp"], n - 1)
                        query = A[h, i, q * P:(q + 1) * P]
                        nc.tensor.matmul(pr.pair[n % 2][:, 256:512], query, B[h, 0, :], start=True, stop=True)
                        nc.tensor.matmul(pr.pair[n % 2][:, 512:1024], query, A[h, 4, :], start=True, stop=True)\
                            .then_inc(s["score"], 1)
                    if 2 <= n <= U + 1:
                        m = n - 2
                        pe.wait_ge(s["scaled"], m + 1)
                        if m:
                            pe.wait_ge(s["tra"], m)
                            pe.wait_ge(s["trv"], m)
                        for k in range(KEY_T):
                            last = nc.tensor.transpose(pr.pair[2][:, k * P:(k + 1) * P], prob[:, m % 3, k * P:(k + 1) * P], c["ident"])
                        last.then_inc(s["tr"], 1)
                    if n >= 3:
                        m = n - 3
                        i, q, g = units[m]
                        pe.wait_ge(s["tra"], m + 1)
                        pe.wait_ge(s["trv"], m + 1)
                        if m % 8 == 0 and i >= 2:
                            pe.wait_ge(s["lo"], i - 1)
                        for k in range(KEY_T):
                            last = nc.tensor.matmul(pr.bank[6 + i % 2][64 * g:64 * g + 64, q * P:(q + 1) * P],
                                                    vN[:, k, 64 * g:64 * g + 64], probT[:, m % 2, k * P:(k + 1) * P],
                                                    start=(k == 0), stop=(k == KEY_T - 1))
                        last.then_inc(s["pv"], 1)

            @block.scalar
            def _(act):
                for n, (x, w) in enumerate(items):
                    nc.scalar.activation(sq[:, n, 0:w], x, ACT.Square).then_inc(s["sq"], 1)
                for n, (x, w) in enumerate(items):
                    act.wait_ge(s["mean"], n + 1)
                    nc.scalar.activation(rstd[:, n, 0:w], pr.bank[n][:, 0:w], ACT.Ln, bias=pr.eps(0)).then_inc(s["log"], 1)
                for n, (x, w) in enumerate(items):
                    act.wait_ge(s["log"], n + 1)
                    nc.scalar.activation(rstd[:, n, 0:w], rstd[:, n, 0:w], ACT.Exp, scale=-0.5).then_inc(s["rstd"], 1)
                act.wait_ge(s["vtr"], 1)
                nc.scalar.copy(vN[:, :, :], pr.pair[3][:, 0:KEYS].rearrange("p (k t) -> p k t", k=KEY_T)).then_inc(s["vout"], 1)
                for n in range(U + 3):
                    if n < U:
                        act.wait_ge(s["negmax"], n + 1)
                        if n >= 3:
                            act.wait_ge(s["tr"], n - 2)
                        nc.scalar.activation(prob[:, n % 3, :], pr.pair[n % 2][:, 256:1024], ACT.Exp,
                                             bias=small[:, n % 4, 0:1], accum_out=small[:, n % 4, 1:2]).then_inc(s["exp"], 1)
                    if 2 <= n <= U + 1:
                        m = n - 2
                        act.wait_ge(s["tr"], m + 1)
                        if m >= 2:
                            act.wait_ge(s["pv"], m - 1)
                        nc.scalar.copy(probT[:, m % 2, 0:T], pr.pair[2][:, 0:T]).then_inc(s["tra"], 1)
                    if n >= 3 and (n - 3) % 8 == 7:
                        i = (n - 3) // 8
                        act.wait_ge(s["pv"], 8 * (i + 1))
                        nc.scalar.copy(out_hi[:, i, :], pr.bank[6 + i % 2]).then_inc(s["hi"], 1)

            @block.vector
            def _(dve):
                dve.wait_ge(s["in"], 32)
                nc.vector.tensor_scalar(qgain[:, :], pr.param("q_norm")(0), ATT_SCALE, None, ALU.mult).then_inc(s["qgain"], 1)
                dve.wait_ge(s["qgain"], 1)
                for n, (x, w) in enumerate(items):
                    dve.wait_ge(s["rstd"], n + 1)
                    nc.vector.scalar_tensor_tensor(x, x, qgain[:, :] if n < 4 else pr.param("k_norm")(0),
                                                   rstd[:, n, 0:w], ALU.mult, ALU.mult).then_inc(s["normed"], 1)
                for i in range(5):
                    dve.wait_ge(s["rot"], i + 1)
                    if i >= 2:
                        dve.wait_ge(s["roped"], i - 1)
                    nc.vector.tensor_tensor(turned[:, i % 2, :], pr.bank[2 + i % 2], table[:, 1, :], ALU.mult).then_inc(s["sin"], 1)
                    nc.vector.tensor_tensor(A[:, i, :], A[:, i, :], table[:, 0, :], ALU.mult).then_inc(s["cos"], 1)
                    dve.wait_ge(s["sin"], i + 1)
                    dve.wait_ge(s["cos"], i + 1)
                    nc.vector.tensor_tensor(A[:, i, :], A[:, i, :], turned[:, i % 2, :], ALU.add).then_inc(s["roped"], 1)
                for n in range(U + 3):
                    if n < U:
                        dve.wait_ge(s["score"], n + 1)
                        if n >= 4:
                            dve.wait_ge(s["scaled"], n - 3)
                        nc.vector.tensor_reduce(small[:, n % 4, 0:1], pr.pair[n % 2][:, 256:1024], AX_X, ALU.max, negate=True)\
                            .then_inc(s["negmax"], 1)
                    if 1 <= n <= U:
                        m = n - 1
                        dve.wait_ge(s["exp"], m + 1)
                        nc.vector.reciprocal(small[:, m % 4, 2:3], small[:, m % 4, 1:2]).then_inc(s["inv"], 1)
                        dve.wait_ge(s["inv"], m + 1)
                        nc.vector.tensor_scalar(prob[:, m % 3, :], prob[:, m % 3, :], small[:, m % 4, 2:3], None, ALU.mult)\
                            .then_inc(s["scaled"], 1)
                    if 2 <= n <= U + 1:
                        m = n - 2
                        dve.wait_ge(s["tr"], m + 1)
                        if m >= 2:
                            dve.wait_ge(s["pv"], m - 1)
                        nc.vector.tensor_copy(probT[:, m % 2, T:KEYS], pr.pair[2][:, T:KEYS]).then_inc(s["trv"], 1)
                    if n >= 3 and (n - 3) % 8 == 7:
                        i = (n - 3) // 8
                        dve.wait_ge(s["hi"], i + 1)
                        nc.vector.tensor_tensor(out_lo[:, i, :], pr.bank[6 + i % 2], out_hi[:, i, :].bitcast(F32), ALU.subtract)\
                            .then_inc(s["lo"], 1)
        pr.release(s)




def bass_two_blocks(nc, dram, out):
    with ExitStack() as ctx:
        pr = Program(nc, ctx, dram)
        stored = pr.sem("out_stored")
        h_spill = nc.dram_tensor("h_spill", (2, P, KT * T), F32, kind="Internal").ap()
        params = pr.tile("params", [P, N_PARAMS])
        derived = pr.tile("derived", [P, 24])
        consts = pr.tile("consts", [P, 4 * P + 64 + 6])
        pr.c = {"ident": consts[:, 0:P], "ones": consts[:, P:2 * P], "head_ones": consts[:, 2 * P:3 * P],
                "head_mean": consts[:, 3 * P:4 * P], "ident64": consts[:, 4 * P:4 * P + 64],
                "own_weight": derived[:, 0:15], "one_minus_ka": derived[:, 15:19], "subln_scaled": derived[:, 19:20]}
        pr.eps = lambda i: consts[:, 4 * P + 64 + i:4 * P + 65 + i]
        pr.param_cols = lambda name: params[:, PARAM_COLS[name][0]:sum(PARAM_COLS[name])]
        pr.param = lambda name: (lambda i: params[:, PARAM_COLS[name][0] + i:PARAM_COLS[name][0] + i + 1])
        pr.mod = pr.tile("mod", [P, 2, 48])
        pr.gains = pr.tile("gains", [P, 3, 8])
        silu_c = pr.tile("silu_c", [P, 2, 8])
        x = pr.tile("x", [P, KT, T])
        o_spill = nc.dram_tensor("o_spill", (2, P, 4 * T), F32, kind="Internal").ap()
        x_view = lambda ap: ap.rearrange("(k p) t -> p k t", p=P)

        ahead_sq, rstd = pr.tile("norm_sq", [P, 2, T]), pr.tile("norm_rstd", [P, 2, T])
        ahead = NormAhead(pr, ahead_sq, rstd)
        with ExitStack() as scope:
            U = pr.tile("rwkv_in", [P, R_TILES, T], F32, scope)
            w_lora = pr.tile("w_lora", [P, 2, RW], F32, scope)
            g2 = pr.tile("g2", [P, RW], F32, scope)
            with ExitStack() as in_scope:
                hi = pr.tile("w_hi", [P, SPLIT_SLOTS, 1024], F32R, in_scope)
                lo = pr.tile("w_lo", [P, SPLIT_SLOTS, 1024], F32R, in_scope)
                h_hi = pr.tile("h_hi", [P, KT, T], F32R, in_scope)
                h_lo = pr.tile("h_lo", [P, KT, T], F32R, in_scope)
                with ExitStack() as x_scope:
                    buf = pr.tile("norm_buf0", [P, KT, T], F32, x_scope)
                    loaded, made, lora_in = pr.sem("consts_in"), pr.sem("derived_made"), pr.sem("lora_in")
                    x_in = [pr.sem(f"x_in{j}") for j in range(KT // 2)]
                    with nc.Block() as block:
                        @block.sync
                        def _(sp):
                            sp.dma_start(params[:, :], dram["params"]).then_inc(loaded, 16)
                            sp.dma_start(consts[:, :], dram["consts"]).then_inc(loaded, 16)
                            for k in range(0, KT, 2):
                                sp.dma_start(x[:, k:k + 2, :], x_view(dram["x"])[:, k:k + 2, :]).then_inc(x_in[k // 2], 16)
                            sp.dma_start(w_lora[:, :, :], dram["w_lora"].rearrange("p (a n) -> p a n", a=2)).then_inc(lora_in, 16)
                            sp.dma_start(g2[:, :], dram["g2"]).then_inc(lora_in, 16)
                            sp.wait_ge(loaded, 32)

                        @block.vector
                        def _(dve):
                            dve.wait_ge(loaded, 32)
                            nc.vector.tensor_tensor(derived[:, 0:15], pr.param_cols("mu_prev"), pr.param_cols("mu_next"),
                                                    ALU.add).then_inc(made, 1)
                            dve.wait_ge(made, 1)
                            nc.vector.tensor_scalar(derived[:, 0:15], derived[:, 0:15], -1.0, 1.0, ALU.mult, ALU.add).then_inc(made, 1)
                            nc.vector.tensor_scalar(derived[:, 15:19], pr.param_cols("k_a"), -1.0, 1.0, ALU.mult, ALU.add)\
                                .then_inc(made, 1)
                            nc.vector.tensor_scalar(derived[:, 19:20], pr.param("subln")(0), 1.0 - LAMBDA_INIT, None, ALU.mult)\
                                .then_inc(made, 1)
                    norm_block(pr, {"sq": buf, "rstd": rstd, "y": buf}, lambda k: x[:, k, :], h_hi, h_lo, pr.param("norm_mix"),
                               ready=lambda engine, k: engine.wait_ge(x_in[k // 2], 16))
                spilled = pr.sem("h_spilled")
                h_parts = split_parts(h_hi, h_lo, KT)
                o_hi, o_lo = pr.tile("o_hi", [P, 4, T], F32R, in_scope), pr.tile("o_lo", [P, 4, T], F32R, in_scope)
                with ExitStack() as da_scope:
                    Q = pr.tile("da_in", [P, 12, T], F32, da_scope)
                    evac = pr.sem("da_in_out")
                    gemm_block(pr, hi, lo, [Job(pr.taken + n, h_parts) for n in range(12)],
                               copy_out(pr, evac, lambda n: Q[:, n, :], scale=lambda n: 64 ** -0.5 if n < 4 else 1.0),
                               nothing, evac, lambda n: n + 1)
                    da_attention_block(pr, Q, U, o_hi, o_lo)
                pad = pr.tile("shift_pad", [P, 2, T + 2], F32, in_scope)
                s_act, s_dve, s_zero = pr.sem("shift_act"), pr.sem("shift_dve"), pr.sem("pad_zeroed")

                def shift_act(act, n, bank, done):
                    act.wait_ge(pr.job_done, done)
                    if n >= 2:
                        act.wait_ge(s_dve, 2 * (n - 1))
                    nc.scalar.copy(pad[:, n % 2, 1:T + 1], bank).then_inc(s_act, 1)
                    nc.scalar.mul(U[:, n, :], bank, pr.c["own_weight"][:, n:n + 1]).then_inc(s_act, 1)

                def shift_dve(dve, n, bank, done):
                    if n == 0:
                        for j in range(2):
                            nc.vector.memset(pad[:, j, 0:1], 0.0).then_inc(s_zero, 1)
                            nc.vector.memset(pad[:, j, T + 1:T + 2], 0.0).then_inc(s_zero, 1)
                        dve.wait_ge(s_zero, 4)
                    dve.wait_ge(s_act, 2 * n + 2)
                    nc.vector.scalar_tensor_tensor(U[:, n, :], pad[:, n % 2, 0:T], pr.param("mu_prev")(n), U[:, n, :],
                                                   ALU.mult, ALU.add).then_inc(s_dve, 1)
                    dve.wait_ge(s_dve, 2 * n + 1)
                    nc.vector.scalar_tensor_tensor(U[:, n, :], pad[:, n % 2, 2:T + 2], pr.param("mu_next")(n), U[:, n, :],
                                                   ALU.mult, ALU.add).then_inc(s_dve, 1)

                with nc.Block() as block:
                    @block.sync
                    def _(sp):
                        sp.dma_start(h_spill[0], h_hi[:, :, :].bitcast(F32).rearrange("p k t -> p (k t)")).then_inc(spilled, 16)
                        sp.dma_start(h_spill[1], h_lo[:, :, :].bitcast(F32).rearrange("p k t -> p (k t)")).then_inc(spilled, 16)
                        sp.dma_start(o_spill[0], o_hi[:, :, :].bitcast(F32).rearrange("p k t -> p (k t)")).then_inc(spilled, 16)
                        sp.dma_start(o_spill[1], o_lo[:, :, :].bitcast(F32).rearrange("p k t -> p (k t)")).then_inc(spilled, 16)
                gemm_block(pr, hi, lo, [Job(pr.taken + n, h_parts) for n in range(R_TILES)], shift_act, shift_dve,
                           s_act, lambda n: 2 * n + 2)
                tanhed = pr.sem("tanhed")
                with nc.Block() as block:
                    @block.scalar
                    def _(act):
                        nc.scalar.activation(U[:, 12, :], U[:, 12, :], ACT.Tanh).then_inc(tanhed, 1)
                        for i, key in enumerate(("c", "c_ctx")):
                            nc.scalar.activation(silu_c[:, i, :], pr.param_cols(key), ACT.Silu).then_inc(tanhed, 1)

                    @block.sync
                    def _(sp):
                        sp.wait_ge(spilled, 64)
                        sp.wait_ge(lora_in, 32)
            rwkv_block(pr, U, w_lora, x)
            hi, lo = (pr.tile(f"w_{k}1", [P, SPLIT_SLOTS, 1024], F32R, scope) for k in ("hi", "lo"))
            h_hi, h_lo = pr.tile("h_hi1", [P, KT, T], F32R, scope), pr.tile("h_lo1", [P, KT, T], F32R, scope)
            flat = lambda tile: tile.bitcast(F32).rearrange("p k t -> p (k t)")
            with ExitStack() as merge_scope:
                y_hi, y_lo = pr.tile("y_hi", [P, 4, T], F32R, merge_scope), pr.tile("y_lo", [P, 4, T], F32R, merge_scope)
                h_back, o_back, x_back = (pr.sem(k + "_back") for k in "hox")
                with nc.Block() as block:
                    @block.sync
                    def _(sp):
                        sp.dma_start(flat(h_hi[:, :, :]), h_spill[0]).then_inc(h_back, 16)
                        sp.dma_start(flat(h_lo[:, :, :]), h_spill[1]).then_inc(h_back, 16)
                        sp.dma_start(x[:, :, :], x_view(dram["x"])).then_inc(x_back, 16)
                rwkv_out_block(pr, U, g2, y_hi, y_lo)
                o_hi, o_lo = pr.tile("o_hi1", [P, 4, T], F32R, merge_scope), pr.tile("o_lo1", [P, 4, T], F32R, merge_scope)
                with nc.Block() as block:
                    @block.sync
                    def _(sp):
                        sp.dma_start(flat(o_hi[:, :, :]), o_spill[0]).then_inc(o_back, 16)
                        sp.dma_start(flat(o_lo[:, :, :]), o_spill[1]).then_inc(o_back, 16)
                m_hi = pr.tile("m_hi", [P, KT, T], F32R, merge_scope)
                m_lo = pr.tile("m_lo", [P, KT, T], F32R, merge_scope)
                sig, part = U[:, 0:2, :], U[:, 2:6, :].rearrange("p (a b) t -> p a b t", a=2)
                g_sig, g_part, g_sum, g_hi, g_lo = (pr.sem("merge_" + k) for k in ("sig", "part", "sum", "hi", "lo"))

                def merge_act(act, n, bank, done):
                    tile, j = divmod(n, 4)
                    act.wait_ge(pr.job_done, done)
                    if j in (0, 2):
                        e = 2 * tile + j // 2
                        if e >= 2:
                            act.wait_ge(g_part, e - 1)
                        nc.scalar.activation(sig[:, e % 2, :], bank, ACT.Sigmoid).then_inc(g_sig, 1)
                    if j == 3:
                        act.wait_ge(g_sum, tile + 1)
                        nc.scalar.copy(m_hi[:, tile, :], part[:, tile % 2, 0, :]).then_inc(g_hi, 1)

                def merge_dve(dve, n, bank, done):
                    tile, j = divmod(n, 4)
                    if j in (1, 3):
                        e = 2 * tile + j // 2
                        dve.wait_ge(pr.job_done, done)
                        dve.wait_ge(g_sig, e + 1)
                        if tile >= 2:
                            dve.wait_ge(g_lo, tile - 1)
                        nc.vector.tensor_tensor(part[:, tile % 2, j // 2, :], bank, sig[:, e % 2, :], ALU.mult).then_inc(g_part, 1)
                    if j == 3:
                        dve.wait_ge(g_part, 2 * tile + 2)
                        nc.vector.tensor_tensor(part[:, tile % 2, 0, :], part[:, tile % 2, 0, :], part[:, tile % 2, 1, :], ALU.add)\
                            .then_inc(g_sum, 1)
                        dve.wait_ge(g_hi, tile + 1)
                        nc.vector.tensor_tensor(m_lo[:, tile, :], part[:, tile % 2, 0, :], m_hi[:, tile, :].bitcast(F32), ALU.subtract)\
                            .then_inc(g_lo, 1)

                def merge_wait(pe, n):
                    if n == 0:
                        pe.wait_ge(h_back, 32)
                    elif n == 3:
                        pe.wait_ge(o_back, 32)
                    if n >= BANKS:
                        old = n - BANKS
                        e = 2 * (old // 4) + (old % 4) // 2
                        pe.wait_ge(g_sig if old % 2 == 0 else g_part, e + 1)

                moving = (split_parts(h_hi, h_lo, KT), split_parts(y_hi, y_lo, 4), split_parts(h_hi, h_lo, KT), split_parts(o_hi, o_lo, 4))
                gemm_block(pr, hi, lo, [Job(pr.taken + n, moving[n % 4]) for n in range(32)], merge_act, merge_dve,
                           None, None, pe_wait=merge_wait)
                residual_gemm(pr, hi, lo, x, split_parts(m_hi, m_lo, KT), "out1",
                              ahead=ahead.begin(x, pr.param("norm_ffn"), h_hi, h_lo), x_in=x_back)
            modulation = Modulation(pr, U, silu_c, spread=60)
            ff_stage(pr, hi, lo, x, split_parts(h_hi, h_lo, KT), "ff1", modulation=modulation,
                     rstd=rstd[:, 1, :], ahead=ahead.begin(x, pr.param("norm_ple"), h_hi, h_lo))
            with ExitStack() as s2:
                p_raw = pr.tile("p_raw", [P, 2, T], F32, s2)
                p_hi, p_lo = pr.tile("p_hi", [P, 2, T], F32R, s2), pr.tile("p_lo", [P, 2, T], F32R, s2)
                ple_stage(pr, hi, lo, x, split_parts(h_hi, h_lo, KT), p_raw, p_hi, p_lo, modulation, rstd[:, 1, :], ahead.begin(x))
        with ExitStack() as scope:
            a_hi, a_lo = pr.tile("a_hi", [P, KT, T], F32R, scope), pr.tile("a_lo", [P, KT, T], F32R, scope)
            with ExitStack() as s1:
                A, B = pr.tile("att_in", [P, 6, T], F32, s1), pr.tile("att_ctx", [P, 2, TC], F32, s1)
                with ExitStack() as s2:
                    V, W = pr.tile("ret_in", [P, 16, T], F32, s2), pr.tile("ret_ctx", [P, 8, TC], F32, s2)
                    with ExitStack() as s3:
                        hi, lo = (pr.tile(f"w_{k}3", [P, SPLIT_SLOTS, 1024], F32R, s3) for k in ("hi", "lo"))
                        c_hi, c_lo = pr.tile("c_hi", [P, KT, TC], F32R, s3), pr.tile("c_lo", [P, KT, TC], F32R, s3)
                        with ExitStack() as s4:
                            buf = pr.tile("norm_buf5", [P, KT, T], F32, s4)
                            rstd5 = pr.tile("norm_rstd5", [P, 2, T], F32, s4)
                            ctx_buf = pr.tile("ctx", [P, KT, TC], F32, s4)
                            ctx_in = pr.sem("ctx_in")
                            with nc.Block() as block:
                                @block.sync
                                def _(sp):
                                    sp.dma_start(ctx_buf[:, :, :], x_view(dram["ctx"])).then_inc(ctx_in, 16)
                            norm_block(pr, {"sq": buf, "rstd": rstd5, "y": buf}, lambda k: x[:, k, :], a_hi, a_lo,
                                       lambda k: pr.gains[:, 0, k:k + 1], bias=lambda k: pr.mod[:, 0, k:k + 1],
                                       before=(pr.param("norm_final"), rstd[:, 1, :]))
                            norm_block(pr, {"sq": buf[:, :, TC:T], "rstd": rstd5, "y": buf[:, :, TC:T]}, lambda k: ctx_buf[:, k, :],
                                       c_hi, c_lo, lambda k: pr.gains[:, 1, k:k + 1], width=TC,
                                       bias=lambda k: pr.mod[:, 1, k:k + 1], ready=lambda engine, k: engine.wait_ge(ctx_in, 16))
                        lat, con = split_parts(a_hi, a_lo, KT), split_parts(c_hi, c_lo, KT)
                        jobs, dests = [], []
                        for n in range(22):
                            scale = RET_SCALE if 4 <= n < 8 else 1.0
                            jobs.append(Job(pr.taken + n, lat))
                            dests.append((V[:, n, :] if n < 16 else A[:, n - 16, :], scale))
                            if 4 <= n < 12 or n >= 20:
                                jobs.append(Job(pr.taken + n, con, TC))
                                dests.append((W[:, n - 4, :] if n < 12 else B[:, n - 20, :], scale))
                        evac = pr.sem("in2_out")
                        gemm_block(pr, hi, lo, jobs, copy_out(pr, evac, lambda n: dests[n][0], scale=lambda n: dests[n][1]),
                                   nothing, evac, lambda n: n + 1)
                    retention_block(pr, V, W, a_hi, a_lo, ahead_sq, rstd)
                gqa_block(pr, A, B, a_hi[:, 4:8, :], a_lo[:, 4:8, :])
            hi, lo = (pr.tile(f"w_{k}4", [P, SPLIT_SLOTS, 1024], F32R, scope) for k in ("hi", "lo"))
            residual_gemm(pr, hi, lo, x, split_parts(a_hi, a_lo, KT), "out2", lambda n: pr.mod[:, 0, 16 + n:17 + n],
                          ahead=ahead.begin(x))
            with ExitStack() as s2:
                buf = pr.tile("norm_buf6", [P, KT, T], F32, s2)
                norm_block(pr, {"sq": None, "rstd": rstd, "y": buf}, lambda k: x[:, k, :], a_hi, a_lo,
                           lambda k: pr.gains[:, 2, k:k + 1], bias=lambda k: pr.mod[:, 0, 24 + k:25 + k], known=True)
            ff_stage(pr, hi, lo, x, split_parts(a_hi, a_lo, KT), "ff2", lambda n: pr.mod[:, 0, 40 + n:41 + n],
                     ahead=ahead.begin(x))
            normed = pr.sem("out_normed")
            with nc.Block() as block:
                @block.vector
                def _(dve):
                    for k in range(KT):
                        nc.vector.scalar_tensor_tensor(x[:, k, :], x[:, k, :], pr.param("final2")(k), rstd[:, 1, :],
                                                       ALU.mult, ALU.mult).then_inc(normed, 1)

                @block.sync
                def _(sp):
                    for k in range(0, KT, 2):
                        sp.wait_ge(normed, k + 2)
                        sp.dma_start(x_view(out)[:, k:k + 2, :], x[:, k:k + 2, :]).then_inc(stored, 16)
                    sp.wait_ge(stored, 16 * KT // 2)
        assert pr.taken == len(TILES) == pr.streamed


def residual_gemm(pr, hi, lo, x, moving, name, gate=None, ahead=None, x_in=None):
    nc = pr.nc
    evac = pr.sem(name + "_out")

    def add(dve, n, bank, done):
        if n == 0 and x_in is not None:
            dve.wait_ge(x_in, 16)
        dve.wait_ge(pr.job_done, done)
        if gate is None:
            nc.vector.tensor_tensor(x[:, n, :], x[:, n, :], bank, ALU.add).then_inc(evac, 1)
        else:
            nc.vector.scalar_tensor_tensor(x[:, n, :], bank, gate(n), x[:, n, :], ALU.mult, ALU.add).then_inc(evac, 1)

        ahead.dve(dve, n)

    gemm_block(pr, hi, lo, [Job(pr.taken + n, moving) for n in range(KT)],
               lambda act, n, bank, done: ahead.act(act, n, evac, n + 1), add, evac, lambda n: n + 1,
               pe_wait=lambda pe, n: ahead.pe(pe, n - 3) if n >= 3 else None,
               pe_after=lambda pe: [ahead.pe(pe, n) for n in range(KT - 3, KT)], act_after=ahead.finish)


def ff_stage(pr, hi, lo, x, moving, name, gate=None, modulation=None, rstd=None, ahead=None):
    nc = pr.nc
    with ExitStack() as ctx:
        f_hi = pr.tile(name + "_f_hi", [P, 2, KT, T], F32R, ctx)
        f_lo = pr.tile(name + "_f_lo", [P, 2, KT, T], F32R, ctx)
        act_buf, sq_buf = pr.tile(name + "_relu", [P, 2, T], F32, ctx), pr.tile(name + "_sq", [P, 2, T], F32, ctx)
        relu_made, sq_made, f_hi_made, f_lo_made, added = (pr.sem(f"{name}_{k}") for k in ("relu", "sq", "hi", "lo", "added"))
        order = [(kind, g, j) for kind, g in ff_order() for j in range(8)]
        ups = [sum(k == "up" for k, _, _ in order[:n]) for n in range(len(order) + 1)]
        downs = [n - u for n, u in enumerate(ups)]
        jobs = [Job(pr.taken + n, moving if kind == "up" else
                    [(f_hi[:, g % 2, k, :], f_lo[:, g % 2, k, :]) for k in range(KT)]) for n, (kind, g, j) in enumerate(order)]
        base = pr.jobs
        last_down = {g: max(n for n, (k, gg, _) in enumerate(order) if k == "down" and gg == g) for g in range(FF_GROUPS)}

        def act_step(act, n, bank, done):
            kind, g, j = order[n]
            if kind == "up":
                u = ups[n]
                act.wait_ge(relu_made, u + 1)
                if u >= 2:
                    act.wait_ge(f_lo_made, u - 1)
                nc.scalar.activation(sq_buf[:, u % 2, :], act_buf[:, u % 2, :], ACT.Square).then_inc(sq_made, 1)
                act.wait_ge(sq_made, u + 1)
                if g >= 2:
                    act.wait_ge(pr.job_done, base + last_down[g - 2] + 1)
                nc.scalar.copy(f_hi[:, g % 2, j, :], sq_buf[:, u % 2, :]).then_inc(f_hi_made, 1)
            elif g == FF_GROUPS - 1:
                ahead.act(act, j, added, downs[n] + 1)

        def dve_step(dve, n, bank, done):
            kind, g, j = order[n]
            dve.wait_ge(pr.job_done, done)
            if kind == "up":
                u = ups[n]
                if u >= 2:
                    dve.wait_ge(sq_made, u - 1)
                if rstd is None:
                    nc.vector.tensor_scalar(act_buf[:, u % 2, :], bank, 0.0, None, ALU.max).then_inc(relu_made, 1)
                else:
                    nc.vector.scalar_tensor_tensor(act_buf[:, u % 2, :], bank, 0.0, rstd, ALU.max, ALU.mult).then_inc(relu_made, 1)
                dve.wait_ge(f_hi_made, u + 1)
                nc.vector.tensor_tensor(f_lo[:, g % 2, j, :], sq_buf[:, u % 2, :], f_hi[:, g % 2, j, :].bitcast(F32), ALU.subtract)\
                    .then_inc(f_lo_made, 1)
            else:
                if g:
                    dve.wait_ge(added, downs[n] - 7)
                if gate is None:
                    nc.vector.tensor_tensor(x[:, j, :], x[:, j, :], bank, ALU.add).then_inc(added, 1)
                else:
                    nc.vector.scalar_tensor_tensor(x[:, j, :], bank, gate(j), x[:, j, :], ALU.mult, ALU.add).then_inc(added, 1)
                if g == FF_GROUPS - 1:
                    ahead.dve(dve, j)
            if modulation is not None:
                modulation.add(dve, n)

        due = [(r + 1) * modulation.spread // MOD_PARTS + 3 for r in range(MOD_PARTS)] if modulation else []

        def pe_wait(pe, n):
            kind, g, j = order[n]
            if n >= BANKS:
                old = order[n - BANKS][0]
                if old == "up":
                    pe.wait_ge(relu_made, ups[n - BANKS] + 1)
                else:
                    pe.wait_ge(added, downs[n - BANKS] + 1)
            if kind == "down" and j == 0:
                pe.wait_ge(f_lo_made, 8 * (g + 1))
            if modulation is not None and n in due:
                modulation.reduce(pe, due.index(n))
            if n >= len(order) - 5:
                ahead.pe(pe, n - len(order) + 5)

        gemm_block(pr, hi, lo, jobs, act_step, dve_step, added, None, pe_wait=pe_wait,
                   pool_step=modulation.load if modulation else None,
                   pe_after=lambda pe: [ahead.pe(pe, n) for n in range(KT - 3, KT)], act_after=ahead.finish)


def ple_stage(pr, hi, lo, x, moving, p_raw, p_hi, p_lo, modulation, rstd, ahead):
    nc = pr.nc
    s_in, s_hi, s_lo, s_gate, s_sig, s_mul, s_add = (pr.sem("ple_" + k) for k in ("in", "hi", "lo", "gate", "sig", "mul", "add"))
    with ExitStack() as ctx:
        sig = pr.tile("ple_sig", [P, 2, T], F32, ctx)
        with nc.Block() as block:
            @block.sync
            def _(sp):
                sp.dma_start(p_raw[:, :, :], pr.dram["p"].rearrange("(k p) t -> p k t", p=P)).then_inc(s_in, 16)

            @block.scalar
            def _(act):
                act.wait_ge(s_in, 16)
                nc.scalar.copy(p_hi[:, :, :], p_raw[:, :, :]).then_inc(s_hi, 1)

            @block.vector
            def _(dve):
                dve.wait_ge(s_hi, 1)
                nc.vector.tensor_tensor(p_lo[:, :, :], p_raw[:, :, :], p_hi[:, :, :].bitcast(F32), ALU.subtract).then_inc(s_lo, 1)
                modulation.finish(dve)

        def act_step(act, n, bank, done):
            tile, j = divmod(n, 2)
            if j == 0:
                act.wait_ge(s_gate, tile + 1)
                nc.scalar.activation(sig[:, tile % 2, :], sig[:, tile % 2, :], ACT.Sigmoid).then_inc(s_sig, 1)
            else:
                ahead.act(act, tile, s_add, tile + 1)

        def dve_step(dve, n, bank, done):
            tile, j = divmod(n, 2)
            dve.wait_ge(pr.job_done, done)
            if j == 0:
                if tile >= 2:
                    dve.wait_ge(s_add, tile - 1)
                nc.vector.tensor_tensor(sig[:, tile % 2, :], bank, rstd, ALU.mult).then_inc(s_gate, 1)
            else:
                dve.wait_ge(s_sig, tile + 1)
                nc.vector.tensor_tensor(sig[:, tile % 2, :], bank, sig[:, tile % 2, :], ALU.mult).then_inc(s_mul, 1)
                dve.wait_ge(s_mul, tile + 1)
                nc.vector.tensor_tensor(x[:, tile, :], x[:, tile, :], sig[:, tile % 2, :], ALU.add).then_inc(s_add, 1)

        def pe_wait(pe, n):
            if n >= BANKS:
                tile, j = divmod(n - BANKS, 2)
                pe.wait_ge(s_mul if j else s_gate, tile + 1)
                if j:
                    ahead.pe(pe, tile)

        gemm_block(pr, hi, lo, [Job(pr.taken + n, moving if n % 2 == 0 else split_parts(p_hi, p_lo, 2)) for n in range(16)],
                   act_step, dve_step, s_add, None, pe_wait=pe_wait,
                   pe_after=lambda pe: [ahead.pe(pe, n) for n in range(KT - 2, KT)], act_after=ahead.finish)


def columns(v):
    return np.asarray(v, np.float32).reshape(-1, P).T


def weight_tiles(w):
    k, n = w.shape
    kt = min(k // P, 8)
    w = w.reshape(k // (kt * P), kt, P, n // P, P)
    return np.ascontiguousarray(w.transpose(0, 3, 2, 1, 4)).reshape(-1, P, kt * P)


def lay_out(inputs):
    a = {k: np.asarray(v) for k, v in inputs.items()}
    first = lambda k: a[k][0]
    w_in = first("w_in")
    heads = np.concatenate([np.r_[64 * i:64 * i + 64, 64 * (i + 4):64 * (i + 4) + 64] for i in range(4)])
    in2 = np.r_[0:2048, 2048 + heads, 2560:2816]
    out2 = np.r_[0:512, 512 + heads]
    dup = lambda v: np.concatenate([v, v])
    pad = lambda v: np.concatenate([v, np.zeros(64, np.float32)])
    vectors = {
        "norm_mix": first("norm_mix"), "mu_prev": first("shift_mu_prev"), "mu_next": first("shift_mu_next"),
        "w0": first("rwkv_w0").reshape(-1), "a0": first("rwkv_a0").reshape(-1), "k_k": first("rwkv_k_k"),
        "k_a": first("rwkv_k_a"), "r_k": first("rwkv_r_k").reshape(-1), "ln_w": first("rwkv_ln_w"),
        "ln_b": first("rwkv_ln_b"), "subln": first("da_subln_w"), "norm_ffn": first("norm_ffn"),
        "norm_ple": first("norm_ple"), "norm_final": a["norm_final"], "b_mod": first("b_mod_2"),
        "norm1": first("norm1_g_2"), "norm2": first("norm2_g_2"), "gn_g": first("ret_gn_g_2"),
        "q_norm": dup(first("q_norm_g_2")), "k_norm": dup(first("k_norm_g_2")), "final2": a["final_norm_g_2"],
        "c": a["c_2"][0], "c_ctx": a["c_ctx_2"],
        "lam": np.concatenate([pad(first(k)) for k in ("da_lq1", "da_lk1", "da_lq2", "da_lk2")]),
        "rate": np.repeat(first("ret_log_rate_2").reshape(-1), P),
    }
    consts = shape_constants()
    out = {
        "x": a["x"][0].T, "ctx": a["ctx_2"][0].T, "p": a["p"][0, 0].T,
        "params": np.concatenate([columns(vectors[k]) for k in PARAM_COLS], 1),
        "consts": np.concatenate([consts.pop(k) for k in ("ident", "ones", "head_ones", "head_mean", "ident64", "eps")], 1),
        "w_lora": np.concatenate([first("rwkv_w2").reshape(P, -1), first("rwkv_a2").reshape(P, -1)], 1),
        "g2": first("rwkv_g2"),
        "w_rwkv": weight_tiles(w_in[:, 0:1920]), "w_da": weight_tiles(w_in[:, 1920:3456]),
        "w_gate": weight_tiles(w_in[:, 3456:5504]), "w_mod": first("w_mod_2").reshape(KT, P, MOD_PARTS, D).transpose(2, 0, 1, 3).reshape(-1, P, D),
        "w_rwkv_o": weight_tiles(first("rwkv_w_o")), "w_da_o": weight_tiles(first("da_w_o")),
        "w_out": weight_tiles(first("w_out")), "w_ff1": weight_tiles(first("w_ff1")), "w_ff2": weight_tiles(first("w_ff2")),
        "w_ple_gate": weight_tiles(first("w_ple_gate")), "w_ple_proj": weight_tiles(first("w_ple_proj")),
        "w_in2": weight_tiles(first("w_in_2")[:, in2]), "w_out2": weight_tiles(first("w_out_2")[out2]),
        "w_ff1_2": weight_tiles(first("w_ff1_2")), "w_ff2_2": weight_tiles(first("w_ff2_2")),
        **consts,
    }
    return {k: np.ascontiguousarray(v) for k, v in out.items()}


def kernel(**inputs):
    import concourse.bacc as bacc
    from concourse.bass_utils import run_bass_kernel_spmd

    nc = bacc.Bacc("TRN2", target_bir_lowering=False, num_devices=1)
    arrays = lay_out(inputs)
    dram = {k: nc.dram_tensor(f"in_{k}", v.shape, F32, kind="ExternalInput").ap() for k, v in arrays.items()}
    out = nc.dram_tensor("out", (D, T), F32, kind="ExternalOutput").ap()
    bass_two_blocks(nc, dram, out)
    results = run_bass_kernel_spmd(nc, [{f"in_{k}": v for k, v in arrays.items()}], core_ids=[0])
    return np.ascontiguousarray(results.results[0]["out"].T)[None]
```
